# Optimizing a Trainium2 kernel written in Bass

```python
import math
import jax, jax.numpy as jnp
from jax import lax
import numpy as np

D_MODEL = 1024
BATCH = 1
SEQ = 512
DEPTH = 2
DEC_BATCH = 8
DEC_SEQ = 1
PAST_LEN = 512
PAGE_SIZE = 128

M_HEADS = 4
M_HEAD_DIM = 128
G_HEADS = 4
G_KEY_DIM = 64
G_VAL_DIM = 128
G_GATE_RANK = 16
G_GATE_TAU = 16.0
A_HEADS = 8
A_QK_DIM = 64
A_V_DIM = 128
CHUNK = 64
Q_BLOCK = 128
FFN_HIDDEN = 2816
CONV_WIDTH = 3
NORM_EPS = 1e-6
N_REC_LAYERS = (DEPTH + 1) // 2
N_ATT_LAYERS = DEPTH // 2

M_W = M_HEADS * M_HEAD_DIM
GK_W = G_HEADS * G_KEY_DIM
GV_W = G_HEADS * G_VAL_DIM
REC_IN_SIZES = (M_W, M_W, M_W, M_W, M_HEADS, M_HEADS, GK_W, GK_W, GV_W, GV_W, G_GATE_RANK)
REC_IN_W = sum(REC_IN_SIZES)
REC_OUT_W = M_W + GV_W
A_QK_W = A_HEADS * 2 * A_QK_DIM
A_V_W = A_HEADS * A_V_DIM
ATT_IN_W = 2 * A_QK_W + A_V_W

kernel_name = 'hybrid_mlstm_gla_diffattn_convffn_step'

def rms_norm(x, gain):
    xf = x.astype(jnp.float32)
    y = xf * lax.rsqrt(jnp.mean(xf * xf, axis=-1, keepdims=True) + NORM_EPS)
    return (y * gain.astype(jnp.float32)).astype(x.dtype)

def _to_chunks(a, L):
    B, T, H = a.shape[:3]
    a = a.reshape((B, T // L, L, H) + a.shape[3:])
    return jnp.moveaxis(a, (1, 3), (0, 2))

def _from_chunks(a):
    a = jnp.moveaxis(a, (0, 2), (1, 3))
    return a.reshape((a.shape[0], a.shape[1] * a.shape[2]) + a.shape[3:])

def mlstm_chunkwise(q, k, v, i_pre, f_pre, c0, n0, m0):
    f32 = jnp.float32
    T = q.shape[1]
    L = CHUNK if T % CHUNK == 0 else T
    mask = jnp.tril(jnp.ones((L, L), dtype=bool))
    xs = (_to_chunks(q.astype(f32), L), _to_chunks(k.astype(f32), L), _to_chunks(v.astype(f32), L),
          _to_chunks(i_pre.astype(f32), L), _to_chunks(jax.nn.log_sigmoid(f_pre.astype(f32)), L))

    def step(carry, chunk):
        c, n, m = carry
        qc, kc, vc, ic, lfc = chunk
        b = jnp.cumsum(lfc, axis=-1)
        inter = b + m[..., None]
        intra = jnp.where(mask, b[..., :, None] - b[..., None, :] + ic[..., None, :], -jnp.inf)
        m_t = jnp.maximum(inter, jnp.max(intra, axis=-1))
        w_inter = jnp.exp(inter - m_t)
        s = jnp.einsum('bhtd,bhsd->bhts', qc, kc) * jnp.exp(intra - m_t[..., None])
        num = w_inter[..., None] * jnp.einsum('bhvk,bhtk->bhtv', c, qc) + jnp.einsum('bhts,bhsv->bhtv', s, vc)
        den = w_inter * jnp.einsum('bhk,bhtk->bht', n, qc) + jnp.sum(s, axis=-1)
        h = num / jnp.maximum(jnp.abs(den), jnp.exp(-m_t))[..., None]
        m_new = m_t[..., -1]
        w_end = jnp.exp(b[..., -1:] - b + ic - m_new[..., None])
        decay = jnp.exp(b[..., -1] + m - m_new)
        c_new = decay[..., None, None] * c + jnp.einsum('bhs,bhsv,bhsk->bhvk', w_end, vc, kc)
        n_new = decay[..., None] * n + jnp.einsum('bhs,bhsk->bhk', w_end, kc)
        return (c_new, n_new, m_new), h

    (c, n, m), hs = lax.scan(step, (c0.astype(f32), n0.astype(f32), m0.astype(f32)), xs)
    return _from_chunks(hs), c, n, m

def gla_chunked(q, k, v, log_a, s0):
    f32 = jnp.float32
    T = q.shape[1]
    L = CHUNK if T % CHUNK == 0 else T
    mask = jnp.tril(jnp.ones((L, L), dtype=bool))[:, :, None]
    xs = (_to_chunks(q.astype(f32), L), _to_chunks(k.astype(f32), L), _to_chunks(v.astype(f32), L),
          _to_chunks(log_a.astype(f32), L))

    def step(s, chunk):
        qc, kc, vc, lac = chunk
        bc = jnp.cumsum(lac, axis=2)
        o_inter = jnp.einsum('bhtk,bhkv->bhtv', qc * jnp.exp(bc), s)
        decay = jnp.exp(jnp.where(mask, bc[:, :, :, None, :] - bc[:, :, None, :, :], -jnp.inf))
        a = jnp.einsum('bhtk,bhsk,bhtsk->bhts', qc, kc, decay)
        o = o_inter + jnp.einsum('bhts,bhsv->bhtv', a, vc)
        b_end = bc[:, :, -1]
        s_new = jnp.exp(b_end)[..., None] * s + jnp.einsum('bhsk,bhsv->bhkv', kc * jnp.exp(b_end[:, :, None, :] - bc), vc)
        return s_new, o

    s, os_ = lax.scan(step, s0.astype(f32), xs)
    return _from_chunks(os_), s

def rec_mixer(h, w_in, b_mgate, w_gate_up, b_gate, m_norm_g, g_norm_g, w_out, c0, n0, m0, s0):
    B, T, _ = h.shape
    f32 = jnp.float32
    idx = np.cumsum(REC_IN_SIZES)[:-1].tolist()
    mq, mk, mv, mo, mi, mf, gq, gk, gv, gg, glr = jnp.split(h @ w_in, idx, axis=-1)
    heads = lambda a, nh: a.reshape(B, T, nh, -1)
    mi = mi + b_mgate[:M_HEADS]
    mf = mf + b_mgate[M_HEADS:]
    hm, c, n, m = mlstm_chunkwise(heads(mq, M_HEADS), heads(mk, M_HEADS) * M_HEAD_DIM ** -0.5,
                                  heads(mv, M_HEADS), mi, mf, c0, n0, m0)
    hm = rms_norm(hm, m_norm_g) * jax.nn.sigmoid(heads(mo, M_HEADS).astype(f32))
    log_a = jax.nn.log_sigmoid((glr @ w_gate_up + b_gate).astype(f32)) / G_GATE_TAU
    hg, s = gla_chunked(heads(gq, G_HEADS) * G_KEY_DIM ** -0.5, heads(gk, G_HEADS), heads(gv, G_HEADS),
                        heads(log_a, G_HEADS), s0)
    hg = rms_norm(hg, g_norm_g) * jax.nn.silu(heads(gg, G_HEADS).astype(f32))
    mix = jnp.concatenate([hm.reshape(B, T, M_W), hg.reshape(B, T, GV_W)], axis=-1).astype(h.dtype)
    return mix @ w_out, c, n, m, s

def att_project(h, w_in, q_g, k_g):
    B, T, _ = h.shape
    q, k, v = jnp.split(h @ w_in, [A_QK_W, 2 * A_QK_W], axis=-1)
    q = rms_norm(q.reshape(B, T, A_HEADS, 2, A_QK_DIM), q_g)
    k = rms_norm(k.reshape(B, T, A_HEADS, 2, A_QK_DIM), k_g)
    return q, k, v.reshape(B, T, A_HEADS, A_V_DIM)

def diff_attend(q, k, v, q_pos, k_pos, lam):
    s = jnp.einsum('bqhcd,bkhcd->bchqk', q, k).astype(jnp.float32) * A_QK_DIM ** -0.5
    s = jnp.where(q_pos[:, None] >= k_pos[None, :], s, -jnp.inf)
    p = jax.nn.softmax(s, axis=-1)
    a = p[:, 0] - lam * p[:, 1]
    return jnp.einsum('bhqk,bkhv->bqhv', a, v.astype(jnp.float32))

def prompt_diff_attention(q, k, v, lam):
    B, T = q.shape[:2]
    qb_len = Q_BLOCK if T % Q_BLOCK == 0 else T
    nb = T // qb_len
    qb = jnp.moveaxis(q.reshape((B, nb, qb_len) + q.shape[2:]), 1, 0)
    pos = jnp.arange(T).reshape(nb, qb_len)
    k_pos = jnp.arange(T)
    out = lax.map(lambda a: diff_attend(a[0], k, v, a[1], k_pos, lam), (qb, pos))
    return jnp.moveaxis(out, 0, 1).reshape(B, T, A_HEADS, A_V_DIM)

def att_output(a, lam_init, out_g, w_out):
    B, T = a.shape[:2]
    o = rms_norm(a, out_g) * (1.0 - lam_init)
    return o.reshape(B, T, A_V_W).astype(w_out.dtype) @ w_out

def conv_ffn(h, w_up, w_gate, conv_w, conv_b, w_down, buf):
    T = h.shape[1]
    u = h @ w_up
    g = h @ w_gate
    up = jnp.concatenate([buf.astype(u.dtype), u], axis=1)
    c = conv_b
    for j in range(CONV_WIDTH):
        c = c + conv_w[j] * up[:, j:j + T]
    y = (jax.nn.gelu(c) * g) @ w_down
    return y, up[:, -(CONV_WIDTH - 1):]

def setup_inputs(seed: int = 0) -> dict:
    key = jax.random.key(seed)
    keys = iter(jax.random.split(key, 48))

    def nrm(shape, scale):
        return jax.random.normal(next(keys), shape, jnp.float32) * scale

    def gain(shape):
        return 1.0 + nrm(shape, 0.02)

    n_pages = PAST_LEN // PAGE_SIZE
    n_pool = (DEC_BATCH * n_pages * 5) // 4
    page_table = jax.random.permutation(next(keys), n_pool)[: DEC_BATCH * n_pages]
    page_table = page_table.reshape(DEC_BATCH, n_pages).astype(jnp.int32)
    f_bias = jnp.linspace(3.0, 6.0, M_HEADS, dtype=jnp.float32)
    return {
        'x_prompt': nrm((BATCH, SEQ, D_MODEL), 1.0),
        'x_sample': nrm((DEC_BATCH, DEC_SEQ, D_MODEL), 1.0),
        'state_mlstm_C': nrm((N_REC_LAYERS, DEC_BATCH, M_HEADS, M_HEAD_DIM, M_HEAD_DIM), 1.0),
        'state_mlstm_n': nrm((N_REC_LAYERS, DEC_BATCH, M_HEADS, M_HEAD_DIM), 1.0),
        'state_mlstm_m': nrm((N_REC_LAYERS, DEC_BATCH, M_HEADS), 1.0),
        'state_gla_S': nrm((N_REC_LAYERS, DEC_BATCH, G_HEADS, G_KEY_DIM, G_VAL_DIM), 0.5),
        'state_ffn_conv': nrm((DEPTH, DEC_BATCH, CONV_WIDTH - 1, FFN_HIDDEN), 1.0),
        'cache_k': nrm((N_ATT_LAYERS, n_pool, PAGE_SIZE, A_HEADS, 2 * A_QK_DIM), 1.0),
        'cache_v': nrm((N_ATT_LAYERS, n_pool, PAGE_SIZE, A_HEADS, A_V_DIM), 1.0),
        'page_table': page_table,
        'norm_mix_g': gain((DEPTH, D_MODEL)),
        'norm_ffn_g': gain((DEPTH, D_MODEL)),
        'rec_w_in': nrm((N_REC_LAYERS, D_MODEL, REC_IN_W), D_MODEL ** -0.5),
        'rec_b_mgate': jnp.concatenate([nrm((N_REC_LAYERS, M_HEADS), 0.1),
                                        f_bias + nrm((N_REC_LAYERS, M_HEADS), 0.1)], axis=-1),
        'rec_w_gate_up': nrm((N_REC_LAYERS, G_GATE_RANK, GK_W), G_GATE_RANK ** -0.5),
        'rec_b_gate': nrm((N_REC_LAYERS, GK_W), 0.1),
        'rec_m_norm_g': gain((N_REC_LAYERS, M_HEAD_DIM)),
        'rec_g_norm_g': gain((N_REC_LAYERS, G_VAL_DIM)),
        'rec_w_out': nrm((N_REC_LAYERS, REC_OUT_W, D_MODEL), REC_OUT_W ** -0.5),
        'att_w_in': nrm((N_ATT_LAYERS, D_MODEL, ATT_IN_W), D_MODEL ** -0.5),
        'att_q_norm_g': gain((N_ATT_LAYERS, A_QK_DIM)),
        'att_k_norm_g': gain((N_ATT_LAYERS, A_QK_DIM)),
        'att_lambda_q1': nrm((N_ATT_LAYERS, A_QK_DIM), 0.1),
        'att_lambda_k1': nrm((N_ATT_LAYERS, A_QK_DIM), 0.1),
        'att_lambda_q2': nrm((N_ATT_LAYERS, A_QK_DIM), 0.1),
        'att_lambda_k2': nrm((N_ATT_LAYERS, A_QK_DIM), 0.1),
        'att_out_norm_g': gain((N_ATT_LAYERS, A_V_DIM)),
        'att_w_out': nrm((N_ATT_LAYERS, A_V_W, D_MODEL), A_V_W ** -0.5),
        'ffn_w_up': nrm((DEPTH, D_MODEL, FFN_HIDDEN), D_MODEL ** -0.5),
        'ffn_w_gate': nrm((DEPTH, D_MODEL, FFN_HIDDEN), D_MODEL ** -0.5),
        'ffn_conv_w': nrm((DEPTH, CONV_WIDTH, FFN_HIDDEN), CONV_WIDTH ** -0.5),
        'ffn_conv_b': nrm((DEPTH, FFN_HIDDEN), 0.02),
        'ffn_w_down': nrm((DEPTH, FFN_HIDDEN, D_MODEL), FFN_HIDDEN ** -0.5),
    }

def reference(x_prompt, x_sample, state_mlstm_C, state_mlstm_n, state_mlstm_m, state_gla_S, state_ffn_conv,
              cache_k, cache_v, page_table, norm_mix_g, norm_ffn_g, rec_w_in, rec_b_mgate, rec_w_gate_up,
              rec_b_gate, rec_m_norm_g, rec_g_norm_g, rec_w_out, att_w_in, att_q_norm_g, att_k_norm_g,
              att_lambda_q1, att_lambda_k1, att_lambda_q2, att_lambda_k2, att_out_norm_g, att_w_out,
              ffn_w_up, ffn_w_gate, ffn_conv_w, ffn_conv_b, ffn_w_down):
    f32 = jnp.float32
    yp, ys = x_prompt, x_sample
    bp_, db_ = x_prompt.shape[0], x_sample.shape[0]
    t_new = x_sample.shape[1]
    n_pages = page_table.shape[1]
    past = n_pages * PAGE_SIZE
    c_p, c_s, n_p, n_s, m_p, m_s, s_p, s_s = [], [], [], [], [], [], [], []
    k_p, k_s, v_p, v_s, f_p, f_s = [], [], [], [], [], []
    for layer in range(DEPTH):
        j = layer // 2
        hp = rms_norm(yp, norm_mix_g[layer])
        hs = rms_norm(ys, norm_mix_g[layer])
        if layer % 2 == 0:
            w = (rec_w_in[j], rec_b_mgate[j], rec_w_gate_up[j], rec_b_gate[j],
                 rec_m_norm_g[j], rec_g_norm_g[j], rec_w_out[j])
            op, c, n, m, s = rec_mixer(hp, *w,
                                       jnp.zeros((bp_, M_HEADS, M_HEAD_DIM, M_HEAD_DIM), f32),
                                       jnp.zeros((bp_, M_HEADS, M_HEAD_DIM), f32),
                                       jnp.zeros((bp_, M_HEADS), f32),
                                       jnp.zeros((bp_, G_HEADS, G_KEY_DIM, G_VAL_DIM), f32))
            c_p.append(c); n_p.append(n); m_p.append(m); s_p.append(s)
            os_, c, n, m, s = rec_mixer(hs, *w, state_mlstm_C[j], state_mlstm_n[j], state_mlstm_m[j], state_gla_S[j])
            c_s.append(c); n_s.append(n); m_s.append(m); s_s.append(s)
        else:
            lam_init = 0.8 - 0.6 * math.exp(-0.3 * layer)
            lam = (jnp.exp(jnp.sum(att_lambda_q1[j].astype(f32) * att_lambda_k1[j].astype(f32)))
                   - jnp.exp(jnp.sum(att_lambda_q2[j].astype(f32) * att_lambda_k2[j].astype(f32))) + lam_init)
            qp, kp, vp = att_project(hp, att_w_in[j], att_q_norm_g[j], att_k_norm_g[j])
            ap = prompt_diff_attention(qp, kp, vp, lam)
            qs, ks, vs = att_project(hs, att_w_in[j], att_q_norm_g[j], att_k_norm_g[j])
            past_k = cache_k[j, page_table].reshape(db_, past, A_HEADS, 2, A_QK_DIM).astype(ks.dtype)
            past_v = cache_v[j, page_table].reshape(db_, past, A_HEADS, A_V_DIM).astype(vs.dtype)
            kk = jnp.concatenate([past_k, ks], axis=1)
            vv = jnp.concatenate([past_v, vs], axis=1)
            as_ = diff_attend(qs, kk, vv, past + jnp.arange(t_new), jnp.arange(past + t_new), lam)
            op = att_output(ap, lam_init, att_out_norm_g[j], att_w_out[j])
            os_ = att_output(as_, lam_init, att_out_norm_g[j], att_w_out[j])
            k_p.append(kp.reshape(kp.shape[:3] + (2 * A_QK_DIM,))); v_p.append(vp)
            k_s.append(ks.reshape(ks.shape[:3] + (2 * A_QK_DIM,))); v_s.append(vs)
        yp = yp + op.astype(yp.dtype)
        ys = ys + os_.astype(ys.dtype)
        fw = (ffn_w_up[layer], ffn_w_gate[layer], ffn_conv_w[layer], ffn_conv_b[layer], ffn_w_down[layer])
        fp, bufp = conv_ffn(rms_norm(yp, norm_ffn_g[layer]), *fw,
                            jnp.zeros((bp_, CONV_WIDTH - 1, FFN_HIDDEN), yp.dtype))
        fs, bufs = conv_ffn(rms_norm(ys, norm_ffn_g[layer]), *fw, state_ffn_conv[layer])
        f_p.append(bufp); f_s.append(bufs)
        yp = yp + fp.astype(yp.dtype)
        ys = ys + fs.astype(ys.dtype)
    return (yp, ys,
            jnp.stack(c_p), jnp.stack(c_s), jnp.stack(n_p), jnp.stack(n_s), jnp.stack(m_p), jnp.stack(m_s),
            jnp.stack(s_p), jnp.stack(s_s),
            jnp.stack(k_p), jnp.stack(k_s), jnp.stack(v_p), jnp.stack(v_s),
            jnp.stack(f_p), jnp.stack(f_s))


_drawn_inputs = setup_inputs


def setup_inputs(seed=0):
    import zlib

    import numpy as np

    out = dict(_drawn_inputs(seed))
    spreads = {}
    factors = {'rec_m_norm_g': 5.813,
     'rec_g_norm_g': 5.55,
     'att_q_norm_g': 6.846,
     'att_k_norm_g': 3.492,
     'att_lambda_k2': 4.949,
     'att_out_norm_g': 6.357,
     'ffn_conv_b': 3.654}
    for name, (base, spread) in spreads.items():
        noise = np.random.default_rng([zlib.crc32(name.encode()), seed]).standard_normal(out[name].shape)
        drawn = base * np.exp(spread * noise) if base else spread * noise
        out[name] = __import__('jax').numpy.asarray(drawn.astype(out[name].dtype))
    for name, factor in factors.items():
        out[name] = (out[name] * factor).astype(out[name].dtype)
    return out
```

```python
import math
from contextlib import ExitStack

import concourse.bass as bass
import numpy as np
from concourse import mybir

P = 128
D_MODEL, T, B = 1024, 512, 8
NT = T + B
HALF = NT // 2
KT = D_MODEL // P
M_HEADS, G_PAIRS, A_HEADS, A_QK = 4, 2, 8, 64
G_KEY = 64
FFN = 2816
FT = FFN // P
KD = FT // 2
PAGE, PAGES, POOL = 128, 4, 40
EPS = 1e-6
LC_M = 128
NC_M = T // LC_M
LC_G = 64
NC_G = T // LC_G
SUB = 16
LAM_INIT = 0.8 - 0.6 * math.exp(-0.3)
NEG = -1e30

S_REC_IN = 29
S_OUT = 8
S_FFN = 2 * FT
S_DOWN = 16
S_ATT_IN = 24
RAW = 4
PHASES = [("rec_in", S_REC_IN, KT), ("rec_out", S_OUT, KT), ("ffn0", S_FFN, KT), ("down0", S_DOWN, KD),
          ("att_in", S_ATT_IN, KT), ("att_out", S_OUT, KT), ("ffn1", S_FFN, KT), ("down1", S_DOWN, KD)]
FIRST = {}
_n = 0
for _name, _s, _k in PHASES:
    FIRST[_name] = _n
    _n += _s
N_SLABS = _n

PARAMS = [("g_mix0", KT), ("g_ffn0", KT), ("g_mix1", KT), ("g_ffn1", KT),
          ("conv_w0", 3 * FT), ("conv_b0", FT), ("conv_w1", 3 * FT), ("conv_b1", FT),
          ("b_gate", G_PAIRS), ("g_m", 1), ("g_g", 1), ("g_q", 1), ("g_k", 1), ("g_out", 1),
          ("b_mgate", 1), ("lam_q", 2), ("lam_k", 2), ("m0", B), ("n0", M_HEADS * B),
          ("conv_s0", FT * 2 * B), ("conv_s1", FT * 2 * B)]
CONSTS = [("ident", P), ("ones", P)]
CONSTS_REC = [("causal_T", P), ("ones_lo", P), ("ones_hi", P), ("sel_head", M_HEADS * P), ("half_sum", 32),
              ("diag_mask", SUB * SUB), ("reset_m", T), ("reset_g", T), ("w_gate_up", G_PAIRS * P)]
CONSTS_ATT = [("causal", P), ("ones_half", P), ("pick_c0", 64), ("pick_c1", 64)]


def columns(table):
    at, out = 0, {}
    for name, n in table:
        out[name] = (at, at + n)
        at += n
    return out, at


class Steps:

    def __init__(self, sem, names):
        self.sem, self.names = sem, names.split()
        self.n = len(self.names)

    def at(self, name, r=0):
        return r * self.n + self.names.index(name) + 1

    def all(self, r):
        return r * self.n


def build(nc, a):
    F32, F32R, I32 = mybir.dt.float32, mybir.dt.float32r, mybir.dt.int32
    ALU, ACT, AX = mybir.AluOpType, mybir.ActivationFunctionType, mybir.AxisListType
    V, S, G, TE = nc.vector, nc.scalar, nc.gpsimd, nc.tensor
    ds = bass.ds
    ctx = ExitStack()
    with ctx:
        END = 229344

        def place(name, shape, dt=F32, at=None):
            size = 4 * int(np.prod(shape[1:]))
            size += -size % 32
            assert at[0] + size <= END, (name, at[0] + size)
            t = nc.alloc_sbuf_tensor_at(name, shape, dt, offset=at[0])
            at[0] += size
            return t

        def sem(name):
            return ctx.enter_context(nc.semaphore(name))

        hold = [16512]
        x = place("x", [P, KT, NT], at=hold)
        cst = place("cst", [P, columns(CONSTS)[1]], at=hold)
        par = place("par", [P, columns(PARAMS)[1]], at=hold)
        eps = place("eps", [P, 1], at=hold)
        one = place("one", [P, 1], at=hold)
        conv_end = place("conv_end", [P, FT, 2 + B], at=hold)
        raw = place("raw", [P, RAW, KD * P], at=hold)
        w_hi = place("w_hi", [P, 2, KD * P], F32R, at=hold)
        w_lo = place("w_lo", [P, 2, KD * P], F32R, at=hold)
        h_hi_at = hold[0]
        h_hi = place("h_hi", [P, KT, NT], F32R, at=hold)
        h_lo_at = hold[0]
        h_lo = place("h_lo", [P, KT, NT], F32R, at=hold)
        region = hold[0]
        norm_at = END - 5 * 4 * NT
        at = [norm_at]
        sq = place("sq", [P, 2, NT], at=at)
        rstd = place("rstd", [P, NT], at=at)
        hn = place("hn", [P, 2, NT], at=at)

        at = [region]
        z = place("z", [P, 28, NT], at=at)
        gates = place("gates", [P, NT], at=at)
        crec = place("crec", [P, columns(CONSTS_REC)[1]], at=at)
        r_intra = place("r_intra", [4, T], at=at)
        r_inter = place("r_inter", [4, T], at=at)
        r_negm = place("r_negm", [4, T], at=at)
        r_s = place("r_s", [4, 3 * B], at=at)
        m_out = place("m_out", [4, 1 + B], at=at)
        a_col = place("a_col", [P, NC_M, 4], at=at)
        n_end = place("n_end", [P, M_HEADS], at=at)
        n_s = place("n_s", [P, M_HEADS, B], at=at)
        work = at[0]
        at = [work]
        i_pre = place("i_pre", [4, NT], at=at)
        f_pre = place("f_pre", [4, NT], at=at)
        f_neg = place("f_neg", [4, NT], at=at)
        f_log = place("f_log", [4, NT], at=at)
        m_run = place("m_run", [4, T], at=at)
        b_row = place("b_row", [4, T], at=at)
        a_row = place("a_row", [4, T], at=at)
        at = [work]
        e_mat = place("e_mat", [P, NC_M, LC_M], at=at)
        w_int = place("w_int", [P, T], at=at)
        q_w = place("q_w", [P, T], at=at)
        k_tok = place("k_tok", [P, NC_M, P], at=at)
        v_tok = place("v_tok", [P, NC_M, P], at=at)
        v_end = place("v_end", [P, NC_M, 2, P], at=at)
        c_s = place("c_s", [P, B, P], at=at)
        kv = place("kv", [P, B, P], at=at)
        assert at[0] <= norm_at, (at[0], norm_at)
        at = [h_lo_at + 4 * NT * 4]
        h_head = place("h_head", [P, NT], at=at)
        den = place("den", [P, T], at=at)
        e_negm = place("e_negm", [P, T], at=at)
        w_s = place("w_s", [P, 3, B], at=at)
        nw = place("nw", [P, B], at=at)
        nq = place("nq", [P, B], at=at)
        v_ws = place("v_ws", [P, B], at=at)
        k_ws = place("k_ws", [P, B], at=at)
        den_s = place("den_s", [P, B], at=at)
        hnum_s = place("hnum_s", [P, B], at=at)
        c_n = place("c_n", [P, 2 * P], at=at)
        assert at[0] <= region
        at = [h_hi_at + 4 * NT * 4]
        diag_k = place("diag_k", [P, B, P], at=at)
        diag_q = place("diag_q", [P, B, P], at=at)
        assert at[0] <= h_lo_at
        at = [region]
        lx = place("lx", [P, 8, SUB, SUB], at=at)
        dg = place("dg", [P, 4, 512], at=at)
        ke = place("ke", [P, NC_G, 3, 48], at=at)
        g_vt = place("g_vt", [64, 2, NC_G, P], at=at)
        g_s = place("g_s", [P, P], at=at)
        assert at[0] <= region + 16 * NT * 4, at[0] - region - 16 * NT * 4
        at = [work]
        log_a = place("log_a", [P, G_PAIRS, NT], at=at)
        bc = place("bc", [P, T], at=at)
        sub0 = place("sub0", [P, NC_G, 4], at=at)
        a_end = place("a_end", [P, NC_G], at=at)
        a_s = place("a_s", [P, B], at=at)
        g_qs = place("g_qs", [P, T], at=at)
        g_qd = place("g_qd", [P, T], at=at)
        g_kd = place("g_kd", [P, T], at=at)
        g_att = place("g_att", [64, 2, NC_G, LC_G], at=at)
        g_kdt = place("g_kdt", [64, NC_G, P], at=at)
        g_h = place("g_h", [P, 2, NT], at=at)
        assert at[0] <= norm_at, (at[0], norm_at)
        ln_t = g_h
        at = [region]
        g_dv = place("g_dv", [P, 2, B, P], at=at)
        g_ss = place("g_ss", [P, B, P], at=at)
        g_kv = place("g_kv", [P, B, P], at=at)

        at = [region]
        a_hi = place("a_hi", [P, FT, NT], F32R, at=at)
        a_lo = place("a_lo", [P, FT, NT], F32R, at=at)
        ub = place("ub", [P, 2, 2 + NT], at=at)
        cc = place("cc", [P, NT], at=at)
        ge = place("ge", [P, NT], at=at)
        pr = place("pr", [P, NT], at=[norm_at])
        assert at[0] <= norm_at, (at[0], norm_at)

        at = [region]
        z2 = place("z2", [P, 24, NT], at=at)
        catt = place("catt", [P, columns(CONSTS_ATT)[1]], at=at)
        pages = place("pages", [P, 4, D_MODEL], at=at)
        ptab = place("ptab", [1, B * PAGES], I32, at=at)
        lam = place("lam", [P, 4], at=at)
        coef = place("coef", [P, 2], at=at)
        g_o2 = place("g_o2", [P, 1], at=at)
        att_work = at[0]
        qn = place("qn", [P, NT], at=at)
        kn = place("kn", [P, NT], at=at)
        vn = place("vn", [P, NT], at=at)
        v_t2 = place("v_t2", [P, 4, P], at=at)
        e_att = place("e_att", [P, 2, 2, T], at=at)
        a_att = place("a_att", [P, 2, T], at=at)
        at_t = place("at_t", [P, 2, T], at=at)
        mx = place("mx", [P, 2, 2], at=at)
        sm = place("sm", [P, 2, 2], at=at)
        rs = place("rs", [P, 2, 2], at=at)
        o_att = place("o_att", [P, T], at=at)
        assert at[0] <= norm_at, (at[0], norm_at)
        at = [att_work]
        qks = place("qks", [P, 2 * A_HEADS, B], at=at)
        qk_r = place("qk_r", [P, 2 * A_HEADS, B], at=at)
        qk_t = place("qk_t", [P, 2 * A_HEADS, B], at=at)
        qd = place("qd", [P, 2, A_HEADS, P], at=at)
        qb = place("qb", [P, 2, D_MODEL], at=at)
        s_prod = place("s_prod", [P, D_MODEL], at=at)
        s_sc = place("s_sc", [P, PAGES, P], at=at)
        s_row = place("s_row", [P, PAGES * P + 1], at=at)
        s_new = place("s_new", [P, P], at=at)
        s_small = place("s_small", [P, 4], at=at)
        s_pick = place("s_pick", [P, 64], at=at)
        s_at = place("s_at", [P, PAGES + 1, 64], at=at)
        s_o = place("s_o", [P, 64], at=at)
        s_o2 = place("s_o2", [P, 64], at=at)
        assert at[0] <= norm_at, (at[0], norm_at)

        ps = ctx.enter_context(nc.psum_tensor("ps", [P, 8, 512], F32))

        def p_(name, k=0, n=None):
            lo, hi = columns(PARAMS)[0][name]
            return par[:, lo + k:(hi if n is None else lo + k + n)]

        def c_(name):
            for table, t in ((CONSTS, cst), (CONSTS_REC, crec), (CONSTS_ATT, catt)):
                cols = columns(table)[0]
                if name in cols:
                    return t[:, cols[name][0]:cols[name][1]]

        def half(bank, h):
            return ps[:, bank + h, 0:HALF]

        def pair(bank):
            return ps[:, bank:bank + 2, 0:HALF]

        def two(ap):
            return ap.rearrange("p (a t) -> p a t", a=2)

        IDENT, ONES = c_("ident"), c_("ones")

        landed = [sem(f"landed{i}") for i in range(RAW)]
        hi_split, lo_split = sem("hi_split"), sem("lo_split")
        slab_done = sem("slab_done")
        drained = sem("drained")
        x_in, par_in = sem("x_in"), sem("par_in")
        crec_in, catt_in, ptab_in = sem("crec_in"), sem("catt_in"), sem("ptab_in")
        small_set = sem("small_set")
        outs = sem("outs")
        c_s_in, g_s_in = sem("c_s_in"), sem("g_s_in")
        c_out, cs_out, gs_out, gss_out = sem("c_out"), sem("cs_out"), sem("gs_out"), sem("gss_out")
        conv_out = sem("conv_out")
        dg_out, diag_in = sem("dg_out"), sem("diag_in")
        kn_out = sem("kn_out")
        page_in = [sem(f"page_in{i}") for i in range(4)]

        nA = Steps(sem("norm_act"), "sq0 sq1 sq2 sq3 sq4 sq5 sq6 sq7 lr rms hi0 hi1 hi2 hi3 hi4 hi5 hi6 hi7")
        nD = Steps(sem("norm_dve"), "n0 lo0 n1 lo1 n2 lo2 n3 lo3 n4 lo4 n5 lo5 n6 lo6 n7 lo7")
        nP = Steps(sem("norm_pe"), "s0 s1 s2 s3 s4 s5 s6 s7")
        gtD = Steps(sem("gate_dve"), "f i neg lf b m lfm ms ri a nm r20 r21 r22 r23 s0 s1 s2 mo0")
        gtA = Steps(sem("gate_act"), "sig silu exp ln acol")
        gtP = Steps(sem("gate_pe"), "acol")
        mP = Steps(sem("mlstm_pe"), "bc0 bc1 bc2 bcs ktr vtr scores num0 st0 num1 st1 num2 st2 num3 st3 kb qb dens ssq")
        mA = Steps(sem("mlstm_act"), "ws wi en e kt vt abs abs_s sq lr rms hi")
        mD = Steps(sem("mlstm_dve"), "em qw ve p cn0 cn1 cn2 cn3 nend den rden h vw kw nw ns nq kv cs cq hs dn rd hs2 t mix lo")
        mG = Steps(sem("mlstm_pool"), "dk dq cw")
        lP = Steps(sem("decay_pe"), "up")
        lA = Steps(sem("decay_act"), "exp ln")
        lD = Steps(sem("decay_dve"), "z neg lf la q8 sub0")
        fA = Steps(sem("ffn_act"), "u tail gelu hi")
        fD = Steps(sem("ffn_dve"), "t0 t1 s1 t2 s0 prod lo")
        gP = Steps(sem("gla_pe"), "dg0 dg1 dg2 dg3 off vt kdt o0 s0 o1 s1 o2 s2 o3 s3 o4 s4 o5 s5 o6 s6 o7 s7 vb os ssq0 ssq1")
        gA = Steps(sem("gla_act"), "eb qe aend kend ex0 dgc0 ex1 dgc1 ex2 dgc2 ex3 dgc3 ke at vt kdt as o0 o1 sq0 sq1 lr0 rms0 lr1 rms1 hi0 hi1")
        gD = Steps(sem("gla_dve"), "bc sb qe ke kem kend x0 xm0 xk0 xq0 x1 xm1 xk1 xq1 x2 xm2 xk2 xq2 x3 xm3 xk3 xq3 qs qd ks kd "
                   "c0 c1 c2 c3 c4 c5 c6 c7 kv ss h0 h1 hs0 hs1 t0 mix0 lo0 t1 mix1 lo1")
        gG = Steps(sem("gla_pool"), "za dv sa")
        small = Steps(sem("small"), "one eps")
        pads = Steps(sem("pads"), "pad")
        aP = Steps(sem("att_pe"), "vtr ssq ssk sc0 sc1 tr0 pv0 sc2 tr1 pv1 sc3 tr2 pv2 tr3 pv3 sso")
        aA = Steps(sem("att_act"), "v vt sqq lrq rq sqk lrk rk ex0 ex1 att0 ex2 att1 ex3 att2 att3 sqo lro ro hi")
        aD = Steps(sem("att_dve"), "qn kn "
                   + " ".join(f"m{i} x{i} nx{i} r{i} rc{i} e{i} a{i}" for i in range(4)) + " mix lo")
        lamP = Steps(sem("lam_pe"), "sum")
        lamA = Steps(sem("lam_act"), "exp")
        lamD = Steps(sem("lam_dve"), "prod sub lam c0 c1 go")
        sP = Steps(sem("samp_pe"), "ssq")
        qbP = Steps(sem("query_pe"), "qb")
        qbA = Steps(sem("query_act"), "qb")
        qbG = Steps(sem("query_pool"), "qd")
        kD = Steps(sem("keys_dve"), "mul0 red0 mul1 red1 mul2 red2 mul3 red3")
        vP = Steps(sem("values_pe"), "v0 v1 v2 v3")
        sA = Steps(sem("samp_act"), "sq lr rms")
        sD = Steps(sem("samp_dve"), "tq tk nq nk nw0 nw1")
        tP = Steps(sem("soft_pe"), "tr new at atn ssq")
        tA = Steps(sem("soft_act"), "row ex at sq lr rms hi")
        tD = Steps(sem("soft_dve"), "newc mx nmx r rc pick0 pick1 ps o1 o2 o3 t mix lo")

        block = ctx.enter_context(nc.Block())

        def wait(eng, steps, name, r=0):
            eng.wait_ge(steps.sem, steps.at(name, r))

        def barrier_free_value(v):
            return not isinstance(v, int) or v > 0

        @block.sync
        def _(sp):
            def load_slab(name, nk, i, s):
                f = FIRST[name]
                before = 4 * i + (f + s - RAW + 1)
                if barrier_free_value(before):
                    sp.wait_ge(lo_split, before)
                slot = (f + s) % RAW
                sp.dma_start(raw[:, slot, 0:nk * P], a["w_" + name][4 * i + s]).then_inc(landed[slot], 16)

            def load_phase(name, groups):
                nk = dict((n, k) for n, _, k in PHASES)[name]
                first, end = groups
                if end - first <= 1:
                    for i in range(first, end):
                        for s in range(4):
                            load_slab(name, nk, i, s)
                else:
                    with sp.Fori(first, end) as i:
                        for s in range(4):
                            load_slab(name, nk, i, s)

            sp.dma_start(x[:, :, :], a["x"]).then_inc(x_in, 16)
            load_phase("rec_in", (0, 1))
            sp.dma_start(crec[:, :], a["crec"]).then_inc(crec_in, 16)
            load_phase("rec_in", (1, 7))
            load_slab("rec_in", KT, 7, 0)
            load_phase("rec_out", (0, 1))
            for p in range(G_PAIRS):
                wait(sp, gA, "dgc3", p)
                wait(sp, gG, "za", p)
                for hh in range(2):
                    sp.dma_start(a["blocks"][p, hh].rearrange("(q m) x -> m q x", m=4),
                                 dg[hh::32, :, :]).then_inc(dg_out, 16)
                sp.wait_ge(dg_out, 32 * (p + 1))
                for j in range(4):
                    t = slice(SUB * j, SUB * (j + 1))
                    src = a["blocks"][p].rearrange("h (c j) (u s t) -> j u s h c t", c=NC_G, u=2, t=SUB)[j // 2, j % 2]
                    for hh in range(2):
                        sp.dma_start(g_att[t, hh, :, t], src[:, hh]).then_inc(diag_in, 16)
            load_phase("rec_out", (1, 2))
            load_phase("ffn0", (0, S_FFN // 4))
            load_phase("down0", (0, S_DOWN // 4))
            load_phase("att_in", (0, S_ATT_IN // 4))
            load_phase("att_out", (0, 1))
            sp.wait_ge(slab_done, FIRST["att_in"])
            sp.dma_start(ptab[:, :], a["page_table"]).then_inc(ptab_in, 16)
            sp.wait_ge(ptab_in, 16)

            def load_pages(cache, b, user, step):
                for j in range(PAGES):
                    if step is not None:
                        user(j)
                    page = sp.value_load(ptab[0:1, ds(PAGES * b + j, 1)], min_val=0, max_val=POOL - 1)
                    sp.dma_start(pages[:, j, :], a[cache][page]).then_inc(page_in[j], 16)

            load_pages("cache_k", 0, None, None)
            with sp.Fori(1, B) as b:
                load_pages("cache_k", b, lambda j: sp.wait_ge(kD.sem, kD.at(f"mul{j}", b - 1)), True)
            load_pages("cache_v", 0, lambda j: wait(sp, kD, f"mul{j}", B - 1), True)
            with sp.Fori(1, B) as b:
                load_pages("cache_v", b, lambda j: sp.wait_ge(vP.sem, vP.at(f"v{j}", b - 1)), True)
            load_phase("att_out", (1, 2))
            load_phase("ffn1", (0, S_FFN // 4))
            load_phase("down1", (0, S_DOWN // 4))

        @block.tensor
        def _(pe):
            def multiply(name, hi, lo, i, s, bank, k_at, ks, first, last, ready=None):
                f = FIRST[name]
                buf = (f + s) % 2
                pe.wait_ge(lo_split, 4 * i + (f + s + 1))
                free = 4 * i + (f + s - 3)
                if barrier_free_value(free):
                    pe.wait_ge(drained, free)
                for k in range(ks):
                    if ready is not None:
                        wait(pe, nD, f"lo{k}", ready)
                    w = slice(k * P, (k + 1) * P)
                    for w_part, parts in ((w_hi, (hi, lo)), (w_lo, (hi,))):
                        for m_part in parts:
                            for h in range(2):
                                start = first and k == 0 and w_part is w_hi and m_part is hi
                                stop = last and k == ks - 1 and w_part is w_lo
                                ins = TE.matmul(half(bank, h), w_part[:, buf, w],
                                                m_part[:, k_at + k, h * HALF:(h + 1) * HALF],
                                                start=start, stop=stop)
                ins.then_inc(slab_done, 1)

            def project(name, n, norm=None):
                def group(i, slabs=4):
                    for s in range(slabs):
                        multiply(name, h_hi, h_lo, i, s, 2 * s, 0, KT, True, True,
                                 norm if s == 0 else None)
                groups = n // 4
                group(0)
                if groups > 2:
                    with pe.Fori(1, groups) as i:
                        group(i)
                elif groups == 2:
                    group(1)
                if n % 4:
                    group(groups, n % 4)

            def down(name):
                with pe.Fori(0, S_DOWN // 4) as i:
                    for s in range(4):
                        multiply(name, a_hi, a_lo, i, s, 4 * (s // 2), KD * (s % 2), KD, s % 2 == 0, s % 2 == 1)

            def norm(r, bank, after=None):
                if after is not None:
                    pe.wait_ge(drained, after)
                for c in range(KT):
                    wait(pe, nA, f"sq{c}", r)
                    for h in range(2):
                        ins = TE.matmul(half(bank, h), ONES, sq[:, c % 2, h * HALF:(h + 1) * HALF],
                                        start=c == 0, stop=c == KT - 1)
                    ins.then_inc(nP.sem, 1)

            pe.wait_ge(par_in, 32)
            norm(0, 6)
            project("rec_in", S_REC_IN, 0)

            pe.wait_ge(drained, S_REC_IN)
            wait(pe, gtD, "a")
            for c in range(NC_M):
                ins = TE.transpose(ps[:, 7, 4 * c:4 * c + 4], a_row[0:4, c * P:(c + 1) * P], IDENT[0:4, 0:4])
            ins.then_inc(gtP.sem, 1)

            SEL = c_("sel_head").rearrange("p (h m) -> p h m", h=M_HEADS)
            for h in range(M_HEADS):
                q, k, v = z[:, h, :], z[:, 4 + h, :], z[:, 8 + h, :]
                if h == 0:
                    wait(pe, gtD, "mo0")
                    wait(pe, gtA, "acol")
                else:
                    pe.wait_ge(mD.sem, mD.all(h))
                for bank, row in enumerate((r_intra, r_inter, r_negm)):
                    TE.matmul(ps[:, bank, :], SEL[0:4, h, :], row[:, :], start=True, stop=True).then_inc(mP.sem, 1)
                TE.matmul(ps[:, 7, 0:3 * B], SEL[0:4, h, :], r_s[:, :], start=True, stop=True).then_inc(mP.sem, 1)
                for bank, rows in ((4, k), (5, v)):
                    for c in range(NC_M):
                        ins = TE.transpose(ps[:, bank, c * P:(c + 1) * P], rows[:, c * P:(c + 1) * P], IDENT)
                    ins.then_inc(mP.sem, 1)
                for c in range(NC_M):
                    t = slice(c * P, (c + 1) * P)
                    ins = TE.matmul(ps[:, 3, t], k[:, t], q[:, t], start=True, stop=True)
                ins.then_inc(mP.sem, 1)
                wait(pe, mD, "p", h)
                wait(pe, mA, "ws", h)
                for c in range(NC_M):
                    t = slice(c * P, (c + 1) * P)
                    if c:
                        wait(pe, mD, f"cn{c - 1}", h)
                    TE.matmul(ps[:, 6, t], v_tok[:, c, :], e_mat[:, c, :], start=True, stop=c == 0)
                    ins = TE.matmul(ps[:, 7, t], ONES, e_mat[:, c, :], start=True, stop=c == 0) if c == 0 else None
                    if c:
                        TE.matmul(ps[:, 6, t], c_n[:, 0:P], q_w[:, t], start=False, stop=True)
                        TE.matmul(ps[:, 7, t], ONES, e_mat[:, c, :], start=True, stop=False)
                        ins = TE.matmul(ps[:, 7, t], c_n[:, P:2 * P], q_w[:, t], start=False, stop=True)
                    ins.then_inc(mP.sem, 1)
                    if c == 0:
                        wait(pe, mD, "em", h)
                        wait(pe, mA, "en", h)
                    TE.matmul(ps[:, c % 2, 0:2 * P], k_tok[:, c, :], v_end[:, c, :, :].rearrange("p a v -> p (a v)"),
                              start=True, stop=True).then_inc(mP.sem, 1)
                wait(pe, mG, "dk", h)
                for n in range(2):
                    ins = TE.matmul(ps[:, 4 + n, :], ONES, diag_k[:, 4 * n:4 * n + 4, :].rearrange("p b k -> p (b k)"),
                                    start=True, stop=True)
                ins.then_inc(mP.sem, 1)
                wait(pe, mG, "dq", h)
                wait(pe, mD, "cn3", h)
                for n in range(2):
                    ins = TE.matmul(ps[:, n, :], ONES, diag_q[:, 4 * n:4 * n + 4, :].rearrange("p b k -> p (b k)"),
                                    start=True, stop=True)
                ins.then_inc(mP.sem, 1)
                wait(pe, mD, "nq", h)
                TE.matmul(ps[:, 2, 0:B], ONES, nq[:, :], start=True, stop=True).then_inc(mP.sem, 1)
                wait(pe, mA, "sq", h)
                wait(pe, mD, "kv", h)
                for n in range(2):
                    ins = TE.matmul(half(4, n), ONES, sq[:, 0, n * HALF:(n + 1) * HALF], start=True, stop=True)
                ins.then_inc(mP.sem, 1)

            pe.wait_ge(mD.sem, mD.all(M_HEADS))
            for p in range(G_PAIRS):
                for n in range(2):
                    ins = TE.matmul(half(2 * p, n), c_("w_gate_up")[64:80, p * P:(p + 1) * P],
                                    gates[64:80, n * HALF:(n + 1) * HALF], start=True, stop=True)
            ins.then_inc(lP.sem, 1)
            wait(pe, lD, "z")
            for p in range(G_PAIRS):
                if p:
                    pe.wait_ge(gD.sem, gD.all(p))
                for n in range(4):
                    wait(pe, gD, f"xq{n}", p)
                    flat = lx[:, :, :, :].rearrange("p b s t -> p (b s t)")
                    for m in range(4):
                        ins = TE.matmul(ps[32 * m:32 * m + 32, n, :], c_("half_sum"), flat[:, 512 * m:512 * m + 512],
                                        start=True, stop=True)
                    ins.then_inc(gP.sem, 1)
                wait(pe, gD, "qs", p)
                wait(pe, gD, "ks", p)
                for hh in range(2):
                    r = slice(64 * hh, 64 * hh + 64)
                    for c in range(NC_G):
                        for j in range(1, 4):
                            at_ = c * LC_G + j * SUB
                            ins = TE.matmul(ps[0:SUB * j, 4 + hh, at_:at_ + SUB], ke[r, c, j - 1, 0:SUB * j],
                                            g_qs[r, at_:at_ + SUB], start=True, stop=True)
                ins.then_inc(gP.sem, 1)
                wait(pe, gA, "dgc1", p)
                for hh in range(2):
                    for c in range(NC_G):
                        bank = (6, 0)[hh] + c // 4
                        ins = TE.transpose(ps[0:64, bank, (c % 4) * P:(c % 4 + 1) * P],
                                           z[:, 20 + 2 * p + hh, c * LC_G:(c + 1) * LC_G], IDENT)
                ins.then_inc(gP.sem, 1)
                wait(pe, gD, "kd", p)
                wait(pe, gA, "dgc3", p)
                for c in range(NC_G):
                    ins = TE.transpose(ps[0:64, 2 + c // 4, (c % 4) * P:(c % 4 + 1) * P],
                                       g_kd[:, c * LC_G:(c + 1) * LC_G], IDENT)
                ins.then_inc(gP.sem, 1)
                wait(pe, gA, "at", p)
                wait(pe, gA, "kdt", p)
                pe.wait_ge(diag_in, 8 * 16 * (p + 1))
                for c in range(NC_G):
                    t = slice(c * LC_G, (c + 1) * LC_G)
                    if c:
                        wait(pe, gD, f"c{c - 1}", p)
                    for hh in range(2):
                        r = slice(64 * hh, 64 * hh + 64)
                        ins = TE.matmul(ps[:, 4 + hh, t], g_vt[:, hh, c, :], g_att[:, hh, c, :], start=True, stop=True)
                        if c:
                            ins = TE.matmul(ps[:, 6 + hh, t], g_s[r, :], g_qd[r, t], start=True, stop=True)
                    ins.then_inc(gP.sem, 1)
                    for hh in range(2):
                        r = slice(64 * hh, 64 * hh + 64)
                        ins = TE.matmul(ps[r, c % 2, 0:P], g_kdt[:, c, r], g_vt[:, hh, c, :], start=True, stop=True)
                    ins.then_inc(gP.sem, 1)
                wait(pe, gG, "dv", p)
                for n in range(2):
                    for hh, half_ones in ((0, c_("ones_lo")), (1, c_("ones_hi"))):
                        ins = TE.matmul(ps[:, 2 + n, :], half_ones,
                                        g_dv[:, hh, 4 * n:4 * n + 4, :].rearrange("p b v -> p (b v)"),
                                        start=hh == 0, stop=hh == 1)
                ins.then_inc(gP.sem, 1)
                wait(pe, gD, "ss", p)
                for hh in range(2):
                    r = slice(64 * hh, 64 * hh + 64)
                    for b in range(B):
                        ins = TE.matmul(ps[:, hh, 256 + b:257 + b], g_ss[r, b, :], z[r, 16 + p, T + b:T + b + 1],
                                        start=True, stop=True)
                ins.then_inc(gP.sem, 1)
                for hh in range(2):
                    wait(pe, gA, f"sq{hh}", p)
                    wait(pe, gD, f"h{hh}", p)
                    bank = (4, 6)[hh]
                    for n in range(2):
                        ins = TE.matmul(half(bank, n), ONES, sq[:, hh, n * HALF:(n + 1) * HALF], start=True, stop=True)
                    ins.then_inc(gP.sem, 1)

            pe.wait_ge(gD.sem, gD.all(G_PAIRS))
            project("rec_out", S_OUT)
            norm(1, 0, FIRST["rec_out"] + 5)
            project("ffn0", S_FFN, 1)
            wait(pe, fD, "lo", FT - 1)
            down("down0")
            norm(2, 6)
            project("att_in", S_ATT_IN, 2)

            pe.wait_ge(catt_in, 16)
            wait(pe, lamD, "prod")
            TE.matmul(ps[:, 0, 0:2], ONES[0:64, :], lam[0:64, 0:2], start=True, stop=True).then_inc(lamP.sem, 1)
            wait(pe, lamD, "go")
            HALVES = c_("ones_half")

            def head(h, first):
                wait(pe, aA, "v", h)
                if not first:
                    pe.wait_ge(aD.sem, aD.all(h))
                for c in range(4):
                    ins = TE.transpose(ps[:, 6, c * P:(c + 1) * P], vn[:, c * P:(c + 1) * P], IDENT)
                ins.then_inc(aP.sem, 1)
                for n, (step, bank) in enumerate((("sqq", 0), ("sqk", 2))):
                    wait(pe, aA, step, h)
                    for g in range(2):
                        ins = TE.matmul(half(bank, g), HALVES, sq[:, n, g * HALF:(g + 1) * HALF], start=True, stop=True)
                    ins.then_inc(aP.sem, 1)

                def scores(i):
                    if i == 0:
                        wait(pe, aD, "kn", h)
                    if i >= 2:
                        wait(pe, aA, f"ex{i - 2}", h)
                    for c in range(2):
                        r = slice(64 * c, 64 * c + 64)
                        ins = TE.matmul(ps[:, 2 * (i % 2) + c, 0:(i + 1) * P], qn[r, i * P:(i + 1) * P],
                                        kn[r, 0:(i + 1) * P], start=True, stop=True)
                    ins.then_inc(aP.sem, 1)

                def values(i):
                    wait(pe, aD, f"a{i}", h)
                    if i == 0:
                        wait(pe, aA, "vt", h)
                    if i >= 2:
                        wait(pe, aA, f"att{i - 2}", h)
                    for c in range(i + 1):
                        ins = TE.transpose(ps[:, 4 + i % 2, c * P:(c + 1) * P], a_att[:, i % 2, c * P:(c + 1) * P], IDENT)
                    ins.then_inc(aP.sem, 1)
                    wait(pe, aA, f"att{i}", h)
                    for c in range(i + 1):
                        ins = TE.matmul(ps[:, 7, i * P:(i + 1) * P], v_t2[:, c, :], at_t[:, i % 2, c * P:(c + 1) * P],
                                        start=c == 0, stop=c == i)
                    ins.then_inc(aP.sem, 1)

                scores(0)
                scores(1)
                values(0)
                scores(2)
                values(1)
                scores(3)
                values(2)
                values(3)
                wait(pe, aA, "sqo", h)
                TE.matmul(ps[:, 6, :], ONES, sq[:, 0, 0:T], start=True, stop=True).then_inc(aP.sem, 1)

            head(0, True)
            with pe.Fori(1, A_HEADS) as h:
                head(h, False)

            wait(pe, sA, "sq")
            pe.wait_ge(aD.sem, aD.all(A_HEADS))
            TE.matmul(ps[:, 0, 0:P], HALVES, qk_r[:, :, :].rearrange("p h b -> p (h b)"),
                      start=True, stop=True).then_inc(sP.sem, 1)

            def query(b, bank, buf, r):
                wait(pe, qbG, "qd", r)
                for n in range(2):
                    ins = TE.matmul(ps[:, bank + n, :], ONES, qd[:, buf, 4 * n:4 * n + 4, :].rearrange("p h k -> p (h k)"),
                                    start=True, stop=True)
                ins.then_inc(qbP.sem, 1)

            with pe.Fori(0, B // 2) as i:
                for u in range(2):
                    query(None, 2 + 2 * u, u, 2 * i + u)

            wait(pe, kD, "red3", B - 1)
            for j in range(PAGES):
                ins = TE.transpose(ps[:, 1, j * P:(j + 1) * P], s_sc[:, j, :], IDENT)
            ins.then_inc(tP.sem, 1)
            wait(pe, sD, "nw1")
            TE.matmul(ps[:, 6, 0:1], s_new[:, :], ONES[:, 0:1], start=True, stop=True).then_inc(tP.sem, 1)
            wait(pe, tD, "ps")
            for j in range(PAGES):
                ins = TE.matmul(ps[:, 2, j * 64:(j + 1) * 64], s_row[:, j * P:(j + 1) * P], s_pick[:, :],
                                start=True, stop=True)
            ins.then_inc(tP.sem, 1)
            TE.matmul(ps[:, 3, 0:64], s_new[:, :], s_pick[:, :], start=True, stop=True).then_inc(tP.sem, 1)
            wait(pe, tA, "at")
            with pe.Fori(0, B) as b:
                for j in range(PAGES):
                    pe.wait_ge(page_in[j], 16 * (B + b) + 16)
                    for h in range(A_HEADS):
                        ins = TE.matmul(ps[:, 4, ds(8 * b + (64 * j + h), 1)], pages[:, j, h * P:(h + 1) * P],
                                        s_at[:, j, ds(8 * b + h, 1)], start=True, stop=True)
                    ins.then_inc(vP.sem, 1)
            wait(pe, tA, "sq")
            TE.matmul(ps[:, 5, 0:64], ONES, qk_t[:, 0:A_HEADS, :].rearrange("p h b -> p (h b)"),
                      start=True, stop=True).then_inc(tP.sem, 1)
            wait(pe, tD, "lo")
            project("att_out", S_OUT)
            norm(3, 0, FIRST["att_out"] + 5)
            project("ffn1", S_FFN, 3)
            wait(pe, fD, "lo", 2 * FT - 1)
            down("down1")

        def walk(eng, name, split, drain):
            nk = dict((n, k) for n, _, k in PHASES)[name]
            total = dict((n, s) for n, s, _ in PHASES)[name]
            loops = (total - 2) // 4

            def step(i, s, left=2):
                if left >= 2:
                    split(name, i, s + 2, nk)
                else:
                    order = [n for n, _, _ in PHASES]
                    after = order.index(name) + 1
                    if after < len(PHASES):
                        split(order[after], 0, 1 - left, PHASES[after][2])
                drain(i, s)

            peeled = 1 if loops == 1 or FIRST[name] == 0 else 0
            for s in range(4 * peeled):
                step(0, s)
            if loops > peeled:
                with eng.Fori(peeled, loops) as i:
                    for s in range(4):
                        step(i, s)
            for n in range(4 * loops, total):
                step(loops, n - 4 * loops, total - 1 - n)

        @block.scalar
        def _(act):
            LN_EXP = "natural_log_exp_and_others"

            def rsqrt(out, total, n, steps, ln, r=0):
                S.activation(out, total, ACT.Ln, bias=eps[:, :], scale=1.0 / n).then_inc(steps.sem, 1)
                wait(act, steps, ln, r)
                return S.activation(out, out, ACT.Exp, scale=-0.5)

            def split(name, i, s, nk):
                n = FIRST[name] + s
                act.wait_ge(landed[n % RAW], 16 * (i + n // RAW + 1))
                if barrier_free_value(4 * i + (n - 1)):
                    act.wait_ge(slab_done, 4 * i + (n - 1))
                S.copy(w_hi[:, n % 2, 0:nk * P], raw[:, n % RAW, 0:nk * P]).then_inc(hi_split, 1)

            def norm(r, bank, before):
                S.preload_act_table_set(LN_EXP)
                for c in range(KT):
                    before(c)
                    if c >= 2:
                        wait(act, nP, f"s{c - 2}", r)
                    S.activation(sq[:, c % 2, :], x[:, c, :], ACT.Square).then_inc(nA.sem, 1)
                wait(act, nP, "s7", r)
                wait(act, small, "eps")
                rsqrt(two(rstd[:, :]), pair(bank), D_MODEL, nA, "lr", r).then_inc(nA.sem, 1)
                for c in range(KT):
                    wait(act, nD, f"n{c}", r)
                    S.copy(h_hi[:, c, :], hn[:, c % 2, :]).then_inc(nA.sem, 1)

            def tile_out(name, out):
                def drain(i, s):
                    act.wait_ge(slab_done, 4 * i + (FIRST[name] + s + 1))
                    S.copy(two(out[:, 4 * i + s, :]) if isinstance(i, int) else
                           out[:, ds(4 * i + s, 1), :].rearrange("p o (a t) -> p (o a) t", a=2),
                           pair(2 * (s % 4))).then_inc(drained, 1)
                return drain

            def rec_drain(i, s):
                if isinstance(i, int) and 4 * i + s == S_REC_IN - 1:
                    act.wait_ge(slab_done, S_REC_IN)
                    S.copy(two(gates[:, :]), pair(2 * (s % 4))).then_inc(drained, 1)
                else:
                    tile_out("rec_in", z)(i, s)

            def nothing(i, s):
                pass

            def ffn(layer):
                name = f"ffn{layer}"

                def drain(i, s):
                    r = 2 * i + (s // 2 + layer * FT)
                    m = 2 * i + s // 2
                    act.wait_ge(slab_done, 4 * i + (FIRST[name] + s + 1))
                    if s % 2 == 0:
                        S.copy(two(ub[:, s // 2, 2:2 + NT]), pair(2 * (s % 4))).then_inc(fA.sem, 1)
                        S.copy(conv_end[:, ds(m, 1), :] if not isinstance(m, int) else conv_end[:, m:m + 1, :],
                               ps[:, 2 * s + 1:2 * s + 2, HALF - 2 - B:HALF]).then_inc(fA.sem, 1)
                        act.wait_ge(fD.sem, fD.at("s0", r))
                        S.activation(ge[:, :], cc[:, :], ACT.Gelu_apprx_tanh).then_inc(fA.sem, 1)
                    else:
                        act.wait_ge(fD.sem, fD.at("prod", r))
                        S.copy(a_hi[:, ds(m, 1), :] if not isinstance(m, int) else a_hi[:, m:m + 1, :],
                               pr[:, :].rearrange("p (o t) -> p o t", o=1)).then_inc(fA.sem, 1)
                S.preload_act_table(ACT.Gelu_apprx_tanh)
                if layer:
                    act.wait_ge(conv_out, 16)
                walk(act, name, split, drain)

            act.dma_start(par[:, :], a["par"]).then_inc(par_in, 16)
            act.dma_start(cst[:, :], a["cst"]).then_inc(par_in, 16)
            act.wait_ge(x_in, 16)
            norm(0, 6, lambda c: None)
            split("rec_in", 0, 0, KT)
            split("rec_in", 0, 1, KT)
            walk(act, "rec_in", split, rec_drain)

            act.wait_ge(drained, S_REC_IN)
            S.activation(z[:, 12:16, :], z[:, 12:16, :], ACT.Sigmoid).then_inc(gtA.sem, 1)
            S.activation(z[:, 24:28, :], z[:, 24:28, :], ACT.Silu).then_inc(gtA.sem, 1)
            S.preload_act_table_set(LN_EXP)
            wait(act, gtD, "neg")
            S.activation(f_log[:, :], f_neg[:, :], ACT.Exp).then_inc(gtA.sem, 1)
            wait(act, gtA, "exp")
            S.activation(f_log[:, :], f_log[:, :], ACT.Ln, bias=one[0:4, :]).then_inc(gtA.sem, 1)
            wait(act, gtP, "acol")
            S.copy(a_col[:, :, :], ps[:, 7, 0:4 * NC_M].rearrange("p (c h) -> p c h", h=4)).then_inc(gtA.sem, 1)

            for h in range(M_HEADS):
                wait(act, mP, "bcs", h)
                S.activation(w_s[:, :, :].rearrange("p a b -> p (a b)"), ps[:, 7, 0:3 * B], ACT.Exp).then_inc(mA.sem, 1)
                S.activation(w_int[:, :], ps[:, 1, :], ACT.Exp).then_inc(mA.sem, 1)
                S.activation(e_negm[:, :], ps[:, 2, :], ACT.Exp).then_inc(mA.sem, 1)
                wait(act, mD, "em", h)
                for c in range(NC_M):
                    ins = S.activation(e_mat[:, c, :], e_mat[:, c, :], ACT.Exp, bias=a_col[:, c, h:h + 1])
                ins.then_inc(mA.sem, 1)
                wait(act, mP, "ktr", h)
                S.copy(k_tok[:, :, :].rearrange("p c k -> p (c k)"), ps[:, 4, :]).then_inc(mA.sem, 1)
                wait(act, mP, "vtr", h)
                S.copy(v_tok[:, :, :].rearrange("p c k -> p (c k)"), ps[:, 5, :]).then_inc(mA.sem, 1)
                wait(act, mP, "num3", h)
                S.activation(den[:, :], ps[:, 7, :], ACT.Abs).then_inc(mA.sem, 1)
                wait(act, mP, "dens", h)
                S.activation(den_s[:, :], ps[:, 2, 0:B], ACT.Abs).then_inc(mA.sem, 1)
                wait(act, mD, "hs2", h)
                S.activation(sq[:, 0, :], h_head[:, :], ACT.Square).then_inc(mA.sem, 1)
                wait(act, mP, "ssq", h)
                rsqrt(two(rstd[:, :]), pair(4), P, mA, "lr", h).then_inc(mA.sem, 1)
                wait(act, mD, "mix", h)
                S.copy(h_hi[:, h, :], hn[:, 1, :]).then_inc(mA.sem, 1)

            wait(act, lD, "neg")
            S.activation(ln_t[:, :, :], ln_t[:, :, :], ACT.Exp).then_inc(lA.sem, 1)
            wait(act, lA, "exp")
            S.activation(ln_t[:, :, :], ln_t[:, :, :], ACT.Ln, bias=one[:, :]).then_inc(lA.sem, 1)
            for p in range(G_PAIRS):
                wait(act, gD, "bc", p)
                S.activation(g_qd[:, :], bc[:, :], ACT.Exp).then_inc(gA.sem, 1)
                wait(act, gD, "qe", p)
                S.activation(g_qs[:, :], g_qs[:, :], ACT.Exp).then_inc(gA.sem, 1)
                S.activation(a_end[:, :], bc[:, LC_G - 1::LC_G], ACT.Exp).then_inc(gA.sem, 1)
                wait(act, gD, "kend", p)
                S.activation(g_kd[:, :], g_kd[:, :], ACT.Exp).then_inc(gA.sem, 1)
                flat = lx[:, :, :, :].rearrange("p b s t -> p (b s t)")
                if p:
                    act.wait_ge(gss_out, 16)
                for n in range(4):
                    wait(act, gD, f"xm{n}", p)
                    S.activation(flat, flat, ACT.Exp).then_inc(gA.sem, 1)
                    wait(act, gP, f"dg{n}", p)
                    S.copy(dg[:, n, :], ps[:, n, :]).then_inc(gA.sem, 1)
                wait(act, gD, "kem", p)
                S.activation(ke[:, :, :, :].rearrange("p c j s -> p (c j s)"),
                             ke[:, :, :, :].rearrange("p c j s -> p (c j s)"), ACT.Exp).then_inc(gA.sem, 1)
                wait(act, gP, "off", p)
                wait(act, gG, "za", p)
                for hh in range(2):
                    for j in range(1, 4):
                        r, t = slice(0, SUB * j), slice(SUB * j, SUB * (j + 1))
                        ins = S.copy(g_att[r, hh, :, t],
                                     ps[r, 4 + hh, :].rearrange("p (c t) -> p c t", c=NC_G)[:, :, t])
                ins.then_inc(gA.sem, 1)
                wait(act, gP, "vt", p)
                for hh in range(2):
                    bank = (6, 0)[hh]
                    ins = S.copy(g_vt[:, hh, :, :].rearrange("p (n c) v -> p n (c v)", n=2), ps[0:64, bank:bank + 2, :])
                ins.then_inc(gA.sem, 1)
                wait(act, gP, "kdt", p)
                S.copy(g_kdt[:, :, :].rearrange("p (n c) v -> p n (c v)", n=2), ps[0:64, 2:4, :]).then_inc(gA.sem, 1)
                S.activation(a_s[:, :], log_a[:, p, T:NT], ACT.Exp).then_inc(gA.sem, 1)
                for hh in range(2):
                    wait(act, gP, "o7", p)
                    S.copy(g_h[:, hh, LC_G:T], ps[:, 6 + hh, LC_G:T]).then_inc(gA.sem, 1)
                for hh in range(2):
                    wait(act, gD, f"hs{hh}", p)
                    S.activation(sq[:, hh, :], g_h[:, hh, :], ACT.Square).then_inc(gA.sem, 1)
                for hh in range(2):
                    wait(act, gP, f"ssq{hh}", p)
                    if hh:
                        wait(act, gD, "t0", p)
                    rsqrt(two(rstd[:, :]), pair((4, 6)[hh]), P, gA, f"lr{hh}", p).then_inc(gA.sem, 1)
                for hh in range(2):
                    wait(act, gD, f"mix{hh}", p)
                    S.copy(h_hi[:, 4 + 2 * p + hh, :], hn[:, hh, :]).then_inc(gA.sem, 1)

            walk(act, "rec_out", split, nothing)
            norm(1, 0, lambda c: act.wait_ge(drained, FIRST["rec_out"] + c + 1))
            ffn(0)
            walk(act, "down0", split, nothing)
            norm(2, 6, lambda c: act.wait_ge(drained, FIRST["down0"] + 2 * (c + 1)))
            walk(act, "att_in", split, tile_out("att_in", z2))

            S.preload_act_table_set(LN_EXP)
            wait(act, lamP, "sum")
            S.activation(lam[:, 2:4], ps[:, 0, 0:2], ACT.Exp).then_inc(lamA.sem, 1)

            def head(h, first):
                def tile_of(k):
                    return z2[:, k + h, :] if isinstance(h, int) else z2[:, ds(h + k, 1), :].rearrange("p o t -> p (o t)")
                if not first:
                    act.wait_ge(aD.sem, aD.all(h))
                else:
                    act.wait_ge(drained, FIRST["att_out"])
                S.copy(vn[:, :], tile_of(16)).then_inc(aA.sem, 1)
                wait(act, aP, "vtr", h)
                S.copy(v_t2[:, :, :].rearrange("p c v -> p (c v)"), ps[:, 6, :]).then_inc(aA.sem, 1)
                S.activation(sq[:, 0, :], tile_of(0), ACT.Square).then_inc(aA.sem, 1)
                wait(act, aP, "ssq", h)
                rsqrt(two(rstd[:, :]), pair(0), A_QK, aA, "lrq", h).then_inc(aA.sem, 1)
                S.activation(sq[:, 1, :], tile_of(8), ACT.Square).then_inc(aA.sem, 1)
                wait(act, aP, "ssk", h)
                wait(act, aD, "qn", h)
                rsqrt(two(rstd[:, :]), pair(2), A_QK, aA, "lrk", h).then_inc(aA.sem, 1)

                def exps(i):
                    wait(act, aD, f"nx{i}", h)
                    for c in range(2):
                        ins = S.activation(e_att[:, i % 2, c, 0:(i + 1) * P], ps[:, 2 * (i % 2) + c, 0:(i + 1) * P], ACT.Exp,
                                           bias=mx[:, i % 2, c:c + 1], scale=A_QK ** -0.5, accum_out=sm[:, i % 2, c:c + 1])
                    ins.then_inc(aA.sem, 1)

                def copy_t(i):
                    wait(act, aP, f"tr{i}", h)
                    S.copy(at_t[:, i % 2, 0:(i + 1) * P], ps[:, 4 + i % 2, 0:(i + 1) * P]).then_inc(aA.sem, 1)

                exps(0)
                exps(1)
                copy_t(0)
                exps(2)
                copy_t(1)
                exps(3)
                copy_t(2)
                copy_t(3)
                wait(act, aP, "pv3", h)
                S.activation(sq[:, 0, 0:T], ps[:, 7, :], ACT.Square).then_inc(aA.sem, 1)
                wait(act, aP, "sso", h)
                rsqrt(rstd[:, 0:T], ps[:, 6, :], P, aA, "lro", h).then_inc(aA.sem, 1)
                wait(act, aD, "mix", h)
                dst = h_hi[:, h, 0:T] if isinstance(h, int) else h_hi[:, ds(h, 1), 0:T].rearrange("p o t -> p (o t)")
                S.copy(dst, o_att[:, :]).then_inc(aA.sem, 1)

            head(0, True)
            with act.Fori(1, A_HEADS) as h:
                head(h, False)

            act.wait_ge(aD.sem, aD.all(A_HEADS))
            S.activation(qk_r[:, :, :], z2[:, 0:16, T:NT], ACT.Square).then_inc(sA.sem, 1)
            wait(act, sP, "ssq")
            rsqrt(qk_t[:, :, :].rearrange("p h b -> p (h b)"), ps[:, 0, 0:P], A_QK, sA, "lr").then_inc(sA.sem, 1)

            def query(r, u, first):
                act.wait_ge(qbP.sem, qbP.at("qb", r))
                if not first:
                    act.wait_ge(kD.sem, kD.at("mul3", r - 2))
                S.copy(qb[:, u, :].rearrange("p (n k) -> p n k", n=2), ps[:, 2 + 2 * u:4 + 2 * u, :]).then_inc(qbA.sem, 1)

            query(0, 0, True)
            query(1, 1, True)
            with act.Fori(1, B // 2) as i:
                for u in range(2):
                    query(2 * i + u, u, False)
            wait(act, tP, "tr")
            S.copy(s_row[:, 0:PAGES * P], ps[:, 1, :]).then_inc(tA.sem, 1)
            wait(act, tD, "nmx")
            S.activation(s_row[:, :], s_row[:, :], ACT.Exp, bias=s_small[:, 0:1], scale=A_QK ** -0.5,
                         accum_out=s_small[:, 1:2]).then_inc(tA.sem, 1)
            wait(act, tP, "atn")
            S.copy(s_at[:, 0:PAGES, :], ps[:, 2, 0:PAGES * 64].rearrange("p (j k) -> p j k", k=64))
            S.copy(s_at[:, PAGES, :], ps[:, 3, 0:64]).then_inc(tA.sem, 1)
            wait(act, tD, "o3")
            S.activation(qk_t[:, 0:A_HEADS, :].rearrange("p h b -> p (h b)"), s_o[:, :], ACT.Square).then_inc(tA.sem, 1)
            wait(act, tP, "ssq")
            rsqrt(qk_t[:, A_HEADS:, :].rearrange("p h b -> p (h b)"), ps[:, 5, 0:64], P, tA, "lr").then_inc(tA.sem, 1)
            wait(act, tD, "mix")
            S.copy(h_hi[:, :, T:NT], s_o2[:, :].rearrange("p (b h) -> p h b", b=B)).then_inc(tA.sem, 1)

            walk(act, "att_out", split, nothing)
            norm(3, 0, lambda c: act.wait_ge(drained, FIRST["att_out"] + c + 1))
            ffn(1)
            walk(act, "down1", split, nothing)

        @block.vector
        def _(dve):
            def split(name, i, s, nk):
                n = FIRST[name] + s
                dve.wait_ge(hi_split, 4 * i + (n + 1))
                V.tensor_tensor(w_lo[:, n % 2, 0:nk * P], raw[:, n % RAW, 0:nk * P],
                                w_hi[:, n % 2, 0:nk * P].bitcast(F32), ALU.subtract).then_inc(lo_split, 1)

            def norm(r, gain):
                wait(dve, nA, "rms", r)
                for c in range(KT):
                    if c >= 2:
                        wait(dve, nD, f"lo{c - 2}", r)
                    V.scalar_tensor_tensor(out=hn[:, c % 2, :], in0=x[:, c, :], scalar=p_(gain, c, 1), in1=rstd[:, :],
                                           op0=ALU.mult, op1=ALU.mult).then_inc(nD.sem, 1)
                    wait(dve, nA, f"hi{c}", r)
                    V.tensor_tensor(h_lo[:, c, :], hn[:, c % 2, :], h_hi[:, c, :].bitcast(F32),
                                    ALU.subtract).then_inc(nD.sem, 1)

            def nothing(i, s):
                pass

            def out_drain(name):
                def drain(i, s):
                    c = 4 * i + s
                    dve.wait_ge(slab_done, 4 * i + (FIRST[name] + s + 1))
                    xc = x[:, c, :]
                    V.tensor_tensor(two(xc), two(xc), pair(2 * (s % 4)), ALU.add).then_inc(drained, 1)
                return drain

            def down_drain(name):
                def drain(i, s):
                    if s % 2:
                        dve.wait_ge(slab_done, 4 * i + (FIRST[name] + s + 1))
                        xc = x[:, 2 * i + s // 2, :] if isinstance(i, int) else \
                            x[:, ds(2 * i + s // 2, 1), :].rearrange("p o t -> p (o t)")
                        V.tensor_tensor(two(xc), two(xc), pair(4 * (s // 2)), ALU.add).then_inc(drained, 2)
                return drain

            def ffn(layer):
                name = f"ffn{layer}"
                cw, cb, cs = (columns(PARAMS)[0][f"{n}{layer}"][0] for n in ("conv_w", "conv_b", "conv_s"))

                def drain(i, s):
                    r = 2 * i + (s // 2 + layer * FT)
                    m = 2 * i + s // 2

                    def col(at, k=0, n=1, step=1):
                        return par[:, ds(step * m + (at + k), n)] if not isinstance(m, int) else \
                            par[:, at + k + step * m:at + k + step * m + n]
                    u = ub[:, s // 2, :]
                    if s % 2 == 0:
                        dve.wait_ge(fA.sem, fA.at("u", r))
                        V.tensor_scalar(cc[:, :], u[:, 2:2 + NT], col(cw, 2 * FT), col(cb), ALU.mult,
                                        ALU.add).then_inc(fD.sem, 1)
                        dve.wait_ge(fD.sem, fD.at("t0", r))
                        V.scalar_tensor_tensor(out=cc[:, 0:T], in0=u[:, 1:1 + T], scalar=col(cw, FT), in1=cc[:, 0:T],
                                               op0=ALU.mult, op1=ALU.add).then_inc(fD.sem, 1)
                        V.scalar_tensor_tensor(out=cc[:, T:NT], in0=col(cs, B, B, 2 * B), scalar=col(cw, FT),
                                               in1=cc[:, T:NT], op0=ALU.mult, op1=ALU.add).then_inc(fD.sem, 1)
                        dve.wait_ge(fD.sem, fD.at("s1", r))
                        V.scalar_tensor_tensor(out=cc[:, 0:T], in0=u[:, 0:T], scalar=col(cw), in1=cc[:, 0:T],
                                               op0=ALU.mult, op1=ALU.add).then_inc(fD.sem, 1)
                        V.scalar_tensor_tensor(out=cc[:, T:NT], in0=col(cs, 0, B, 2 * B), scalar=col(cw),
                                               in1=cc[:, T:NT], op0=ALU.mult, op1=ALU.add).then_inc(fD.sem, 1)
                    else:
                        dve.wait_ge(fA.sem, fA.at("gelu", r))
                        dve.wait_ge(slab_done, 4 * i + (FIRST[name] + s + 1))
                        V.tensor_tensor(two(pr[:, :]), two(ge[:, :]), pair(2 * (s % 4)), ALU.mult).then_inc(fD.sem, 1)
                        dve.wait_ge(fD.sem, fD.at("prod", r))
                        dve.sem_inc(drained, 2)
                        dve.wait_ge(fA.sem, fA.at("hi", r))
                        lo = a_lo[:, ds(m, 1), :] if not isinstance(m, int) else a_lo[:, m:m + 1, :]
                        hi = a_hi[:, ds(m, 1), :] if not isinstance(m, int) else a_hi[:, m:m + 1, :]
                        V.tensor_tensor(lo, pr[:, :].rearrange("p (o t) -> p o t", o=1), hi.bitcast(F32),
                                        ALU.subtract).then_inc(fD.sem, 1)
                wait(dve, pads, "pad", layer)
                walk(dve, name, split, drain)

            dve.wait_ge(par_in, 32)
            norm(0, "g_mix0")
            split("rec_in", 0, 0, KT)
            split("rec_in", 0, 1, KT)
            walk(dve, "rec_in", split, nothing)

            dve.wait_ge(drained, S_REC_IN)
            dve.wait_ge(crec_in, 16)
            bm = columns(PARAMS)[0]["b_mgate"][0]
            V.tensor_scalar(f_pre[:, :], gates[32:36, :], par[32:36, bm:bm + 1], None, ALU.add).then_inc(gtD.sem, 1)
            V.tensor_scalar(i_pre[:, :], gates[0:4, :], par[0:4, bm:bm + 1], None, ALU.add).then_inc(gtD.sem, 1)
            wait(dve, gtD, "i")
            V.scalar_tensor_tensor(out=f_neg[:, :], in0=f_pre[:, :], scalar=-1.0, in1=f_pre[:, :], op0=ALU.mult,
                                   op1=ALU.min).then_inc(gtD.sem, 1)
            wait(dve, gtA, "ln")
            V.scalar_tensor_tensor(out=f_neg[:, :], in0=f_pre[:, :], scalar=0.0, in1=f_log[:, :], op0=ALU.min,
                                   op1=ALU.subtract).then_inc(gtD.sem, 1)
            wait(dve, gtD, "lf")
            V.tensor_tensor_scan(b_row[:, :], c_("reset_m")[0:4, :], f_neg[:, 0:T], 0.0, ALU.mult, ALU.add).then_inc(gtD.sem, 1)
            V.tensor_tensor_scan(m_run[:, :], f_neg[:, 0:T], i_pre[:, 0:T], 0.0, ALU.add, ALU.max).then_inc(gtD.sem, 1)
            V.tensor_tensor(r_s[:, 0:B], f_neg[:, T:NT], p_("m0")[0:4, :], ALU.add).then_inc(gtD.sem, 1)
            wait(dve, gtD, "lfm")
            V.tensor_tensor(m_out[:, 1:1 + B], r_s[:, 0:B], i_pre[:, T:NT], ALU.max).then_inc(gtD.sem, 1)
            V.tensor_tensor(r_intra[:, :], b_row[:, :], m_run[:, :], ALU.subtract).then_inc(gtD.sem, 1)
            V.tensor_tensor(a_row[:, :], i_pre[:, 0:T], b_row[:, :], ALU.subtract).then_inc(gtD.sem, 1)
            V.tensor_scalar(r_negm[:, :], m_run[:, :], -1.0, None, ALU.mult).then_inc(gtD.sem, 1)
            wait(dve, gtD, "nm")
            V.tensor_copy(r_inter[:, 0:P], r_intra[:, 0:P]).then_inc(gtD.sem, 1)
            for c in range(1, NC_M):
                t = slice(c * P, (c + 1) * P)
                V.tensor_scalar(r_inter[:, t], r_intra[:, t], m_run[:, c * P - 1:c * P], None, ALU.add).then_inc(gtD.sem, 1)
            V.tensor_tensor(r_s[:, 0:B], r_s[:, 0:B], m_out[:, 1:1 + B], ALU.subtract).then_inc(gtD.sem, 1)
            V.tensor_scalar(r_s[:, B:2 * B], m_out[:, 1:1 + B], -1.0, None, ALU.mult).then_inc(gtD.sem, 1)
            V.tensor_tensor(r_s[:, 2 * B:3 * B], i_pre[:, T:NT], m_out[:, 1:1 + B], ALU.subtract).then_inc(gtD.sem, 1)
            V.tensor_copy(m_out[:, 0:1], m_run[:, T - 1:T]).then_inc(gtD.sem, 1)

            K_SCALE = float(P) ** -0.5

            def rows(ap, n):
                return ap.unsqueeze(2).to_broadcast([P, ap.shape[1], n])

            def cols_(ap, n):
                return ap.unsqueeze(1).to_broadcast([P, n, ap.shape[1]])

            for h in range(M_HEADS):
                q, k, v, gate = z[:, h, :], z[:, 4 + h, :], z[:, 8 + h, :], z[:, 12 + h, :]
                wait(dve, mP, "bc0", h)
                V.tensor_tensor(e_mat[:, :, :], ps[:, 0, :].rearrange("p (c t) -> p c t", c=NC_M),
                                cols_(c_("causal_T"), NC_M), ALU.add).then_inc(mD.sem, 1)
                wait(dve, mA, "wi", h)
                V.tensor_tensor(q_w[:, :], q[:, 0:T], w_int[:, :], ALU.mult).then_inc(mD.sem, 1)
                wait(dve, mA, "vt", h)
                for c in range(NC_M):
                    end = e_mat[:, c, P - 1:P]
                    V.tensor_scalar(v_end[:, c, 0, :], v_tok[:, c, :], end, K_SCALE, ALU.mult, ALU.mult)
                    ins = V.tensor_scalar(v_end[:, c, 1, :], ONES, end, K_SCALE, ALU.mult, ALU.mult)
                ins.then_inc(mD.sem, 1)
                wait(dve, mP, "scores", h)
                wait(dve, mD, "ve", h)
                flat = e_mat[:, :, :].rearrange("p c t -> p (c t)")
                V.scalar_tensor_tensor(out=flat, in0=ps[:, 3, :], scalar=K_SCALE, in1=flat, op0=ALU.mult,
                                       op1=ALU.mult).then_inc(mD.sem, 1)
                for c in range(NC_M):
                    wait(dve, mP, f"st{c}", h)
                    if c == 0:
                        if h:
                            dve.wait_ge(c_out, 16 * h)
                        V.tensor_copy(c_n[:, :], ps[:, 0, 0:2 * P]).then_inc(mD.sem, 1)
                    else:
                        wait(dve, mD, f"cn{c - 1}", h)
                        V.scalar_tensor_tensor(out=c_n[:, :], in0=c_n[:, :], scalar=w_int[:, (c + 1) * P - 1:(c + 1) * P],
                                               in1=ps[:, c % 2, 0:2 * P], op0=ALU.mult, op1=ALU.add).then_inc(mD.sem, 1)
                wait(dve, mD, "cn3", h)
                V.tensor_copy(n_end[:, h:h + 1], c_n[:, P:P + 1]).then_inc(mD.sem, 1)
                wait(dve, mA, "abs", h)
                V.tensor_tensor(den[:, :], den[:, :], e_negm[:, :], ALU.max).then_inc(mD.sem, 1)
                wait(dve, mD, "den", h)
                V.reciprocal(den[:, :], den[:, :]).then_inc(mD.sem, 1)
                wait(dve, mD, "rden", h)
                V.tensor_tensor(h_head[:, 0:T], ps[:, 6, :], den[:, :], ALU.mult).then_inc(mD.sem, 1)
                V.scalar_tensor_tensor(out=v_ws[:, :], in0=v[:, T:NT], scalar=K_SCALE, in1=w_s[:, 2, :], op0=ALU.mult,
                                       op1=ALU.mult).then_inc(mD.sem, 1)
                V.scalar_tensor_tensor(out=k_ws[:, :], in0=k[:, T:NT], scalar=K_SCALE, in1=w_s[:, 2, :], op0=ALU.mult,
                                       op1=ALU.mult).then_inc(mD.sem, 1)
                V.tensor_tensor(nw[:, :], p_("n0", h * B, B), w_s[:, 0, :], ALU.mult).then_inc(mD.sem, 1)
                wait(dve, mD, "nw", h)
                V.tensor_tensor(n_s[:, h, :], nw[:, :], k_ws[:, :], ALU.add).then_inc(mD.sem, 1)
                wait(dve, mD, "ns", h)
                V.tensor_tensor(nq[:, :], n_s[:, h, :], q[:, T:NT], ALU.mult).then_inc(mD.sem, 1)
                wait(dve, mP, "kb", h)
                row4 = ps[:, 4:6, :].rearrange("p n (b k) -> p (n b) k", k=P)
                row0 = ps[:, 0:2, :].rearrange("p n (b k) -> p (n b) k", k=P)
                V.tensor_tensor(kv[:, :, :], row4, rows(v_ws[:, :], P), ALU.mult).then_inc(mD.sem, 1)
                wait(dve, mG, "cw", h)
                wait(dve, mD, "kv", h)
                V.tensor_tensor(c_s[:, :, :], c_s[:, :, :], kv[:, :, :], ALU.add).then_inc(mD.sem, 1)
                wait(dve, mD, "cs", h)
                wait(dve, mP, "qb", h)
                V.tensor_tensor(kv[:, :, :], c_s[:, :, :], row0, ALU.mult).then_inc(mD.sem, 1)
                wait(dve, mD, "cq", h)
                V.tensor_reduce(hnum_s[:, :], kv[:, :, :], AX.X, ALU.add).then_inc(mD.sem, 1)
                wait(dve, mA, "abs_s", h)
                V.tensor_tensor(den_s[:, :], den_s[:, :], w_s[:, 1, :], ALU.max).then_inc(mD.sem, 1)
                wait(dve, mD, "dn", h)
                V.reciprocal(den_s[:, :], den_s[:, :]).then_inc(mD.sem, 1)
                wait(dve, mD, "rd", h)
                V.tensor_tensor(h_head[:, T:NT], hnum_s[:, :], den_s[:, :], ALU.mult).then_inc(mD.sem, 1)
                wait(dve, mA, "rms", h)
                V.tensor_tensor(hn[:, 0, :], h_head[:, :], rstd[:, :], ALU.mult).then_inc(mD.sem, 1)
                wait(dve, mD, "t", h)
                V.scalar_tensor_tensor(out=hn[:, 1, :], in0=hn[:, 0, :], scalar=p_("g_m"), in1=gate, op0=ALU.mult,
                                       op1=ALU.mult).then_inc(mD.sem, 1)
                wait(dve, mA, "hi", h)
                V.tensor_tensor(h_lo[:, h, :], hn[:, 1, :], h_hi[:, h, :].bitcast(F32), ALU.subtract).then_inc(mD.sem, 1)

            wait(dve, lP, "up")
            dve.wait_ge(c_out, 16 * M_HEADS)
            dve.wait_ge(cs_out, 16 * M_HEADS)
            for p in range(G_PAIRS):
                ins = V.tensor_scalar(two(log_a[:, p, :]), pair(2 * p), p_("b_gate", p, 1), None, ALU.add)
            ins.then_inc(lD.sem, 1)
            wait(dve, lD, "z")
            V.scalar_tensor_tensor(out=ln_t[:, :, :], in0=log_a[:, :, :], scalar=-1.0, in1=log_a[:, :, :], op0=ALU.mult,
                                   op1=ALU.min).then_inc(lD.sem, 1)
            wait(dve, lA, "ln")
            V.scalar_tensor_tensor(out=log_a[:, :, :], in0=log_a[:, :, :], scalar=0.0, in1=ln_t[:, :, :], op0=ALU.min,
                                   op1=ALU.subtract).then_inc(lD.sem, 1)
            wait(dve, lD, "lf")
            V.tensor_scalar(log_a[:, :, :], log_a[:, :, :], 1.0 / 16.0, None, ALU.mult).then_inc(lD.sem, 1)
            V.tensor_scalar(z[:, 16:18, :], z[:, 16:18, :], float(G_KEY) ** -0.5, None, ALU.mult).then_inc(lD.sem, 1)
            V.memset(sub0[:, :, :], 0.0).then_inc(lD.sem, 1)
            wait(dve, lD, "sub0")
            mask = c_("diag_mask")
            for p in range(G_PAIRS):
                q, k = z[:, 16 + p, :], z[:, 18 + p, :]
                q_t = q[:, 0:T].rearrange("p (c t) -> p c t", c=NC_G)
                k_t = k[:, 0:T].rearrange("p (c t) -> p c t", c=NC_G)
                bc_c = bc[:, :].rearrange("p (c t) -> p c t", c=NC_G)
                V.tensor_tensor_scan(bc[:, :], c_("reset_g"), log_a[:, p, 0:T], 0.0, ALU.mult, ALU.add).then_inc(gD.sem, 1)
                wait(dve, gD, "bc", p)
                V.tensor_copy(sub0[:, :, 1:4], bc[:, :].rearrange("p (c j t) -> p c j t", c=NC_G, j=4)[:, :, 0:3, SUB - 1])\
                    .then_inc(gD.sem, 1)
                wait(dve, gD, "sb", p)
                V.tensor_tensor(g_qs[:, :].rearrange("p (j t) -> p j t", t=SUB),
                                bc[:, :].rearrange("p (j t) -> p j t", t=SUB),
                                rows(sub0[:, :, :].rearrange("p c j -> p (c j)"), SUB), ALU.subtract).then_inc(gD.sem, 1)
                V.tensor_tensor(ke[:, :, :, :], sub0[:, :, 1:4].unsqueeze(3).to_broadcast([P, NC_G, 3, 48]),
                                bc_c[:, :, 0:48].unsqueeze(2).to_broadcast([P, NC_G, 3, 48]), ALU.subtract).then_inc(gD.sem, 1)
                wait(dve, gD, "ke", p)
                V.tensor_scalar(ke[:, :, :, :], ke[:, :, :, :], 0.0, None, ALU.min).then_inc(gD.sem, 1)
                V.tensor_tensor(g_kd[:, :].rearrange("p (c t) -> p c t", c=NC_G),
                                bc_c[:, :, LC_G - 1:LC_G].to_broadcast([P, NC_G, LC_G]), bc_c, ALU.subtract).then_inc(gD.sem, 1)
                for n in range(4):
                    def block_rows(ap):
                        return ap[:, n * P:(n + 1) * P].rearrange("p (b t) -> p b t", t=SUB).unsqueeze(2)\
                            .to_broadcast([P, 8, SUB, SUB])

                    def block_cols(ap):
                        return ap[:, n * P:(n + 1) * P].rearrange("p (b t) -> p b t", t=SUB).unsqueeze(3)\
                            .to_broadcast([P, 8, SUB, SUB])
                    if n:
                        wait(dve, gP, f"dg{n - 1}", p)
                    V.tensor_tensor(lx[:, :, :, :], block_rows(bc), block_cols(bc), ALU.subtract).then_inc(gD.sem, 1)
                    wait(dve, gD, f"x{n}", p)
                    flat = lx[:, :, :, :].rearrange("p b s t -> p b (s t)")
                    V.tensor_tensor(flat, flat, cols_(mask, 8), ALU.add).then_inc(gD.sem, 1)
                    wait(dve, gA, f"ex{n}", p)
                    V.tensor_tensor(lx[:, :, :, :], lx[:, :, :, :], block_cols(k), ALU.mult).then_inc(gD.sem, 1)
                    wait(dve, gD, f"xk{n}", p)
                    V.tensor_tensor(lx[:, :, :, :], lx[:, :, :, :], block_rows(q), ALU.mult).then_inc(gD.sem, 1)
                V.tensor_tensor(g_qs[:, :], g_qs[:, :], q[:, 0:T], ALU.mult).then_inc(gD.sem, 1)
                V.tensor_tensor(g_qd[:, :], g_qd[:, :], q[:, 0:T], ALU.mult).then_inc(gD.sem, 1)
                wait(dve, gA, "ke", p)
                V.tensor_tensor(ke[:, :, :, :], ke[:, :, :, :], k_t[:, :, 0:48].unsqueeze(2).to_broadcast([P, NC_G, 3, 48]),
                                ALU.mult).then_inc(gD.sem, 1)
                V.tensor_tensor(g_kd[:, :], g_kd[:, :], k[:, 0:T], ALU.mult).then_inc(gD.sem, 1)
                for c in range(NC_G):
                    wait(dve, gP, f"s{c}", p)
                    if c == 0:
                        if p:
                            dve.wait_ge(gs_out, 16)
                        V.tensor_copy(g_s[:, :], ps[:, 0, 0:P]).then_inc(gD.sem, 1)
                    else:
                        wait(dve, gD, f"c{c - 1}", p)
                        V.scalar_tensor_tensor(out=g_s[:, :], in0=g_s[:, :], scalar=a_end[:, c:c + 1],
                                               in1=ps[:, c % 2, 0:P], op0=ALU.mult, op1=ALU.add).then_inc(gD.sem, 1)
                wait(dve, gP, "vb", p)
                V.tensor_tensor(g_kv[:, :, :], ps[:, 2:4, :].rearrange("p n (b k) -> p (n b) k", k=P), rows(k[:, T:NT], P),
                                ALU.mult).then_inc(gD.sem, 1)
                wait(dve, gG, "sa", p)
                wait(dve, gD, "kv", p)
                V.tensor_tensor(g_ss[:, :, :], g_ss[:, :, :], g_kv[:, :, :], ALU.add).then_inc(gD.sem, 1)
                for hh in range(2):
                    wait(dve, gA, f"o{hh}", p)
                    V.tensor_tensor(g_h[:, hh, LC_G:T], g_h[:, hh, LC_G:T], ps[:, 4 + hh, LC_G:T], ALU.add)
                    V.tensor_copy(g_h[:, hh, 0:LC_G], ps[:, 4 + hh, 0:LC_G]).then_inc(gD.sem, 1)
                for hh in range(2):
                    wait(dve, gP, "os", p)
                    V.tensor_copy(g_h[:, hh, T:NT], ps[:, hh, 256:256 + B]).then_inc(gD.sem, 1)
                for hh in range(2):
                    wait(dve, gA, f"rms{hh}", p)
                    V.tensor_tensor(g_h[:, hh, :], g_h[:, hh, :], rstd[:, :], ALU.mult).then_inc(gD.sem, 1)
                    wait(dve, gD, f"t{hh}", p)
                    V.scalar_tensor_tensor(out=hn[:, hh, :], in0=g_h[:, hh, :], scalar=p_("g_g"), in1=z[:, 24 + 2 * p + hh, :],
                                           op0=ALU.mult, op1=ALU.mult).then_inc(gD.sem, 1)
                    wait(dve, gA, f"hi{hh}", p)
                    c = 4 + 2 * p + hh
                    V.tensor_tensor(h_lo[:, c, :], hn[:, hh, :], h_hi[:, c, :].bitcast(F32), ALU.subtract).then_inc(gD.sem, 1)

            walk(dve, "rec_out", split, out_drain("rec_out"))
            norm(1, "g_ffn0")
            ffn(0)
            walk(dve, "down0", split, down_drain("down0"))
            norm(2, "g_mix1")
            walk(dve, "att_in", split, nothing)

            V.tensor_tensor(lam[0:64, 0:2], p_("lam_q")[0:64, :], p_("lam_k")[0:64, :], ALU.mult).then_inc(lamD.sem, 1)
            wait(dve, lamA, "exp")
            V.tensor_tensor(lam[:, 0:1], lam[:, 2:3], lam[:, 3:4], ALU.subtract).then_inc(lamD.sem, 1)
            wait(dve, lamD, "sub")
            V.tensor_scalar(lam[:, 0:1], lam[:, 0:1], LAM_INIT, None, ALU.add).then_inc(lamD.sem, 1)
            V.memset(coef[:, 0:1], 1.0).then_inc(lamD.sem, 1)
            wait(dve, lamD, "lam")
            V.tensor_copy(coef[:, 1:2], lam[:, 0:1]).then_inc(lamD.sem, 1)
            V.tensor_scalar(g_o2[:, :], p_("g_out"), 1.0 - LAM_INIT, None, ALU.mult).then_inc(lamD.sem, 1)
            dve.wait_ge(catt_in, 16)

            def head(h, first):
                def tile_of(k):
                    return z2[:, k + h, :] if isinstance(h, int) else z2[:, ds(h + k, 1), :].rearrange("p o t -> p (o t)")
                for k, rms, gain, out in ((0, "rq", "g_q", qn), (8, "rk", "g_k", kn)):
                    n = "q" if k == 0 else "k"
                    wait(dve, aA, rms, h)
                    if k and not first:
                        dve.wait_ge(kn_out, 16 * h)
                    V.scalar_tensor_tensor(out=out[:, :], in0=tile_of(k), scalar=p_(gain), in1=rstd[:, :], op0=ALU.mult,
                                           op1=ALU.mult).then_inc(aD.sem, 1)

                def stats(i):
                    wait(dve, aP, f"sc{i}", h)
                    s = ps[:, 2 * (i % 2):2 * (i % 2) + 2, :]
                    V.tensor_tensor(s[:, :, i * P:(i + 1) * P], s[:, :, i * P:(i + 1) * P], cols_(c_("causal"), 2),
                                    ALU.add).then_inc(aD.sem, 1)
                    wait(dve, aD, f"m{i}", h)
                    V.tensor_reduce(mx[:, i % 2, :], s[:, :, 0:(i + 1) * P], AX.X, ALU.max).then_inc(aD.sem, 1)
                    wait(dve, aD, f"x{i}", h)
                    V.tensor_scalar(mx[:, i % 2, :], mx[:, i % 2, :], -(A_QK ** -0.5), None, ALU.mult).then_inc(aD.sem, 1)

                def combine(i):
                    b = i % 2
                    w = slice(0, (i + 1) * P)
                    wait(dve, aA, f"ex{i}", h)
                    V.reciprocal(rs[:, b, :], sm[:, b, :]).then_inc(aD.sem, 1)
                    wait(dve, aD, f"r{i}", h)
                    V.tensor_tensor(rs[:, b, :], rs[:, b, :], coef[:, :], ALU.mult).then_inc(aD.sem, 1)
                    wait(dve, aD, f"rc{i}", h)
                    V.tensor_scalar(e_att[:, b, 1, w], e_att[:, b, 1, w], rs[:, b, 1:2], None, ALU.mult).then_inc(aD.sem, 1)
                    wait(dve, aD, f"e{i}", h)
                    if i >= 2:
                        wait(dve, aP, f"tr{i - 2}", h)
                    V.scalar_tensor_tensor(out=a_att[:, b, w], in0=e_att[:, b, 0, w], scalar=rs[:, b, 0:1],
                                           in1=e_att[:, b, 1, w], op0=ALU.mult, op1=ALU.subtract).then_inc(aD.sem, 1)

                for i in range(4):
                    stats(i)
                    combine(i)
                wait(dve, aA, "ro", h)
                V.scalar_tensor_tensor(out=o_att[:, :], in0=ps[:, 7, :], scalar=g_o2[:, :], in1=rstd[:, 0:T], op0=ALU.mult,
                                       op1=ALU.mult).then_inc(aD.sem, 1)
                wait(dve, aA, "hi", h)
                lo, hi = ((t[:, h, 0:T] if isinstance(h, int) else t[:, ds(h, 1), 0:T].rearrange("p o t -> p (o t)"))
                          for t in (h_lo, h_hi))
                V.tensor_tensor(lo, o_att[:, :], hi.bitcast(F32), ALU.subtract).then_inc(aD.sem, 1)

            head(0, True)
            with dve.Fori(1, A_HEADS) as h:
                head(h, False)

            dve.wait_ge(kn_out, 16 * A_HEADS)
            wait(dve, sA, "rms")
            V.tensor_tensor(qks[:, :, :], z2[:, 0:16, T:NT], qk_t[:, :, :], ALU.mult).then_inc(sD.sem, 1)
            wait(dve, sD, "tq")
            V.tensor_scalar(qks[:, 0:8, :], qks[:, 0:8, :], p_("g_q"), None, ALU.mult).then_inc(sD.sem, 1)
            V.tensor_scalar(qks[:, 8:16, :], qks[:, 8:16, :], p_("g_k"), None, ALU.mult).then_inc(sD.sem, 1)
            V.memset(s_new[:, :], 0.0).then_inc(sD.sem, 1)
            wait(dve, sD, "nk")
            for c in range(2):
                r = slice(64 * c, 64 * c + 64)
                V.tensor_tensor(s_new[r, :].rearrange("p (b h c) -> p b h c", b=B, c=2)[:, :, :, c],
                                qks[r, 0:8, :].rearrange("p h b -> p b h"), qks[r, 8:16, :].rearrange("p h b -> p b h"),
                                ALU.mult).then_inc(sD.sem, 1)
            with dve.Fori(0, B // 2) as i:
                for u in range(2):
                    r = 2 * i + u
                    dve.wait_ge(qbA.sem, qbA.at("qb", r))
                    for j in range(PAGES):
                        dve.wait_ge(page_in[j], 16 * r + 16)
                        V.tensor_tensor(s_prod[:, :], pages[:, j, :], qb[:, u, :], ALU.mult).then_inc(kD.sem, 1)
                        dve.wait_ge(kD.sem, kD.at(f"mul{j}", r))
                        V.tensor_reduce(s_sc[:, j, ds(16 * r, 16)], s_prod[:, :].rearrange("p (h d) -> p h d", d=A_QK),
                                        AX.X, ALU.add).then_inc(kD.sem, 1)
                        dve.wait_ge(kD.sem, kD.at(f"red{j}", r))
            wait(dve, tP, "new")
            V.tensor_copy(s_row[:, PAGES * P:PAGES * P + 1], ps[:, 6, 0:1]).then_inc(tD.sem, 1)
            wait(dve, tA, "row")
            wait(dve, tD, "newc")
            V.tensor_reduce(s_small[:, 0:1], s_row[:, :], AX.X, ALU.max).then_inc(tD.sem, 1)
            wait(dve, tD, "mx")
            V.tensor_scalar(s_small[:, 0:1], s_small[:, 0:1], -(A_QK ** -0.5), None, ALU.mult).then_inc(tD.sem, 1)
            wait(dve, tA, "ex")
            V.reciprocal(s_small[:, 2:3], s_small[:, 1:2]).then_inc(tD.sem, 1)
            wait(dve, tD, "r")
            V.tensor_tensor(s_small[:, 3:4], s_small[:, 2:3], lam[:, 0:1], ALU.mult).then_inc(tD.sem, 1)
            wait(dve, tD, "rc")
            V.tensor_scalar(s_pick[:, :], c_("pick_c1"), s_small[:, 3:4], None, ALU.mult).then_inc(tD.sem, 1)
            wait(dve, tD, "pick0")
            V.scalar_tensor_tensor(out=s_pick[:, :], in0=c_("pick_c0"), scalar=s_small[:, 2:3], in1=s_pick[:, :],
                                   op0=ALU.mult, op1=ALU.subtract).then_inc(tD.sem, 1)
            V.tensor_scalar(s_new[:, :], ONES, s_row[:, PAGES * P:PAGES * P + 1], None, ALU.mult).then_inc(tD.sem, 1)
            wait(dve, vP, "v3", B - 1)
            V.tensor_reduce(s_o[:, :], ps[:, 4, 0:PAGES * 64].rearrange("p (j k) -> p k j", j=PAGES), AX.X,
                            ALU.add).then_inc(tD.sem, 1)
            V.tensor_tensor(s_o2[:, :].rearrange("p (b h) -> p b h", b=B), s_at[:, PAGES, :].rearrange("p (b h) -> p b h", b=B),
                            z2[:, 16:24, T:NT].rearrange("p h b -> p b h"), ALU.mult).then_inc(tD.sem, 1)
            wait(dve, tD, "o2")
            V.tensor_tensor(s_o[:, :], s_o[:, :], s_o2[:, :], ALU.add).then_inc(tD.sem, 1)
            wait(dve, tA, "rms")
            rr = qk_t[:, A_HEADS:, :].rearrange("p h b -> p (h b)")
            V.tensor_tensor(s_o[:, :], s_o[:, :], rr, ALU.mult).then_inc(tD.sem, 1)
            wait(dve, tD, "t")
            V.tensor_scalar(s_o2[:, :], s_o[:, :], g_o2[:, :], None, ALU.mult).then_inc(tD.sem, 1)
            wait(dve, tA, "hi")
            V.tensor_tensor(h_lo[:, :, T:NT], s_o2[:, :].rearrange("p (b h) -> p h b", b=B), h_hi[:, :, T:NT].bitcast(F32),
                            ALU.subtract).then_inc(tD.sem, 1)

            walk(dve, "att_out", split, out_drain("att_out"))
            norm(3, "g_ffn1")
            ffn(1)
            walk(dve, "down1", split, down_drain("down1"))

        @block.gpsimd
        def _(pool):
            def times_rows(out, a_, row, n):
                return G.tensor_tensor(out, a_, row.unsqueeze(2).to_broadcast([P, B, n]), ALU.mult)

            def spread(out, row, n=B):
                return G.tensor_tensor(out, IDENT.unsqueeze(1).to_broadcast([P, n, P]),
                                       row.unsqueeze(2).to_broadcast([P, n, P]), ALU.mult)

            G.memset(one[:, :], 1.0).then_inc(small.sem, 1)
            G.memset(eps[:, :], EPS).then_inc(small.sem, 1)
            pool.wait_ge(par_in, 32)
            for layer in range(2):
                pool.dma_start(a["o_conv_s1"][layer], p_(f"conv_s{layer}").rearrange("p (m j b) -> p m j b", j=2, b=B)[:, :, 1, :])\
                    .then_inc(outs, 16)
            wait(pool, gtD, "mo0")
            pool.dma_start(a["o_m"], m_out[:, :]).then_inc(outs, 16)
            wait(pool, gtA, "acol")
            for h in range(M_HEADS):
                if h:
                    pool.wait_ge(cs_out, 16 * h)
                    wait(pool, mD, "cq", h - 1)
                pool.dma_start(c_s[:, :, :], a["state_c"][:, h]).then_inc(c_s_in, 16)
                wait(pool, mP, "bc0", h)
                spread(diag_k[:, :, :], z[:, 4 + h, T:NT]).then_inc(mG.sem, 1)
                spread(diag_q[:, :, :], z[:, h, T:NT]).then_inc(mG.sem, 1)
                wait(pool, mA, "ws", h)
                pool.wait_ge(c_s_in, 16 * (h + 1))
                times_rows(c_s[:, :, :], c_s[:, :, :], w_s[:, 0, :], P).then_inc(mG.sem, 1)
                wait(pool, mD, "nend", h)
                pool.dma_start(a["o_c"][:, h], c_n[:, 0:P]).then_inc(c_out, 16)
                wait(pool, mD, "cs", h)
                pool.dma_start(a["o_cs"][:, h], c_s[:, :, :]).then_inc(cs_out, 16)
            pool.dma_start(a["o_n"], n_end[:, :]).then_inc(outs, 16)
            pool.dma_start(a["o_ns"], n_s[:, :, :]).then_inc(outs, 16)

            pool.wait_ge(mD.sem, mD.all(M_HEADS))
            for p in range(G_PAIRS):
                if p:
                    pool.wait_ge(gD.sem, gD.all(p))
                    G.memset(g_att[:, :, :, :], 0.0).then_inc(gG.sem, 1)
                else:
                    pool.wait_ge(c_out, 16 * M_HEADS)
                    pool.wait_ge(cs_out, 16 * M_HEADS)
                    G.memset(g_att[:, :, :, :], 0.0).then_inc(gG.sem, 1)
                wait(pool, gP, "dg3", p)
                pool.wait_ge(dg_out, 32 * (p + 1))
                if p:
                    pool.wait_ge(gss_out, 16)
                pool.dma_start(g_ss[:, :, :], a["state_s"][:, p]).then_inc(g_s_in, 16)
                for hh in range(2):
                    ins = spread(g_dv[:, hh, :, :], z[:, 20 + 2 * p + hh, T:NT])
                ins.then_inc(gG.sem, 1)
                wait(pool, gA, "as", p)
                pool.wait_ge(g_s_in, 16 * (p + 1))
                times_rows(g_ss[:, :, :], g_ss[:, :, :], a_s[:, :], P).then_inc(gG.sem, 1)
                wait(pool, gD, "c7", p)
                pool.dma_start(a["o_s"][:, p], g_s[:, :]).then_inc(gs_out, 16)
                wait(pool, gD, "ss", p)
                pool.dma_start(a["o_ss"][:, p], g_ss[:, :, :]).then_inc(gss_out, 16)

            pool.wait_ge(gs_out, 16 * G_PAIRS)
            pool.wait_ge(gss_out, 16 * G_PAIRS)
            pool.wait_ge(outs, 16 * 5)
            pool.wait_ge(slab_done, FIRST["ffn0"])
            G.memset(ub[:, :, 0:2], 0.0).then_inc(pads.sem, 1)
            pool.wait_ge(fD.sem, fD.all(FT))
            pool.dma_start(a["o_conv"][0], conv_end[:, :, :]).then_inc(conv_out, 16)

            pool.wait_ge(slab_done, FIRST["att_in"])
            pool.dma_start(catt[:, :], a["catt"]).then_inc(catt_in, 16)
            pool.wait_ge(drained, FIRST["att_out"])
            pool.dma_start(a["o_v"], z2[:, 16:24, :]).then_inc(outs, 16)
            for h in range(A_HEADS):
                wait(pool, aD, "kn", h)
                pool.dma_start(a["o_k"][:, h, :], kn[:, :]).then_inc(kn_out, 16)

            def query(r, u, first):
                if not first:
                    pool.wait_ge(qbA.sem, qbA.at("qb", r - 2))
                row = qks[:, 0:8, r] if isinstance(r, int) else \
                    qks[:, 0:8, ds(r, 1)].rearrange("p h o -> p (h o)")
                spread(qd[:, u, :, :], row, A_HEADS).then_inc(qbG.sem, 1)

            wait(pool, sD, "nq")
            query(0, 0, True)
            query(1, 1, True)
            with pool.Fori(1, B // 2) as i:
                for u in range(2):
                    query(2 * i + u, u, False)

            pool.wait_ge(slab_done, FIRST["ffn1"])
            pool.wait_ge(outs, 16 * 6)
            G.memset(ub[:, :, 0:2], 0.0).then_inc(pads.sem, 1)
            pool.wait_ge(fD.sem, fD.all(2 * FT))
            pool.dma_start(a["o_conv"][1], conv_end[:, :, :]).then_inc(conv_out, 16)
            for c in range(KT):
                pool.wait_ge(drained, FIRST["down1"] + 2 * (c + 1))
                pool.dma_start(a["o_y"][:, c, :], x[:, c, :]).then_inc(outs, 16)
            pool.wait_ge(outs, 16 * (6 + KT))
            pool.wait_ge(c_out, 16 * M_HEADS)
            pool.wait_ge(cs_out, 16 * M_HEADS)
            pool.wait_ge(gs_out, 16 * G_PAIRS)
            pool.wait_ge(gss_out, 16 * G_PAIRS)
            pool.wait_ge(conv_out, 32)
            pool.wait_ge(kn_out, 16 * A_HEADS)
            pool.wait_ge(dg_out, 32 * G_PAIRS)


def slabs(w):
    k, n = w.shape
    return w.reshape(k // P, P, n // P, P).transpose(2, 1, 0, 3).reshape(n // P, P, k)


def down_slabs(w):
    s = slabs(w)
    return s.reshape(s.shape[0], P, 2, KD * P).transpose(0, 2, 1, 3).reshape(2 * s.shape[0], P, KD * P)


def feature_tiles(v):
    return v.reshape(-1, P).T


def rec_columns(w):
    last = np.zeros((w.shape[0], P), w.dtype)
    last[:, 0:4], last[:, 32:36], last[:, 64:80] = w[:, 2048:2052], w[:, 2052:2056], w[:, 3592:3608]
    return np.concatenate([w[:, 0:2048], w[:, 2056:3592], last], axis=1)


def constants():
    f = np.float32
    i = np.arange(P)
    before = (i[:, None] <= i[None, :])
    lo = i < 64
    causal_t = np.where(before, 0, NEG).astype(f)
    sel = np.zeros((P, M_HEADS, P), f)
    for h in range(M_HEADS):
        sel[h, h] = 1
    half_sum = np.zeros((P, 32), f)
    half_sum[lo, 0] = half_sum[~lo, 1] = 1
    s = np.arange(SUB)
    diag = np.where(s[:, None] <= s[None, :], 0, NEG).astype(f).reshape(1, -1)
    t = np.arange(T)
    cst = {"ident": np.eye(P), "ones": np.ones((P, P))}
    rec = {"causal_T": causal_t, "ones_lo": np.tile(lo, (P, 1)), "ones_hi": np.tile(~lo, (P, 1)),
           "sel_head": sel.reshape(P, -1), "half_sum": half_sum, "diag_mask": np.tile(diag, (P, 1)),
           "reset_m": np.tile(t % LC_M != 0, (P, 1)), "reset_g": np.tile(t % LC_G != 0, (P, 1))}
    pick = np.zeros((2, P, 64), f)
    for r in range(P):
        pick[r % 2, r, r // 2] = 1
    att = {"causal": causal_t.T, "ones_half": lo[:, None] == lo[None, :], "pick_c0": pick[0], "pick_c1": pick[1]}
    return cst, rec, att


def packed(table, parts):
    return np.ascontiguousarray(np.concatenate([np.asarray(parts[n], np.float32) for n, _ in table], axis=1))


def kernel(**inputs):
    import concourse.bacc as bacc
    from concourse.bass_utils import run_bass_kernel_spmd

    v = {k: np.asarray(x) for k, x in inputs.items()}
    f = np.float32

    def column(values, rows=P, at=0):
        out = np.zeros((P, 1), f)
        out[at:at + len(values), 0] = values
        return out

    x_all = np.concatenate([v["x_prompt"][0], v["x_sample"][:, 0]], axis=0)
    tokens = x_all.T.reshape(KT, P, NT).transpose(1, 0, 2)
    cst, rec, att = constants()
    gate_up = np.zeros((P, G_PAIRS * P), f)
    gate_up[64:80] = v["rec_w_gate_up"][0]
    rec["w_gate_up"] = gate_up
    b_mgate = np.zeros((P, 1), f)
    b_mgate[0:4, 0], b_mgate[32:36, 0] = v["rec_b_mgate"][0, :4], v["rec_b_mgate"][0, 4:]
    pads_ = lambda u: np.concatenate([u, np.zeros((P - u.shape[0], u.shape[1]), f)], axis=0)
    twice = lambda u: np.concatenate([u, u])[:, None]
    par = {"g_mix0": feature_tiles(v["norm_mix_g"][0]), "g_mix1": feature_tiles(v["norm_mix_g"][1]),
           "g_ffn0": feature_tiles(v["norm_ffn_g"][0]), "g_ffn1": feature_tiles(v["norm_ffn_g"][1]),
           "b_gate": feature_tiles(v["rec_b_gate"][0]), "g_m": v["rec_m_norm_g"][0][:, None],
           "g_g": v["rec_g_norm_g"][0][:, None], "g_q": twice(v["att_q_norm_g"][0]), "g_k": twice(v["att_k_norm_g"][0]),
           "g_out": v["att_out_norm_g"][0][:, None], "b_mgate": b_mgate,
           "lam_q": pads_(np.stack([v["att_lambda_q1"][0], v["att_lambda_q2"][0]], 1)),
           "lam_k": pads_(np.stack([v["att_lambda_k1"][0], v["att_lambda_k2"][0]], 1)),
           "m0": pads_(v["state_mlstm_m"][0].T), "n0": v["state_mlstm_n"][0].transpose(2, 1, 0).reshape(P, M_HEADS * B)}
    for layer in range(2):
        par[f"conv_w{layer}"] = v["ffn_conv_w"][layer].reshape(3, FT, P).transpose(2, 0, 1).reshape(P, 3 * FT)
        par[f"conv_b{layer}"] = feature_tiles(v["ffn_conv_b"][layer])
        par[f"conv_s{layer}"] = v["state_ffn_conv"][layer].reshape(B, 2, FT, P).transpose(3, 2, 1, 0).reshape(P, -1)

    def ffn_slabs(layer):
        up, gate = slabs(v["ffn_w_up"][layer]), slabs(v["ffn_w_gate"][layer])
        return np.stack([up, gate], 1).reshape(S_FFN, P, D_MODEL)

    arrays = {
        "x": tokens, "cst": packed(CONSTS, cst), "crec": packed(CONSTS_REC, rec), "catt": packed(CONSTS_ATT, att),
        "par": packed(PARAMS, par),
        "w_rec_in": slabs(rec_columns(v["rec_w_in"][0])), "w_rec_out": slabs(v["rec_w_out"][0]),
        "w_att_in": slabs(v["att_w_in"][0]), "w_att_out": slabs(v["att_w_out"][0]),
        "w_ffn0": ffn_slabs(0), "w_ffn1": ffn_slabs(1),
        "w_down0": down_slabs(v["ffn_w_down"][0]), "w_down1": down_slabs(v["ffn_w_down"][1]),
        "state_c": v["state_mlstm_C"][0].transpose(2, 1, 0, 3),
        "state_s": v["state_gla_S"][0].reshape(B, G_PAIRS, P, P).transpose(2, 1, 0, 3),
        "cache_k": v["cache_k"][0].reshape(POOL, PAGE, D_MODEL), "cache_v": v["cache_v"][0].reshape(POOL, PAGE, D_MODEL),
        "page_table": v["page_table"].reshape(1, B * PAGES),
    }
    outs = {"o_y": (P, KT, NT), "o_m": (4, 1 + B), "o_c": (P, M_HEADS, P), "o_cs": (P, M_HEADS, B, P),
            "o_n": (P, M_HEADS), "o_ns": (P, M_HEADS, B), "o_s": (P, G_PAIRS, P), "o_ss": (P, G_PAIRS, B, P),
            "o_k": (P, A_HEADS, NT), "o_v": (P, A_HEADS, NT), "o_conv": (2, P, FT, 2 + B), "o_conv_s1": (2, P, FT, B)}
    nc = bacc.Bacc("TRN2", target_bir_lowering=False, num_devices=1)
    aps = {}
    arrays = {n: np.ascontiguousarray(t) for n, t in arrays.items()}
    for n, t in arrays.items():
        aps[n] = nc.dram_tensor(f"in_{n}", t.shape, mybir.dt.from_np(t.dtype), kind="ExternalInput").ap()
    for n, shape in outs.items():
        aps[n] = nc.dram_tensor(f"out_{n}", shape, mybir.dt.float32, kind="ExternalOutput").ap()
    aps["blocks"] = nc.dram_tensor("blocks", (G_PAIRS, 2, 16, 512), mybir.dt.float32, kind="Internal").ap()
    build(nc, aps)
    r = run_bass_kernel_spmd(nc, [{f"in_{n}": t for n, t in arrays.items()}], core_ids=[0]).results[0]
    o = {n: np.asarray(r[f"out_{n}"]) for n in outs}

    y = o["o_y"].transpose(2, 1, 0).reshape(NT, D_MODEL)
    k = o["o_k"].transpose(2, 1, 0)
    vv = o["o_v"].transpose(2, 1, 0)
    conv = o["o_conv"].transpose(0, 3, 2, 1).reshape(2, 2 + B, FFN)
    s1 = o["o_conv_s1"].transpose(0, 3, 2, 1).reshape(2, B, FFN)
    c = np.ascontiguousarray
    return (c(y[None, :T]), c(y[T:, None]),
            c(o["o_c"].transpose(1, 2, 0)[None, None]), c(o["o_cs"].transpose(2, 1, 0, 3)[None]),
            c(o["o_n"].T[None, None]), c(o["o_ns"].transpose(2, 1, 0)[None]),
            c(o["o_m"][:, 0][None, None]), c(o["o_m"][:, 1:].T[None]),
            c(o["o_s"].transpose(1, 0, 2).reshape(1, 1, 4, G_KEY, P)),
            c(o["o_ss"].transpose(2, 1, 0, 3).reshape(1, B, 4, G_KEY, P)),
            c(k[None, None, :T]), c(k[T:][None, :, None]), c(vv[None, None, :T]), c(vv[T:][None, :, None]),
            c(conv[:, None, 0:2]), c(np.stack([s1, conv[:, 2:]], axis=2)))
```

```python
import math
from contextlib import ExitStack

import concourse.bass as bass
import numpy as np
from concourse import mybir

P = 128
D_MODEL, T, B = 1024, 512, 8
NT = T + B
HALF = NT // 2
KT = D_MODEL // P
M_HEADS, G_PAIRS, A_HEADS, A_QK = 4, 2, 8, 64
G_KEY = 64
FFN = 2816
FT = FFN // P
KD = FT // 2
PAGE, PAGES, POOL = 128, 4, 40
EPS = 1e-6
LC_M = 128
NC_M = T // LC_M
LC_G = 64
NC_G = T // LC_G
SUB = 16
LAM_INIT = 0.8 - 0.6 * math.exp(-0.3)
NEG = -1e30

S_REC_IN = 29
S_OUT = 8
S_FFN = 2 * FT
S_DOWN = 16
RAW = 4
PHASES = [("rec_in", S_REC_IN, KT), ("rec_out", S_OUT, KT), ("ffn0", S_FFN, KT), ("down0", S_DOWN, KD),
          ("att_q", A_HEADS, KT), ("att_kv", 2 * A_HEADS, KT), ("att_out", S_OUT, KT), ("ffn1", S_FFN, KT), ("down1", S_DOWN, KD)]
FIRST_SLABS = [28, 0, 4, 8, 12]
HEAD_SLABS = [[13, 1, 5, 9, 24, 25], [14, 2, 6, 10, 26, 27], [15, 3, 7, 11, 16, 17], [18, 19, 20, 21, 22, 23]]
REC_TILES = FIRST_SLABS + sum(HEAD_SLABS, [])
PER_HEAD = len(HEAD_SLABS[0])
FIRST = {}
_n = 0
for _name, _s, _k in PHASES:
    FIRST[_name] = _n
    _n += _s
N_SLABS = _n

PARAMS = [("g_mix0", KT), ("g_ffn0", KT), ("g_mix1", KT), ("g_ffn1", KT),
          ("conv_w0", 3 * FT), ("conv_b0", FT), ("conv_w1", 3 * FT), ("conv_b1", FT),
          ("b_gate", G_PAIRS), ("g_m", 1), ("g_g", 1), ("g_q", 1), ("g_k", 1), ("g_out", 1),
          ("b_mgate", 1), ("lam_q", 2), ("lam_k", 2), ("m0", B), ("n0", M_HEADS * B),
          ("conv_s0", FT * 2 * B), ("conv_s1", FT * 2 * B)]
CONSTS = [("ident", P), ("ones", P)]
CONSTS_REC = [("causal_T", P), ("ones_lo", P), ("ones_hi", P), ("sel_head", M_HEADS * P), ("half_sum", 32),
              ("diag_mask", SUB * SUB), ("reset_m", T), ("reset_g", T), ("w_gate_up", G_PAIRS * P)]
CONSTS_ATT = [("causal", P), ("ones_half", P)]


def columns(table):
    at, out = 0, {}
    for name, n in table:
        out[name] = (at, at + n)
        at += n
    return out, at


class Steps:

    def __init__(self, sem, names):
        self.sem, self.names = sem, names.split()
        self.n = len(self.names)

    def at(self, name, r=0):
        return r * self.n + self.names.index(name) + 1

    def all(self, r):
        return r * self.n


def build(nc, a):
    F32, F32R, I32 = mybir.dt.float32, mybir.dt.float32r, mybir.dt.int32
    ALU, ACT, AX = mybir.AluOpType, mybir.ActivationFunctionType, mybir.AxisListType
    V, S, G, TE = nc.vector, nc.scalar, nc.gpsimd, nc.tensor
    ds = bass.ds
    ctx = ExitStack()
    with ctx:
        END = 229344

        def place(name, shape, dt=F32, at=None):
            size = 4 * int(np.prod(shape[1:]))
            size += -size % 32
            assert at[0] + size <= END, (name, at[0] + size)
            t = nc.alloc_sbuf_tensor_at(name, shape, dt, offset=at[0])
            at[0] += size
            return t

        def sem(name):
            return ctx.enter_context(nc.semaphore(name))

        hold = [16512]
        x = place("x", [P, KT, NT], at=hold)
        cst = place("cst", [P, columns(CONSTS)[1]], at=hold)
        par = place("par", [P, columns(PARAMS)[1]], at=hold)
        eps = place("eps", [P, 1], at=hold)
        one = place("one", [P, 1], at=hold)
        conv_end = place("conv_end", [P, FT, 2 + B], at=hold)
        raw = place("raw", [P, RAW, KD * P], at=hold)
        w_hi = place("w_hi", [P, 2, KD * P], F32R, at=hold)
        w_lo = place("w_lo", [P, 2, KD * P], F32R, at=hold)
        h_hi_at = hold[0]
        h_hi = place("h_hi", [P, KT, NT], F32R, at=hold)
        h_lo_at = hold[0]
        h_lo = place("h_lo", [P, KT, NT], F32R, at=hold)
        region = hold[0]
        norm_at = END - 5 * 4 * NT
        at = [norm_at]
        sq = place("sq", [P, 2, NT], at=at)
        rstd = place("rstd", [P, NT], at=at)
        hn = place("hn", [P, 2, NT], at=at)

        at = [region]
        z = place("z", [P, 28, NT], at=at)
        gates = place("gates", [P, NT], at=at)
        crec = place("crec", [P, columns(CONSTS_REC)[1]], at=at)
        r_intra = place("r_intra", [4, T], at=at)
        r_inter = place("r_inter", [4, T], at=at)
        r_negm = place("r_negm", [4, T], at=at)
        r_s = place("r_s", [4, 3 * B], at=at)
        m_out = place("m_out", [4, 1 + B], at=at)
        a_col = place("a_col", [P, NC_M, 4], at=at)
        n_end = place("n_end", [P, M_HEADS], at=at)
        n_s = place("n_s", [P, M_HEADS, B], at=at)
        work = at[0]
        at = [work]
        i_pre = place("i_pre", [4, NT], at=at)
        f_pre = place("f_pre", [4, NT], at=at)
        f_neg = place("f_neg", [4, NT], at=at)
        f_log = place("f_log", [4, NT], at=at)
        m_run = place("m_run", [4, T], at=at)
        b_row = place("b_row", [4, T], at=at)
        a_row = place("a_row", [4, T], at=at)
        at = [work]
        e_mat = place("e_mat", [P, NC_M, LC_M], at=at)
        w_int = place("w_int", [P, T], at=at)
        q_w = place("q_w", [P, T], at=at)
        k_tok = place("k_tok", [P, NC_M, P], at=at)
        v_tok = place("v_tok", [P, NC_M, P], at=at)
        v_end = place("v_end", [P, NC_M, 2, P], at=at)
        c_s = place("c_s", [P, B, P], at=at)
        kv = place("kv", [P, B, P], at=at)
        c_n = place("c_n", [P, 2 * P], at=at)
        w_s = place("w_s", [P, 3, B], at=at)
        nw = place("nw", [P, B], at=at)
        nq = place("nq", [P, B], at=at)
        v_ws = place("v_ws", [P, B], at=at)
        k_ws = place("k_ws", [P, B], at=at)
        den_s = place("den_s", [P, B], at=at)
        hnum_s = place("hnum_s", [P, B], at=at)
        assert at[0] <= norm_at, (at[0], norm_at)
        diag_q, diag_k = v_end[:, :, :, :].rearrange("p c a v -> p (c a) v"), kv
        h_head, den, e_negm = sq[:, 1, :], rstd[:, 0:T], hn[:, 0, 0:T]
        at = [region]
        lx = place("lx", [P, 8, SUB, SUB], at=at)
        dg = place("dg", [P, 4, 512], at=at)
        ke = place("ke", [P, NC_G, 3, 48], at=at)
        g_vt = place("g_vt", [64, 2, NC_G, P], at=at)
        g_s = place("g_s", [P, P], at=at)
        assert at[0] <= region + 16 * NT * 4, at[0] - region - 16 * NT * 4
        at = [work]
        log_a = place("log_a", [P, G_PAIRS, NT], at=at)
        bc = place("bc", [P, T], at=at)
        sub0 = place("sub0", [P, NC_G, 4], at=at)
        a_end = place("a_end", [P, NC_G], at=at)
        a_s = place("a_s", [P, B], at=at)
        g_qs = place("g_qs", [P, T], at=at)
        g_qd = place("g_qd", [P, T], at=at)
        g_kd = place("g_kd", [P, T], at=at)
        g_att = place("g_att", [64, 2, NC_G, LC_G], at=at)
        g_kdt = place("g_kdt", [64, NC_G, P], at=at)
        g_h = place("g_h", [P, 2, NT], at=at)
        assert at[0] <= norm_at, (at[0], norm_at)
        ln_t = g_h
        at = [region]
        g_dv = place("g_dv", [P, 2, B, P], at=at)
        g_ss = place("g_ss", [P, B, P], at=at)
        g_kv = place("g_kv", [P, B, P], at=at)

        at = [region]
        a_hi = place("a_hi", [P, FT, NT], F32R, at=at)
        a_lo = place("a_lo", [P, FT, NT], F32R, at=at)
        ub = place("ub", [P, 2, 2 + NT], at=at)
        cc = place("cc", [P, NT], at=at)
        ge = place("ge", [P, NT], at=at)
        pr = place("pr", [P, NT], at=[norm_at])
        assert at[0] <= norm_at, (at[0], norm_at)

        at = [region]
        k_pages = place("k_pages", [P, PAGES, D_MODEL], at=at)
        v_pages = place("v_pages", [P, PAGES, D_MODEL], at=at)
        zq = place("zq", [P, A_HEADS, NT], at=at)
        catt = place("catt", [P, columns(CONSTS_ATT)[1]], at=at)
        ptab = place("ptab", [1, B * PAGES], I32, at=at)
        lam = place("lam", [P, 4], at=at)
        coef = place("coef", [P, 2], at=at)
        g_o2 = place("g_o2", [P, 1], at=at)
        qs = place("qs", [P, A_HEADS, B], at=at)
        ks = place("ks", [P, A_HEADS, B], at=at)
        vs = place("vs", [P, A_HEADS, B], at=at)
        qs_r = place("qs_r", [P, A_HEADS, B], at=at)
        qs_t = place("qs_t", [P, A_HEADS, B], at=at)
        qn = place("qn", [P, 2, NT], at=at)
        kn = place("kn", [P, 2, NT], at=at)
        v_t2 = place("v_t2", [P, 2, 4, P], at=at)
        e_att = place("e_att", [P, 2, 2, T], at=at)
        kraw = place("kraw", [P, NT], at=at)
        a_att = place("a_att", [P, 2, T], at=at)
        mx = place("mx", [P, 2, 2], at=at)
        sm = place("sm", [P, 2, 2], at=at)
        rs = place("rs", [P, 2, 2], at=at)
        s_sc = place("s_sc", [P, PAGES, 16], at=at)
        s_m = place("s_m", [P, 1], at=at)
        s_dm = place("s_dm", [P, 16], at=at)
        m_all = place("m_all", [P, B, 16], at=at)
        l_all = place("l_all", [P, B, 16], at=at)
        o_all = place("o_all", [P, B, 16], at=at)
        vn = place("vn", [P, NT], at=at)
        at_t = place("at_t", [P, 2, T], at=at)
        sq3 = place("sq3", [P, 3, NT], at=at)
        rs3 = place("rs3", [P, 3, NT], at=at)
        s_prod = place("s_prod", [P, D_MODEL], at=at)
        qb = place("qb", [P, D_MODEL], at=at)
        qd = place("qd", [P, A_HEADS, P], at=at)
        at = [region]
        s_new = place("s_new", [P, P], at=at)
        s_w = [place(f"s_w{i}", [P, P], at=at) for i in range(6)]
        s_o = place("s_o", [P, 64], at=at)
        s_o2 = place("s_o2", [P, 64], at=at)
        s_r2 = place("s_r2", [P, 2, 64], at=at)

        ps = ctx.enter_context(nc.psum_tensor("ps", [P, 8, 512], F32))

        def p_(name, k=0, n=None):
            lo, hi = columns(PARAMS)[0][name]
            return par[:, lo + k:(hi if n is None else lo + k + n)]

        def c_(name):
            for table, t in ((CONSTS, cst), (CONSTS_REC, crec), (CONSTS_ATT, catt)):
                cols = columns(table)[0]
                if name in cols:
                    return t[:, cols[name][0]:cols[name][1]]

        def half(bank, h):
            return ps[:, bank + h, 0:HALF]

        def pair(bank):
            return ps[:, bank:bank + 2, 0:HALF]

        def two(ap):
            return ap.rearrange("p (a t) -> p a t", a=2)

        IDENT, ONES = c_("ident"), c_("ones")

        landed = [sem(f"landed{i}") for i in range(RAW)]
        hi_split, lo_split = sem("hi_split"), sem("lo_split")
        slab_done = sem("slab_done")
        drained = sem("drained")
        x_in, par_in = sem("x_in"), sem("par_in")
        crec_in, catt_in, ptab_in = sem("crec_in"), sem("catt_in"), sem("ptab_in")
        small_set = sem("small_set")
        outs = sem("outs")
        c_s_in, g_s_in = sem("c_s_in"), sem("g_s_in")
        c_out, cs_out, gs_out, gss_out = sem("c_out"), sem("cs_out"), sem("gs_out"), sem("gss_out")
        conv_out = sem("conv_out")
        dg_out, diag_in = sem("dg_out"), sem("diag_in")
        kn_out = sem("kn_out")
        k_in = [sem(f"k_in{i}") for i in range(PAGES)]
        v_in = [sem(f"v_in{i}") for i in range(PAGES)]
        vn_out = sem("vn_out")

        nA = Steps(sem("norm_act"), "sq0 sq1 sq2 sq3 sq4 sq5 sq6 sq7 lr rms hi0 hi1 hi2 hi3 hi4 hi5 hi6 hi7")
        nD = Steps(sem("norm_dve"), "n0 lo0 n1 lo1 n2 lo2 n3 lo3 n4 lo4 n5 lo5 n6 lo6 n7 lo7")
        nP = Steps(sem("norm_pe"), "s0 s1 s2 s3 s4 s5 s6 s7")
        gtD = Steps(sem("gate_dve"), "f i neg lf b m lfm ms ri a nm r20 r21 r22 r23 s0 s1 s2 mo0")
        gtA = Steps(sem("gate_act"), "exp ln acol")
        gtP = Steps(sem("gate_pe"), "acol")
        mP = Steps(sem("mlstm_pe"), "bc0 bc1 bc2 bcs scores vtr ktr num0 st0 num1 st1 num2 st2 num3 st3 kb qb dens ssq")
        mA = Steps(sem("mlstm_act"), "ws wi en e kt vt gate abs abs_s sq lr rms")
        mD = Steps(sem("mlstm_dve"), "em qw ve p cn0 cn1 cn2 cn3 nend den rden h vw kw nw ns nq kv cs cq hs dn rd hs2 t mix")
        hA, hD = Steps(sem("mlstm_out_act"), "hi"), Steps(sem("mlstm_out_dve"), "lo")
        mG = Steps(sem("mlstm_pool"), "dk cw dq")
        lP = Steps(sem("decay_pe"), "up")
        lA = Steps(sem("decay_act"), "exp ln")
        lD = Steps(sem("decay_dve"), "z neg lf la q8 sub0")
        fA = Steps(sem("ffn_act"), "u tail gelu hi")
        fD = Steps(sem("ffn_dve"), "t0 t1 s1 t2 s0 prod lo")
        gP = Steps(sem("gla_pe"), "dg0 dg1 dg2 dg3 off vt kdt o0 s0 o1 s1 o2 s2 o3 s3 o4 s4 o5 s5 o6 s6 o7 s7 vb os ssq0 ssq1")
        gA = Steps(sem("gla_act"), "eb qe aend kend ex0 dgc0 ex1 dgc1 ex2 dgc2 ex3 dgc3 ke at vt kdt as o0 o1 sq0 sq1 lr0 rms0 lr1 rms1 hi0 hi1")
        gD = Steps(sem("gla_dve"), "bc sb qe ke kem kend x0 xm0 xk0 xq0 x1 xm1 xk1 xq1 x2 xm2 xk2 xq2 x3 xm3 xk3 xq3 qs qd ks kd "
                   "c0 c1 c2 c3 c4 c5 c6 c7 kv ss h0 h1 hs0 hs1 t0 mix0 lo0 t1 mix1 lo1")
        gG = Steps(sem("gla_pool"), "za dv sa")
        small = Steps(sem("small"), "one eps")
        pads = Steps(sem("pads"), "pad")
        NEXT = "sqq lrq rq kr sqk vr lrk rk vt ssq ssk vtr qn kn"
        def both(engine, names):
            last = " ".join(n for n in names.split() if n not in NEXT.split())
            return Steps(sem("att_" + engine), names), Steps(sem("last_" + engine), last)
        aP, zP = both("pe", "s0 qb s1 ssq t0 v0 s2 t1 v1 s3 t2 v2 t3 v3 st ssk sso mb vtr pv")
        aA, zA = both("act", "sqq ex0 qb ex1 lrq rq att0 ex2 att1 kr sqk ex3 att2 att3 sqo vr lrk rk lro ro se vt")
        aD, zD = both("dve", "m0 x0 nx0 r0 rc0 e0 a0 m1 x1 nx1 mul0 red0 r1 rc1 e1 a1 m2 x2 nx2 mul1 red1 r2 rc2 e2 a2 "
                      "m3 x3 nx3 mul2 red2 r3 rc3 e3 a3 mul3 red3 smax dmx qn kn msv sub mix oall lall")
        aG = Steps(sem("att_pool"), "qd ks vs")
        bP = Steps(sem("first_pe"), "sqs ssq ssk vtr")
        bA = Steps(sem("first_act"), "sqs lrs rqs sqq lrq rq kr sqk vr lrk rk vt")
        bD = Steps(sem("first_dve"), "qs qn kn")
        lamP = Steps(sem("lam_pe"), "sum")
        lamA = Steps(sem("lam_act"), "exp")
        lamD = Steps(sem("lam_dve"), "prod sub lam c0 c1 go")
        tP = Steps(sem("soft_pe"), "new ssq")
        tA = Steps(sem("soft_act"), "ex sq lr rms hi")
        tD = Steps(sem("soft_dve"), "zero new0 new1 newc mt d1 d2 l1 l2 r o1 v1 o2 o3 c1 a mix lo")
        eA = Steps(sem("heads_act"), "hi0 hi1 hi2")
        eD = Steps(sem("heads_dve"), "lo0 lo1 lo2")

        block = ctx.enter_context(nc.Block())

        def wait(eng, steps, name, r=0):
            eng.wait_ge(steps.sem, steps.at(name, r))

        def is_a_wait(v):
            return not isinstance(v, int) or v > 0

        @block.sync
        def _(sp):
            def load_slab(name, nk, i, s):
                f = FIRST[name]
                before = 4 * i + (f + s - RAW + 1)
                if is_a_wait(before):
                    sp.wait_ge(lo_split, before)
                slot = (f + s) % RAW
                sp.dma_start(raw[:, slot, 0:nk * P], a["w_" + name][4 * i + s]).then_inc(landed[slot], 16)

            def load_phase(name, groups):
                nk = dict((n, k) for n, _, k in PHASES)[name]
                first, end = groups
                if end - first <= 1:
                    for i in range(first, end):
                        for s in range(4):
                            load_slab(name, nk, i, s)
                else:
                    with sp.Fori(first, end) as i:
                        for s in range(4):
                            load_slab(name, nk, i, s)

            sp.dma_start(x[:, :, :], a["x"]).then_inc(x_in, 16)
            load_phase("rec_in", (0, 1))
            sp.dma_start(crec[:, :], a["crec"]).then_inc(crec_in, 16)
            load_phase("rec_in", (1, 7))
            load_slab("rec_in", KT, 7, 0)
            load_phase("rec_out", (0, 1))
            for p in range(G_PAIRS):
                wait(sp, gA, "dgc3", p)
                wait(sp, gG, "za", p)
                for hh in range(2):
                    sp.dma_start(a["blocks"][p, hh].rearrange("(q m) x -> m q x", m=4),
                                 dg[hh::32, :, :]).then_inc(dg_out, 16)
                sp.wait_ge(dg_out, 32 * (p + 1))
                for j in range(4):
                    t = slice(SUB * j, SUB * (j + 1))
                    src = a["blocks"][p].rearrange("h (c j) (u s t) -> j u s h c t", c=NC_G, u=2, t=SUB)[j // 2, j % 2]
                    for hh in range(2):
                        sp.dma_start(g_att[t, hh, :, t], src[:, hh]).then_inc(diag_in, 16)
            load_phase("rec_out", (1, 2))
            load_phase("ffn0", (0, S_FFN // 4))
            load_phase("down0", (0, S_DOWN // 4))
            load_phase("att_q", (0, 1))
            sp.wait_ge(slab_done, FIRST["att_q"])
            sp.dma_start(ptab[:, :], a["page_table"]).then_inc(ptab_in, 16)
            sp.wait_ge(ptab_in, 16)

            def load_page(cache, buf, landed_, b, j, free=None):
                page = sp.value_load(ptab[0:1, ds(PAGES * b + j, 1)], min_val=0, max_val=POOL - 1)
                if free is not None:
                    wait(sp, *free)
                sp.dma_start(buf[:, j, :], a[cache][page]).then_inc(landed_[j], 16)

            for j in range(PAGES):
                load_page("cache_k", k_pages, k_in, 0, j)
            load_phase("att_q", (1, 2))
            for j in range(PAGES):
                load_page("cache_v", v_pages, v_in, 0, j)
            load_phase("att_kv", (0, 2))

            def sample_pages(h, slabs_):
                for j in range(PAGES):
                    load_page("cache_k", k_pages, k_in, h + 1, j, (aD, f"mul{j}", h))
                    if j in (1, 3):
                        slabs_(j // 2)
                for j in range(PAGES):
                    load_page("cache_v", v_pages, v_in, h + 1, j, (aP, "pv", h))

            sample_pages(0, lambda u: load_slab("att_kv", KT, 0, 8 + u))
            with sp.Fori(0, (A_HEADS - 2) // 2) as i:
                for w in range(2):
                    sample_pages(2 * i + (1 + w), lambda u: load_slab("att_kv", KT, i, 10 + 2 * w + u))
            load_slab("att_kv", KT, 0, 22)
            load_slab("att_kv", KT, 0, 23)
            load_phase("ffn1", (0, S_FFN // 4))
            load_phase("down1", (0, S_DOWN // 4))

        @block.tensor
        def _(pe):
            def multiply(name, hi, lo, i, s, bank, k_at, ks, first, last, ready=None):
                f = FIRST[name]
                buf = (f + s) % 2
                pe.wait_ge(lo_split, 4 * i + (f + s + 1))
                free = 4 * i + (f + s - 3)
                if is_a_wait(free):
                    pe.wait_ge(drained, free)
                for k in range(ks):
                    if ready is not None:
                        wait(pe, nD, f"lo{k}", ready)
                    w = slice(k * P, (k + 1) * P)
                    for w_part, parts in ((w_hi, (hi, lo)), (w_lo, (hi,))):
                        for m_part in parts:
                            for h in range(2):
                                start = first and k == 0 and w_part is w_hi and m_part is hi
                                stop = last and k == ks - 1 and w_part is w_lo
                                ins = TE.matmul(half(bank, h), w_part[:, buf, w],
                                                m_part[:, k_at + k, h * HALF:(h + 1) * HALF],
                                                start=start, stop=stop)
                ins.then_inc(slab_done, 1)

            def project(name, n, norm=None):
                def group(i, slabs=4):
                    for s in range(slabs):
                        multiply(name, h_hi, h_lo, i, s, 2 * s, 0, KT, True, True,
                                 norm if s == 0 else None)
                groups = n // 4
                group(0)
                if groups > 2:
                    with pe.Fori(1, groups) as i:
                        group(i)
                elif groups == 2:
                    group(1)
                if n % 4:
                    group(groups, n % 4)

            def down(name):
                with pe.Fori(0, S_DOWN // 4) as i:
                    for s in range(4):
                        multiply(name, a_hi, a_lo, i, s, 4 * (s // 2), KD * (s % 2), KD, s % 2 == 0, s % 2 == 1)

            def slab_part(n, buf, ks, bank):
                if ks[0] == 0:
                    pe.wait_ge(lo_split, n + 1)
                for k in ks:
                    w = slice(k * P, (k + 1) * P)
                    for w_part, parts in ((w_hi, (h_hi, h_lo)), (w_lo, (h_hi,))):
                        for m_part in parts:
                            for g in range(2):
                                ins = TE.matmul(half(bank, g), w_part[:, buf, w], m_part[:, k, g * HALF:(g + 1) * HALF],
                                                start=k == 0 and w_part is w_hi and m_part is h_hi,
                                                stop=k == KT - 1 and w_part is w_lo)
                if KT - 1 in ks:
                    ins.then_inc(slab_done, 1)

            def norm(r, bank, after=None):
                if after is not None:
                    pe.wait_ge(drained, after)
                for c in range(KT):
                    wait(pe, nA, f"sq{c}", r)
                    for h in range(2):
                        ins = TE.matmul(half(bank, h), ONES, sq[:, c % 2, h * HALF:(h + 1) * HALF],
                                        start=c == 0, stop=c == KT - 1)
                    ins.then_inc(nP.sem, 1)

            pe.wait_ge(par_in, 32)
            norm(0, 6)
            for n in range(len(FIRST_SLABS)):
                multiply("rec_in", h_hi, h_lo, 0, n, 2 * (n % 4), 0, KT, True, True, 0 if n == 0 else None)

            pe.wait_ge(drained, 4)
            wait(pe, gtD, "a")
            for c in range(NC_M):
                ins = TE.transpose(ps[:, 7, 4 * c:4 * c + 4], a_row[0:4, c * P:(c + 1) * P], IDENT[0:4, 0:4])
            ins.then_inc(gtP.sem, 1)

            SEL = c_("sel_head").rearrange("p (h m) -> p h m", h=M_HEADS)
            for h in range(M_HEADS):
                q, k, v = z[:, h, :], z[:, 4 + h, :], z[:, 8 + h, :]
                first = len(FIRST_SLABS) + PER_HEAD * h

                def part(j, k0=0, k1=KT):
                    n = first + j
                    if k0 == 0:
                        pe.wait_ge(drained, n)
                    slab_part(n, n % 2, range(k0, k1), 2)

                if h == 0:
                    pe.wait_ge(drained, len(FIRST_SLABS))
                    wait(pe, gtD, "mo0")
                    wait(pe, gtA, "acol")
                else:
                    wait(pe, mD, "cq", h - 1)
                    wait(pe, mA, "rms", h - 1)
                for bank, row in ((0, r_intra), (1, r_inter), (6, r_negm)):
                    TE.matmul(ps[:, bank, :], SEL[0:4, h, :], row[:, :], start=True, stop=True).then_inc(mP.sem, 1)
                TE.matmul(ps[:, 4, 0:3 * B], SEL[0:4, h, :], r_s[:, :], start=True, stop=True).then_inc(mP.sem, 1)
                for c in range(NC_M):
                    t = slice(c * P, (c + 1) * P)
                    ins = TE.matmul(ps[:, 7, t], k[:, t], q[:, t], start=True, stop=True)
                ins.then_inc(mP.sem, 1)
                for bank, rows in ((5, v), (4, k)):
                    if bank == 4:
                        wait(pe, mA, "ws", h)
                    for c in range(NC_M):
                        ins = TE.transpose(ps[:, bank, c * P:(c + 1) * P], rows[:, c * P:(c + 1) * P], IDENT)
                    ins.then_inc(mP.sem, 1)
                part(0)
                part(1)
                wait(pe, mD, "p", h)
                wait(pe, mA, "en", h)
                for c in range(NC_M):
                    t = slice(c * P, (c + 1) * P)
                    if c:
                        wait(pe, mD, f"cn{c - 1}", h)
                    TE.matmul(ps[:, 6, t], v_tok[:, c, :], e_mat[:, c, :], start=True, stop=c == 0)
                    ins = TE.matmul(ps[:, 7, t], ONES, e_mat[:, c, :], start=True, stop=c == 0) if c == 0 else None
                    if c:
                        TE.matmul(ps[:, 6, t], c_n[:, 0:P], q_w[:, t], start=False, stop=True)
                        TE.matmul(ps[:, 7, t], ONES, e_mat[:, c, :], start=True, stop=False)
                        ins = TE.matmul(ps[:, 7, t], c_n[:, P:2 * P], q_w[:, t], start=False, stop=True)
                    ins.then_inc(mP.sem, 1)
                    TE.matmul(ps[:, c % 2, 0:2 * P], k_tok[:, c, :], v_end[:, c, :, :].rearrange("p a v -> p (a v)"),
                              start=True, stop=True).then_inc(mP.sem, 1)
                    part(2, 2 * c, 2 * c + 2)
                wait(pe, mG, "dk", h)
                for n in range(2):
                    ins = TE.matmul(ps[:, 4 + n, :], ONES, diag_k[:, 4 * n:4 * n + 4, :].rearrange("p b k -> p (b k)"),
                                    start=True, stop=True)
                ins.then_inc(mP.sem, 1)
                part(3)
                wait(pe, mG, "dq", h)
                wait(pe, mD, "cn3", h)
                for n in range(2):
                    ins = TE.matmul(ps[:, n, :], ONES, diag_q[:, 4 * n:4 * n + 4, :].rearrange("p b k -> p (b k)"),
                                    start=True, stop=True)
                ins.then_inc(mP.sem, 1)
                wait(pe, mD, "nq", h)
                TE.matmul(ps[:, 6, 0:B], ONES, nq[:, :], start=True, stop=True).then_inc(mP.sem, 1)
                part(4)
                wait(pe, mA, "sq", h)
                wait(pe, mD, "kv", h)
                for n in range(2):
                    ins = TE.matmul(half(4, n), ONES, sq[:, 0, n * HALF:(n + 1) * HALF], start=True, stop=True)
                ins.then_inc(mP.sem, 1)
                part(5)

            pe.wait_ge(mD.sem, mD.all(M_HEADS))
            pe.wait_ge(drained, S_REC_IN)
            for p in range(G_PAIRS):
                for n in range(2):
                    ins = TE.matmul(half(2 * p, n), c_("w_gate_up")[64:80, p * P:(p + 1) * P],
                                    gates[64:80, n * HALF:(n + 1) * HALF], start=True, stop=True)
            ins.then_inc(lP.sem, 1)
            wait(pe, lD, "z")
            for p in range(G_PAIRS):
                if p:
                    pe.wait_ge(gD.sem, gD.all(p))
                for n in range(4):
                    wait(pe, gD, f"xq{n}", p)
                    flat = lx[:, :, :, :].rearrange("p b s t -> p (b s t)")
                    for m in range(4):
                        ins = TE.matmul(ps[32 * m:32 * m + 32, n, :], c_("half_sum"), flat[:, 512 * m:512 * m + 512],
                                        start=True, stop=True)
                    ins.then_inc(gP.sem, 1)
                wait(pe, gD, "qs", p)
                wait(pe, gD, "ks", p)
                for hh in range(2):
                    r = slice(64 * hh, 64 * hh + 64)
                    for c in range(NC_G):
                        for j in range(1, 4):
                            at_ = c * LC_G + j * SUB
                            ins = TE.matmul(ps[0:SUB * j, 4 + hh, at_:at_ + SUB], ke[r, c, j - 1, 0:SUB * j],
                                            g_qs[r, at_:at_ + SUB], start=True, stop=True)
                ins.then_inc(gP.sem, 1)
                wait(pe, gA, "dgc1", p)
                for hh in range(2):
                    for c in range(NC_G):
                        bank = (6, 0)[hh] + c // 4
                        ins = TE.transpose(ps[0:64, bank, (c % 4) * P:(c % 4 + 1) * P],
                                           z[:, 20 + 2 * p + hh, c * LC_G:(c + 1) * LC_G], IDENT)
                ins.then_inc(gP.sem, 1)
                wait(pe, gD, "kd", p)
                wait(pe, gA, "dgc3", p)
                for c in range(NC_G):
                    ins = TE.transpose(ps[0:64, 2 + c // 4, (c % 4) * P:(c % 4 + 1) * P],
                                       g_kd[:, c * LC_G:(c + 1) * LC_G], IDENT)
                ins.then_inc(gP.sem, 1)
                wait(pe, gA, "at", p)
                wait(pe, gA, "kdt", p)
                pe.wait_ge(diag_in, 8 * 16 * (p + 1))
                for c in range(NC_G):
                    t = slice(c * LC_G, (c + 1) * LC_G)
                    if c:
                        wait(pe, gD, f"c{c - 1}", p)
                    for hh in range(2):
                        r = slice(64 * hh, 64 * hh + 64)
                        ins = TE.matmul(ps[:, 4 + hh, t], g_vt[:, hh, c, :], g_att[:, hh, c, :], start=True, stop=True)
                        if c:
                            ins = TE.matmul(ps[:, 6 + hh, t], g_s[r, :], g_qd[r, t], start=True, stop=True)
                    ins.then_inc(gP.sem, 1)
                    for hh in range(2):
                        r = slice(64 * hh, 64 * hh + 64)
                        ins = TE.matmul(ps[r, c % 2, 0:P], g_kdt[:, c, r], g_vt[:, hh, c, :], start=True, stop=True)
                    ins.then_inc(gP.sem, 1)
                wait(pe, gG, "dv", p)
                for n in range(2):
                    for hh, half_ones in ((0, c_("ones_lo")), (1, c_("ones_hi"))):
                        ins = TE.matmul(ps[:, 2 + n, :], half_ones,
                                        g_dv[:, hh, 4 * n:4 * n + 4, :].rearrange("p b v -> p (b v)"),
                                        start=hh == 0, stop=hh == 1)
                ins.then_inc(gP.sem, 1)
                wait(pe, gD, "ss", p)
                for hh in range(2):
                    r = slice(64 * hh, 64 * hh + 64)
                    for b in range(B):
                        ins = TE.matmul(ps[:, hh, 256 + b:257 + b], g_ss[r, b, :], z[r, 16 + p, T + b:T + b + 1],
                                        start=True, stop=True)
                ins.then_inc(gP.sem, 1)
                for hh in range(2):
                    wait(pe, gA, f"sq{hh}", p)
                    wait(pe, gD, f"h{hh}", p)
                    bank = (4, 6)[hh]
                    for n in range(2):
                        ins = TE.matmul(half(bank, n), ONES, sq[:, hh, n * HALF:(n + 1) * HALF], start=True, stop=True)
                    ins.then_inc(gP.sem, 1)

            pe.wait_ge(gD.sem, gD.all(G_PAIRS))
            project("rec_out", S_OUT)
            norm(1, 0, FIRST["rec_out"] + 5)
            project("ffn0", S_FFN, 1)
            wait(pe, fD, "lo", FT - 1)
            down("down0")
            norm(2, 6)
            project("att_q", A_HEADS, 2)

            pe.wait_ge(catt_in, 16)
            pe.wait_ge(drained, FIRST["att_kv"])
            wait(pe, lamD, "prod")
            TE.matmul(ps[:, 0, 0:2], ONES[0:64, :], lam[0:64, 0:2], start=True, stop=True).then_inc(lamP.sem, 1)
            HALVES = c_("ones_half")

            def sums(bank, n, steps):
                for g in range(2):
                    ins = TE.matmul(half(bank, g), HALVES, sq3[:, n, g * HALF:(g + 1) * HALF], start=True, stop=True)
                ins.then_inc(steps.sem, 1)

            def v_rows(steps):
                for c in range(4):
                    ins = TE.transpose(ps[:, 0, c * P:(c + 1) * P], vn[:, c * P:(c + 1) * P], IDENT)
                ins.then_inc(steps.sem, 1)

            wait(pe, bA, "sqs")
            TE.matmul(ps[:, 6, 0:64], HALVES, qs_r[:, :, :].rearrange("p h b -> p (h b)"), start=True,
                      stop=True).then_inc(bP.sem, 1)
            wait(pe, lamA, "exp")
            slab_part(FIRST["att_kv"], FIRST["att_kv"] % 2, range(KT), 0)
            wait(pe, bA, "sqq")
            sums(2, 0, bP)
            wait(pe, bA, "sqk")
            slab_part(FIRST["att_kv"] + 1, (FIRST["att_kv"] + 1) % 2, range(KT), 0)
            sums(4, 1, bP)
            wait(pe, bA, "vr")
            v_rows(bP)

            def head(h, u, r_=None, first=False, last=False):
                sP_, sA_, sD_, r = (zP, zA, zD, 0) if last else (aP, aA, aD, h)
                n = FIRST["att_kv"] + 2 * (h + 1)
                bufs = (FIRST["att_kv"] % 2, (FIRST["att_kv"] + 1) % 2)

                def part(s, k0, k1):
                    if not last:
                        slab_part(n + s, bufs[s], range(k0, k1), 0)

                def scores(i):
                    for c in range(2):
                        g = slice(64 * c, 64 * c + 64)
                        ins = TE.matmul(ps[:, 2 + c, 0:(i + 1) * P], qn[g, u, i * P:(i + 1) * P],
                                        kn[g, u, 0:(i + 1) * P], start=True, stop=True)
                    ins.then_inc(sP_.sem, 1)

                def turn(i):
                    wait(pe, sD_, f"a{i}", r)
                    for c in range(i + 1):
                        ins = TE.transpose(ps[:, 4, c * P:(c + 1) * P], a_att[:, i % 2, c * P:(c + 1) * P], IDENT)
                    ins.then_inc(sP_.sem, 1)

                def values(i):
                    wait(pe, sA_, f"att{i}", r)
                    for c in range(i + 1):
                        ins = TE.matmul(ps[:, 5, i * P:(i + 1) * P], v_t2[:, u, c, :], at_t[:, i % 2, c * P:(c + 1) * P],
                                        start=c == 0, stop=c == i)
                    ins.then_inc(sP_.sem, 1)

                if first:
                    wait(pe, bD, "kn")
                else:
                    wait(pe, aD, "kn", h - 1)
                scores(0)
                if first:
                    wait(pe, bA, "vt")
                else:
                    wait(pe, aA, "vt", h - 1)
                part(0, 0, 2)
                if first:
                    wait(pe, bA, "rqs")
                    wait(pe, aG, "qd", 0)
                else:
                    wait(pe, aD, "lall", h - 1)
                    wait(pe, aG, "qd", h)
                for g in range(2):
                    ins = TE.matmul(ps[:, 6 + g, :], ONES, qd[:, 4 * g:4 * g + 4, :].rearrange("p h k -> p (h k)"),
                                    start=True, stop=True)
                ins.then_inc(sP_.sem, 1)
                part(0, 2, 4)
                wait(pe, sA_, "ex0", r)
                scores(1)
                if not last:
                    wait(pe, sA_, "qb", r)
                    wait(pe, sA_, "sqq", r)
                    sums(6, 0, sP_)
                if not first:
                    wait(pe, aA, "ro", h - 1)
                turn(0)
                part(0, 4, 6)
                values(0)
                wait(pe, sA_, "ex1", r)
                scores(2)
                turn(1)
                part(0, 6, 8)
                values(1)
                wait(pe, sA_, "ex2", r)
                scores(3)
                turn(2)
                if not last:
                    wait(pe, sA_, "sqk", r)
                part(1, 0, 3)
                values(2)
                turn(3)
                part(1, 3, 6)
                values(3)
                wait(pe, sD_, "red3", r)
                if last:
                    wait(pe, sA_, "qb", r)
                else:
                    wait(pe, sA_, "rq", r)
                for j in range(PAGES):
                    ins = TE.transpose(ps[0:16, 6, j * P:(j + 1) * P], s_sc[:, j, :], IDENT)
                ins.then_inc(sP_.sem, 1)
                part(1, 6, 8)
                if not last:
                    wait(pe, sA_, "ex3", r)
                    sums(2, 1, sP_)
                wait(pe, sA_, "sqo", r)
                TE.matmul(ps[:, 4, :], ONES, sq3[:, 2, 0:T], start=True, stop=True).then_inc(sP_.sem, 1)
                wait(pe, sD_, "dmx", r)
                TE.matmul(ps[:, 7, 0:16], ONES[0:16, :], s_dm[0:16, :], start=True, stop=True).then_inc(sP_.sem, 1)
                if not last:
                    wait(pe, sA_, "vr", r)
                    v_rows(sP_)
                wait(pe, sA_, "se", r)
                wait(pe, sD_, "sub", r)
                for j in range(PAGES):
                    TE.matmul(ps[:, 7, 16:32], ONES, s_sc[:, j, :], start=j == 0, stop=j == PAGES - 1)
                for j in range(PAGES):
                    pe.wait_ge(v_in[j], 16 * h + 16)
                    for g in range(A_HEADS):
                        ins = TE.matmul(ps[:, 7, 64 + 16 * j + 2 * g:66 + 16 * j + 2 * g], v_pages[:, j, g * P:(g + 1) * P],
                                        s_sc[:, j, 2 * g:2 * g + 2], start=True, stop=True)
                ins.then_inc(sP_.sem, 1)

            head(0, 0, first=True)
            with pe.Fori(0, (A_HEADS - 2) // 2) as i:
                for u in range(2):
                    head(2 * i + (1 + u), 1 - u)
            head(A_HEADS - 1, 1, last=True)

            wait(pe, tD, "new1")
            TE.matmul(ps[:, 0, 0:P], ONES, s_new[:, :], start=True, stop=True).then_inc(tP.sem, 1)
            wait(pe, tA, "sq")
            TE.matmul(ps[:, 6, 0:64], ONES, s_r2[:, 0, :], start=True, stop=True).then_inc(tP.sem, 1)
            wait(pe, tD, "lo")
            wait(pe, eD, "lo2")
            project("att_out", S_OUT)
            norm(3, 0, FIRST["att_out"] + 5)
            project("ffn1", S_FFN, 3)
            wait(pe, fD, "lo", 2 * FT - 1)
            down("down1")

        def walk(eng, name, split, drain):
            nk = dict((n, k) for n, _, k in PHASES)[name]
            total = dict((n, s) for n, s, _ in PHASES)[name]
            loops = (total - 2) // 4

            def step(i, s, left=2):
                if left >= 2:
                    split(name, i, s + 2, nk)
                else:
                    order = [n for n, _, _ in PHASES]
                    after = order.index(name) + 1
                    if after < len(PHASES):
                        split(order[after], 0, 1 - left, PHASES[after][2])
                drain(i, s)

            peeled = 1 if loops == 1 or FIRST[name] == 0 else 0
            for s in range(4 * peeled):
                step(0, s)
            if loops > peeled:
                with eng.Fori(peeled, loops) as i:
                    for s in range(4):
                        step(i, s)
            for n in range(4 * loops, total):
                step(loops, n - 4 * loops, total - 1 - n)

        @block.scalar
        def _(act):
            LN_EXP = "natural_log_exp_and_others"

            def rsqrt(out, total, n, steps, ln, r=0):
                S.activation(out, total, ACT.Ln, bias=eps[:, :], scale=1.0 / n).then_inc(steps.sem, 1)
                wait(act, steps, ln, r)
                return S.activation(out, out, ACT.Exp, scale=-0.5)

            def split(name, i, s, nk):
                n = FIRST[name] + s
                act.wait_ge(landed[n % RAW], 16 * (i + n // RAW + 1))
                if is_a_wait(4 * i + (n - 1)):
                    act.wait_ge(slab_done, 4 * i + (n - 1))
                S.copy(w_hi[:, n % 2, 0:nk * P], raw[:, n % RAW, 0:nk * P]).then_inc(hi_split, 1)

            def norm(r, bank, before):
                S.preload_act_table_set(LN_EXP)
                for c in range(KT):
                    before(c)
                    if c >= 2:
                        wait(act, nP, f"s{c - 2}", r)
                    S.activation(sq[:, c % 2, :], x[:, c, :], ACT.Square).then_inc(nA.sem, 1)
                wait(act, nP, "s7", r)
                wait(act, small, "eps")
                rsqrt(two(rstd[:, :]), pair(bank), D_MODEL, nA, "lr", r).then_inc(nA.sem, 1)
                for c in range(KT):
                    wait(act, nD, f"n{c}", r)
                    S.copy(h_hi[:, c, :], hn[:, c % 2, :]).then_inc(nA.sem, 1)

            def tile_out(name, out):
                def drain(i, s):
                    act.wait_ge(slab_done, 4 * i + (FIRST[name] + s + 1))
                    S.copy(two(out[:, 4 * i + s, :]) if isinstance(i, int) else
                           out[:, ds(4 * i + s, 1), :].rearrange("p o (a t) -> p (o a) t", a=2),
                           pair(2 * (s % 4))).then_inc(drained, 1)
                return drain

            def rec_step(n):
                if n + 2 < S_REC_IN:
                    split("rec_in", 0, n + 2, KT)
                else:
                    split("rec_out", 0, n + 2 - S_REC_IN, KT)
                act.wait_ge(slab_done, n + 1)
                out = gates[:, :] if REC_TILES[n] == 28 else z[:, REC_TILES[n], :]
                bank = 2 * (n % 4) if n < len(FIRST_SLABS) else 2
                S.copy(two(out), pair(bank)).then_inc(drained, 1)

            def nothing(i, s):
                pass

            def ffn(layer):
                name = f"ffn{layer}"

                def drain(i, s):
                    r = 2 * i + (s // 2 + layer * FT)
                    m = 2 * i + s // 2
                    act.wait_ge(slab_done, 4 * i + (FIRST[name] + s + 1))
                    if s % 2 == 0:
                        S.copy(two(ub[:, s // 2, 2:2 + NT]), pair(2 * (s % 4))).then_inc(fA.sem, 1)
                        S.copy(conv_end[:, ds(m, 1), :] if not isinstance(m, int) else conv_end[:, m:m + 1, :],
                               ps[:, 2 * s + 1:2 * s + 2, HALF - 2 - B:HALF]).then_inc(fA.sem, 1)
                        act.wait_ge(fD.sem, fD.at("s0", r))
                        S.activation(ge[:, :], cc[:, :], ACT.Gelu_apprx_tanh).then_inc(fA.sem, 1)
                    else:
                        act.wait_ge(fD.sem, fD.at("prod", r))
                        S.copy(a_hi[:, ds(m, 1), :] if not isinstance(m, int) else a_hi[:, m:m + 1, :],
                               pr[:, :].rearrange("p (o t) -> p o t", o=1)).then_inc(fA.sem, 1)
                S.preload_act_table(ACT.Gelu_apprx_tanh)
                if layer:
                    act.wait_ge(conv_out, 16)
                walk(act, name, split, drain)

            act.dma_start(par[:, :], a["par"]).then_inc(par_in, 16)
            act.dma_start(cst[:, :], a["cst"]).then_inc(par_in, 16)
            act.wait_ge(x_in, 16)
            norm(0, 6, lambda c: None)
            split("rec_in", 0, 0, KT)
            split("rec_in", 0, 1, KT)
            rec_step(0)

            rec_step(1)
            wait(act, gtD, "neg")
            S.activation(f_log[:, :], f_neg[:, :], ACT.Exp).then_inc(gtA.sem, 1)
            wait(act, gtA, "exp")
            S.activation(f_log[:, :], f_log[:, :], ACT.Ln, bias=one[0:4, :]).then_inc(gtA.sem, 1)
            for n in range(2, len(FIRST_SLABS)):
                rec_step(n)
            wait(act, gtP, "acol")
            S.copy(a_col[:, :, :], ps[:, 7, 0:4 * NC_M].rearrange("p (c h) -> p c h", h=4)).then_inc(gtA.sem, 1)

            for h in range(M_HEADS):
                first = len(FIRST_SLABS) + PER_HEAD * h
                wait(act, mP, "bcs", h)
                S.activation(w_s[:, :, :].rearrange("p a b -> p (a b)"), ps[:, 4, 0:3 * B], ACT.Exp).then_inc(mA.sem, 1)
                S.activation(w_int[:, :], ps[:, 1, :], ACT.Exp).then_inc(mA.sem, 1)
                if h:
                    wait(act, mD, "mix", h - 1)
                S.activation(e_negm[:, :], ps[:, 6, :], ACT.Exp).then_inc(mA.sem, 1)
                wait(act, mD, "em", h)
                for c in range(NC_M):
                    ins = S.activation(e_mat[:, c, :], e_mat[:, c, :], ACT.Exp, bias=a_col[:, c, h:h + 1])
                ins.then_inc(mA.sem, 1)
                wait(act, mP, "ktr", h)
                S.copy(k_tok[:, :, :].rearrange("p c k -> p (c k)"), ps[:, 4, :]).then_inc(mA.sem, 1)
                S.copy(v_tok[:, :, :].rearrange("p c k -> p (c k)"), ps[:, 5, :]).then_inc(mA.sem, 1)
                rec_step(first)
                act.wait_ge(drained, first + 1)
                gate = (z[:, 12:14, :], z[:, 14, :], z[:, 15, :], None)[h]
                if gate is not None:
                    ins = S.activation(gate, gate, ACT.Sigmoid)
                if h == 2:
                    S.activation(z[:, 24:28, :], z[:, 24:28, :], ACT.Silu)
                if gate is not None:
                    S.preload_act_table_set(LN_EXP)
                act.sem_inc(mA.sem, 1)
                rec_step(first + 1)
                wait(act, mP, "num3", h)
                S.activation(den[:, :], ps[:, 7, :], ACT.Abs).then_inc(mA.sem, 1)
                rec_step(first + 2)
                rec_step(first + 3)
                wait(act, mP, "dens", h)
                S.activation(den_s[:, :], ps[:, 6, 0:B], ACT.Abs).then_inc(mA.sem, 1)
                wait(act, mD, "hs2", h)
                S.activation(sq[:, 0, :], h_head[:, :], ACT.Square).then_inc(mA.sem, 1)
                rec_step(first + 4)
                wait(act, mP, "ssq", h)
                rsqrt(two(rstd[:, :]), pair(4), P, mA, "lr", h).then_inc(mA.sem, 1)
                rec_step(first + 5)
            act.wait_ge(slab_done, S_REC_IN)
            wait(act, mD, "mix", M_HEADS - 1)
            S.copy(h_hi[:, 0:4, :], z[:, 12:16, :]).then_inc(hA.sem, 1)

            wait(act, lD, "neg")
            S.activation(ln_t[:, :, :], ln_t[:, :, :], ACT.Exp).then_inc(lA.sem, 1)
            wait(act, lA, "exp")
            S.activation(ln_t[:, :, :], ln_t[:, :, :], ACT.Ln, bias=one[:, :]).then_inc(lA.sem, 1)
            for p in range(G_PAIRS):
                wait(act, gD, "bc", p)
                S.activation(g_qd[:, :], bc[:, :], ACT.Exp).then_inc(gA.sem, 1)
                wait(act, gD, "qe", p)
                S.activation(g_qs[:, :], g_qs[:, :], ACT.Exp).then_inc(gA.sem, 1)
                S.activation(a_end[:, :], bc[:, LC_G - 1::LC_G], ACT.Exp).then_inc(gA.sem, 1)
                wait(act, gD, "kend", p)
                S.activation(g_kd[:, :], g_kd[:, :], ACT.Exp).then_inc(gA.sem, 1)
                flat = lx[:, :, :, :].rearrange("p b s t -> p (b s t)")
                if p:
                    act.wait_ge(gss_out, 16)
                for n in range(4):
                    wait(act, gD, f"xm{n}", p)
                    S.activation(flat, flat, ACT.Exp).then_inc(gA.sem, 1)
                    wait(act, gP, f"dg{n}", p)
                    S.copy(dg[:, n, :], ps[:, n, :]).then_inc(gA.sem, 1)
                wait(act, gD, "kem", p)
                S.activation(ke[:, :, :, :].rearrange("p c j s -> p (c j s)"),
                             ke[:, :, :, :].rearrange("p c j s -> p (c j s)"), ACT.Exp).then_inc(gA.sem, 1)
                wait(act, gP, "off", p)
                wait(act, gG, "za", p)
                for hh in range(2):
                    for j in range(1, 4):
                        r, t = slice(0, SUB * j), slice(SUB * j, SUB * (j + 1))
                        ins = S.copy(g_att[r, hh, :, t],
                                     ps[r, 4 + hh, :].rearrange("p (c t) -> p c t", c=NC_G)[:, :, t])
                ins.then_inc(gA.sem, 1)
                wait(act, gP, "vt", p)
                for hh in range(2):
                    bank = (6, 0)[hh]
                    ins = S.copy(g_vt[:, hh, :, :].rearrange("p (n c) v -> p n (c v)", n=2), ps[0:64, bank:bank + 2, :])
                ins.then_inc(gA.sem, 1)
                wait(act, gP, "kdt", p)
                S.copy(g_kdt[:, :, :].rearrange("p (n c) v -> p n (c v)", n=2), ps[0:64, 2:4, :]).then_inc(gA.sem, 1)
                S.activation(a_s[:, :], log_a[:, p, T:NT], ACT.Exp).then_inc(gA.sem, 1)
                for hh in range(2):
                    wait(act, gP, "o7", p)
                    S.copy(g_h[:, hh, LC_G:T], ps[:, 6 + hh, LC_G:T]).then_inc(gA.sem, 1)
                for hh in range(2):
                    wait(act, gD, f"hs{hh}", p)
                    S.activation(sq[:, hh, :], g_h[:, hh, :], ACT.Square).then_inc(gA.sem, 1)
                for hh in range(2):
                    wait(act, gP, f"ssq{hh}", p)
                    if hh:
                        wait(act, gD, "t0", p)
                    rsqrt(two(rstd[:, :]), pair((4, 6)[hh]), P, gA, f"lr{hh}", p).then_inc(gA.sem, 1)
                for hh in range(2):
                    wait(act, gD, f"mix{hh}", p)
                    S.copy(h_hi[:, 4 + 2 * p + hh, :], hn[:, hh, :]).then_inc(gA.sem, 1)

            walk(act, "rec_out", split, nothing)
            norm(1, 0, lambda c: act.wait_ge(drained, FIRST["rec_out"] + c + 1))
            ffn(0)
            walk(act, "down0", split, nothing)
            norm(2, 6, lambda c: act.wait_ge(drained, FIRST["down0"] + 2 * (c + 1)))
            walk(act, "att_q", split, tile_out("att_q", zq))

            S.preload_act_table_set(LN_EXP)
            wait(act, lamP, "sum")
            S.activation(lam[:, 2:4], ps[:, 0, 0:2], ACT.Exp).then_inc(lamA.sem, 1)

            def zq_of(h):
                return zq[:, h, :] if isinstance(h, int) else zq[:, ds(h, 1), :].rearrange("p o t -> p (o t)")

            F_KV = FIRST["att_kv"]
            act.wait_ge(drained, F_KV)
            S.activation(qs_r[:, :, :], zq[:, :, T:NT], ACT.Square).then_inc(bA.sem, 1)
            wait(act, bP, "sqs")
            rsqrt(qs_t[:, :, :].rearrange("p h b -> p (h b)"), ps[:, 6, 0:64], A_QK, bA, "lrs").then_inc(bA.sem, 1)
            S.activation(sq3[:, 0, :], zq[:, 0, :], ACT.Square).then_inc(bA.sem, 1)
            wait(act, bP, "ssq")
            rsqrt(two(rs3[:, 0, :]), pair(2), A_QK, bA, "lrq").then_inc(bA.sem, 1)
            act.wait_ge(slab_done, F_KV + 1)
            S.copy(two(kraw[:, :]), pair(0)).then_inc(bA.sem, 1)
            S.activation(two(sq3[:, 1, :]), pair(0), ACT.Square).then_inc(bA.sem, 1)
            split("att_kv", 0, 2, KT)
            act.wait_ge(slab_done, F_KV + 2)
            S.copy(two(vn[:, :]), pair(0)).then_inc(bA.sem, 1)
            split("att_kv", 0, 3, KT)
            wait(act, bP, "ssk")
            rsqrt(two(rs3[:, 1, :]), pair(4), A_QK, bA, "lrk").then_inc(bA.sem, 1)
            wait(act, bP, "vtr")
            S.copy(v_t2[:, 0, :, :].rearrange("p c v -> p (c v)"), ps[:, 0, :]).then_inc(bA.sem, 1)

            def head(h, u, i, h0, last=False):
                sP_, sA_, sD_, r = (zP, zA, zD, 0) if last else (aP, aA, aD, h)

                def exps(k):
                    wait(act, sD_, f"nx{k}", r)
                    for c in range(2):
                        ins = S.activation(e_att[:, k % 2, c, 0:(k + 1) * P], ps[:, 2 + c, 0:(k + 1) * P], ACT.Exp,
                                           bias=mx[:, k % 2, c:c + 1], scale=A_QK ** -0.5, accum_out=sm[:, k % 2, c:c + 1])
                    ins.then_inc(sA_.sem, 1)

                def copy_t(k):
                    wait(act, sP_, f"t{k}", r)
                    S.copy(at_t[:, k % 2, 0:(k + 1) * P], ps[:, 4, 0:(k + 1) * P]).then_inc(sA_.sem, 1)

                if not last:
                    S.activation(sq3[:, 0, :], zq_of(h + 1), ACT.Square).then_inc(sA_.sem, 1)
                exps(0)
                wait(act, sP_, "qb", r)
                S.copy(qb[:, :].rearrange("p (n k) -> p n k", n=2), ps[:, 6:8, :]).then_inc(sA_.sem, 1)
                exps(1)
                if not last:
                    wait(act, sP_, "ssq", r)
                    rsqrt(two(rs3[:, 0, :]), pair(6), A_QK, sA_, "lrq", r).then_inc(sA_.sem, 1)
                copy_t(0)
                exps(2)
                copy_t(1)
                if not last:
                    n0 = F_KV + 2 * (h + 1)
                    act.wait_ge(slab_done, n0 + 1)
                    S.copy(two(kraw[:, :]), pair(0)).then_inc(sA_.sem, 1)
                    S.activation(two(sq3[:, 1, :]), pair(0), ACT.Square).then_inc(sA_.sem, 1)
                    split("att_kv", i, 2 * (h0 + 2), KT)
                exps(3)
                if last:
                    S.copy(h_hi[:, 0:4, 0:T], zq[:, 0:4, 0:T]).then_inc(eA.sem, 1)
                copy_t(2)
                copy_t(3)
                if last:
                    S.copy(h_hi[:, 4:7, 0:T], zq[:, 4:7, 0:T]).then_inc(eA.sem, 1)
                wait(act, sP_, "v3", r)
                S.activation(sq3[:, 2, 0:T], ps[:, 5, :], ACT.Square).then_inc(sA_.sem, 1)
                if not last:
                    act.wait_ge(slab_done, n0 + 2)
                    act.wait_ge(vn_out, 16 * (h + 1))
                    wait(act, aG, "vs", h)
                    S.copy(two(vn[:, :]), pair(0)).then_inc(sA_.sem, 1)
                    split("att_kv", i, 2 * (h0 + 2) + 1, KT)
                    wait(act, sP_, "ssk", r)
                    rsqrt(two(rs3[:, 1, :]), pair(2), A_QK, sA_, "lrk", r).then_inc(sA_.sem, 1)
                wait(act, sP_, "sso", r)
                rsqrt(rs3[:, 2, 0:T], ps[:, 4, :], P, sA_, "lro", r).then_inc(sA_.sem, 1)
                wait(act, sD_, "sub", r)
                flat = s_sc[:, :, :].rearrange("p j k -> p (j k)")
                S.activation(flat, flat, ACT.Exp, scale=A_QK ** -0.5).then_inc(sA_.sem, 1)
                if not last:
                    wait(act, sP_, "vtr", r)
                    S.copy(v_t2[:, 1 - u, :, :].rearrange("p c v -> p (c v)"), ps[:, 0, :]).then_inc(sA_.sem, 1)

            head(0, 0, 0, 0)
            with act.Fori(0, (A_HEADS - 2) // 2) as i:
                for w in range(2):
                    head(2 * i + (1 + w), 1 - w, i, 1 + w)
            head(A_HEADS - 1, 1, 0, A_HEADS - 1, last=True)
            wait(act, zD, "mix")
            S.copy(h_hi[:, A_HEADS - 1, 0:T], zq[:, A_HEADS - 1, 0:T]).then_inc(eA.sem, 1)

            wait(act, tD, "d2")
            S.activation(s_w[1][:, :], s_w[1][:, :], ACT.Exp, scale=A_QK ** -0.5)
            S.activation(s_w[2][:, :], s_w[2][:, :], ACT.Exp, scale=A_QK ** -0.5).then_inc(tA.sem, 1)
            wait(act, tD, "a")
            S.activation(s_r2[:, 0, :], s_o[:, :], ACT.Square).then_inc(tA.sem, 1)
            wait(act, tP, "ssq")
            rsqrt(s_r2[:, 1, :], ps[:, 6, 0:64], P, tA, "lr").then_inc(tA.sem, 1)
            wait(act, tD, "mix")
            S.copy(h_hi[:, :, T:NT], s_o2[:, :].rearrange("p (b h) -> p h b", b=B)).then_inc(tA.sem, 1)
            act.sem_inc(drained, 2 * A_HEADS)
            act.wait_ge(vn_out, 16 * A_HEADS)

            walk(act, "att_out", split, nothing)
            norm(3, 0, lambda c: act.wait_ge(drained, FIRST["att_out"] + c + 1))
            ffn(1)
            walk(act, "down1", split, nothing)

        @block.vector
        def _(dve):
            def split(name, i, s, nk):
                n = FIRST[name] + s
                dve.wait_ge(hi_split, 4 * i + (n + 1))
                V.tensor_tensor(w_lo[:, n % 2, 0:nk * P], raw[:, n % RAW, 0:nk * P],
                                w_hi[:, n % 2, 0:nk * P].bitcast(F32), ALU.subtract).then_inc(lo_split, 1)

            def norm(r, gain):
                wait(dve, nA, "rms", r)
                for c in range(KT):
                    if c >= 2:
                        wait(dve, nD, f"lo{c - 2}", r)
                    V.scalar_tensor_tensor(out=hn[:, c % 2, :], in0=x[:, c, :], scalar=p_(gain, c, 1), in1=rstd[:, :],
                                           op0=ALU.mult, op1=ALU.mult).then_inc(nD.sem, 1)
                    wait(dve, nA, f"hi{c}", r)
                    V.tensor_tensor(h_lo[:, c, :], hn[:, c % 2, :], h_hi[:, c, :].bitcast(F32),
                                    ALU.subtract).then_inc(nD.sem, 1)

            def nothing(i, s):
                pass

            def out_drain(name):
                def drain(i, s):
                    c = 4 * i + s
                    dve.wait_ge(slab_done, 4 * i + (FIRST[name] + s + 1))
                    xc = x[:, c, :]
                    V.tensor_tensor(two(xc), two(xc), pair(2 * (s % 4)), ALU.add).then_inc(drained, 1)
                return drain

            def down_drain(name):
                def drain(i, s):
                    if s % 2:
                        dve.wait_ge(slab_done, 4 * i + (FIRST[name] + s + 1))
                        xc = x[:, 2 * i + s // 2, :] if isinstance(i, int) else \
                            x[:, ds(2 * i + s // 2, 1), :].rearrange("p o t -> p (o t)")
                        V.tensor_tensor(two(xc), two(xc), pair(4 * (s // 2)), ALU.add).then_inc(drained, 2)
                return drain

            def ffn(layer):
                name = f"ffn{layer}"
                cw, cb, cs = (columns(PARAMS)[0][f"{n}{layer}"][0] for n in ("conv_w", "conv_b", "conv_s"))

                def drain(i, s):
                    r = 2 * i + (s // 2 + layer * FT)
                    m = 2 * i + s // 2

                    def col(at, k=0, n=1, step=1):
                        return par[:, ds(step * m + (at + k), n)] if not isinstance(m, int) else \
                            par[:, at + k + step * m:at + k + step * m + n]
                    u = ub[:, s // 2, :]
                    if s % 2 == 0:
                        dve.wait_ge(fA.sem, fA.at("u", r))
                        V.tensor_scalar(cc[:, :], u[:, 2:2 + NT], col(cw, 2 * FT), col(cb), ALU.mult,
                                        ALU.add).then_inc(fD.sem, 1)
                        dve.wait_ge(fD.sem, fD.at("t0", r))
                        V.scalar_tensor_tensor(out=cc[:, 0:T], in0=u[:, 1:1 + T], scalar=col(cw, FT), in1=cc[:, 0:T],
                                               op0=ALU.mult, op1=ALU.add).then_inc(fD.sem, 1)
                        V.scalar_tensor_tensor(out=cc[:, T:NT], in0=col(cs, B, B, 2 * B), scalar=col(cw, FT),
                                               in1=cc[:, T:NT], op0=ALU.mult, op1=ALU.add).then_inc(fD.sem, 1)
                        dve.wait_ge(fD.sem, fD.at("s1", r))
                        V.scalar_tensor_tensor(out=cc[:, 0:T], in0=u[:, 0:T], scalar=col(cw), in1=cc[:, 0:T],
                                               op0=ALU.mult, op1=ALU.add).then_inc(fD.sem, 1)
                        V.scalar_tensor_tensor(out=cc[:, T:NT], in0=col(cs, 0, B, 2 * B), scalar=col(cw),
                                               in1=cc[:, T:NT], op0=ALU.mult, op1=ALU.add).then_inc(fD.sem, 1)
                    else:
                        dve.wait_ge(fA.sem, fA.at("gelu", r))
                        dve.wait_ge(slab_done, 4 * i + (FIRST[name] + s + 1))
                        V.tensor_tensor(two(pr[:, :]), two(ge[:, :]), pair(2 * (s % 4)), ALU.mult).then_inc(fD.sem, 1)
                        dve.wait_ge(fD.sem, fD.at("prod", r))
                        dve.sem_inc(drained, 2)
                        dve.wait_ge(fA.sem, fA.at("hi", r))
                        lo = a_lo[:, ds(m, 1), :] if not isinstance(m, int) else a_lo[:, m:m + 1, :]
                        hi = a_hi[:, ds(m, 1), :] if not isinstance(m, int) else a_hi[:, m:m + 1, :]
                        V.tensor_tensor(lo, pr[:, :].rearrange("p (o t) -> p o t", o=1), hi.bitcast(F32),
                                        ALU.subtract).then_inc(fD.sem, 1)
                wait(dve, pads, "pad", layer)
                walk(dve, name, split, drain)

            dve.wait_ge(par_in, 32)
            norm(0, "g_mix0")
            split("rec_in", 0, 0, KT)
            split("rec_in", 0, 1, KT)
            split("rec_in", 0, 2, KT)

            dve.wait_ge(drained, 1)
            dve.wait_ge(crec_in, 16)
            bm = columns(PARAMS)[0]["b_mgate"][0]
            V.tensor_scalar(f_pre[:, :], gates[32:36, :], par[32:36, bm:bm + 1], None, ALU.add).then_inc(gtD.sem, 1)
            V.tensor_scalar(i_pre[:, :], gates[0:4, :], par[0:4, bm:bm + 1], None, ALU.add).then_inc(gtD.sem, 1)
            wait(dve, gtD, "i")
            V.scalar_tensor_tensor(out=f_neg[:, :], in0=f_pre[:, :], scalar=-1.0, in1=f_pre[:, :], op0=ALU.mult,
                                   op1=ALU.min).then_inc(gtD.sem, 1)
            split("rec_in", 0, 3, KT)
            wait(dve, gtA, "ln")
            V.scalar_tensor_tensor(out=f_neg[:, :], in0=f_pre[:, :], scalar=0.0, in1=f_log[:, :], op0=ALU.min,
                                   op1=ALU.subtract).then_inc(gtD.sem, 1)
            wait(dve, gtD, "lf")
            V.tensor_tensor_scan(b_row[:, :], c_("reset_m")[0:4, :], f_neg[:, 0:T], 0.0, ALU.mult, ALU.add).then_inc(gtD.sem, 1)
            V.tensor_tensor_scan(m_run[:, :], f_neg[:, 0:T], i_pre[:, 0:T], 0.0, ALU.add, ALU.max).then_inc(gtD.sem, 1)
            V.tensor_tensor(r_s[:, 0:B], f_neg[:, T:NT], p_("m0")[0:4, :], ALU.add).then_inc(gtD.sem, 1)
            wait(dve, gtD, "lfm")
            V.tensor_tensor(m_out[:, 1:1 + B], r_s[:, 0:B], i_pre[:, T:NT], ALU.max).then_inc(gtD.sem, 1)
            V.tensor_tensor(r_intra[:, :], b_row[:, :], m_run[:, :], ALU.subtract).then_inc(gtD.sem, 1)
            V.tensor_tensor(a_row[:, :], i_pre[:, 0:T], b_row[:, :], ALU.subtract).then_inc(gtD.sem, 1)
            split("rec_in", 0, 4, KT)
            V.tensor_scalar(r_negm[:, :], m_run[:, :], -1.0, None, ALU.mult).then_inc(gtD.sem, 1)
            wait(dve, gtD, "nm")
            V.tensor_copy(r_inter[:, 0:P], r_intra[:, 0:P]).then_inc(gtD.sem, 1)
            for c in range(1, NC_M):
                t = slice(c * P, (c + 1) * P)
                V.tensor_scalar(r_inter[:, t], r_intra[:, t], m_run[:, c * P - 1:c * P], None, ALU.add).then_inc(gtD.sem, 1)
            V.tensor_tensor(r_s[:, 0:B], r_s[:, 0:B], m_out[:, 1:1 + B], ALU.subtract).then_inc(gtD.sem, 1)
            V.tensor_scalar(r_s[:, B:2 * B], m_out[:, 1:1 + B], -1.0, None, ALU.mult).then_inc(gtD.sem, 1)
            V.tensor_tensor(r_s[:, 2 * B:3 * B], i_pre[:, T:NT], m_out[:, 1:1 + B], ALU.subtract).then_inc(gtD.sem, 1)
            V.tensor_copy(m_out[:, 0:1], m_run[:, T - 1:T]).then_inc(gtD.sem, 1)
            split("rec_in", 0, 5, KT)
            split("rec_in", 0, 6, KT)

            K_SCALE = float(P) ** -0.5

            def rows(ap, n):
                return ap.unsqueeze(2).to_broadcast([P, ap.shape[1], n])

            def cols_(ap, n):
                return ap.unsqueeze(1).to_broadcast([P, n, ap.shape[1]])

            for h in range(M_HEADS):
                q, k, v, gate = z[:, h, :], z[:, 4 + h, :], z[:, 8 + h, :], z[:, 12 + h, :]

                def rec_split(j):
                    n = len(FIRST_SLABS) + PER_HEAD * h + j + 2
                    if n < S_REC_IN:
                        split("rec_in", 0, n, KT)
                    else:
                        split("rec_out", 0, n - S_REC_IN, KT)

                wait(dve, mP, "bc0", h)
                V.tensor_tensor(e_mat[:, :, :], ps[:, 0, :].rearrange("p (c t) -> p c t", c=NC_M),
                                cols_(c_("causal_T"), NC_M), ALU.add).then_inc(mD.sem, 1)
                wait(dve, mA, "wi", h)
                V.tensor_tensor(q_w[:, :], q[:, 0:T], w_int[:, :], ALU.mult).then_inc(mD.sem, 1)
                wait(dve, mA, "vt", h)
                for c in range(NC_M):
                    end = e_mat[:, c, P - 1:P]
                    V.tensor_scalar(v_end[:, c, 0, :], v_tok[:, c, :], end, K_SCALE, ALU.mult, ALU.mult)
                    ins = V.tensor_scalar(v_end[:, c, 1, :], ONES, end, K_SCALE, ALU.mult, ALU.mult)
                ins.then_inc(mD.sem, 1)
                wait(dve, mP, "scores", h)
                wait(dve, mD, "ve", h)
                flat = e_mat[:, :, :].rearrange("p c t -> p (c t)")
                V.scalar_tensor_tensor(out=flat, in0=ps[:, 7, :], scalar=K_SCALE, in1=flat, op0=ALU.mult,
                                       op1=ALU.mult).then_inc(mD.sem, 1)
                rec_split(0)
                rec_split(1)
                for c in range(NC_M):
                    wait(dve, mP, f"st{c}", h)
                    if c == 0:
                        if h:
                            dve.wait_ge(c_out, 16 * h)
                        V.tensor_copy(c_n[:, :], ps[:, 0, 0:2 * P]).then_inc(mD.sem, 1)
                    else:
                        wait(dve, mD, f"cn{c - 1}", h)
                        V.scalar_tensor_tensor(out=c_n[:, :], in0=c_n[:, :], scalar=w_int[:, (c + 1) * P - 1:(c + 1) * P],
                                               in1=ps[:, c % 2, 0:2 * P], op0=ALU.mult, op1=ALU.add).then_inc(mD.sem, 1)
                wait(dve, mD, "cn3", h)
                V.tensor_copy(n_end[:, h:h + 1], c_n[:, P:P + 1]).then_inc(mD.sem, 1)
                wait(dve, mA, "abs", h)
                V.tensor_tensor(den[:, :], den[:, :], e_negm[:, :], ALU.max).then_inc(mD.sem, 1)
                wait(dve, mD, "den", h)
                V.reciprocal(den[:, :], den[:, :]).then_inc(mD.sem, 1)
                rec_split(2)
                wait(dve, mD, "rden", h)
                V.tensor_tensor(h_head[:, 0:T], ps[:, 6, :], den[:, :], ALU.mult).then_inc(mD.sem, 1)
                V.scalar_tensor_tensor(out=v_ws[:, :], in0=v[:, T:NT], scalar=K_SCALE, in1=w_s[:, 2, :], op0=ALU.mult,
                                       op1=ALU.mult).then_inc(mD.sem, 1)
                V.scalar_tensor_tensor(out=k_ws[:, :], in0=k[:, T:NT], scalar=K_SCALE, in1=w_s[:, 2, :], op0=ALU.mult,
                                       op1=ALU.mult).then_inc(mD.sem, 1)
                V.tensor_tensor(nw[:, :], p_("n0", h * B, B), w_s[:, 0, :], ALU.mult).then_inc(mD.sem, 1)
                wait(dve, mD, "nw", h)
                V.tensor_tensor(n_s[:, h, :], nw[:, :], k_ws[:, :], ALU.add).then_inc(mD.sem, 1)
                wait(dve, mD, "ns", h)
                V.tensor_tensor(nq[:, :], n_s[:, h, :], q[:, T:NT], ALU.mult).then_inc(mD.sem, 1)
                wait(dve, mP, "kb", h)
                row4 = ps[:, 4:6, :].rearrange("p n (b k) -> p (n b) k", k=P)
                row0 = ps[:, 0:2, :].rearrange("p n (b k) -> p (n b) k", k=P)
                V.tensor_tensor(kv[:, :, :], row4, rows(v_ws[:, :], P), ALU.mult).then_inc(mD.sem, 1)
                wait(dve, mG, "cw", h)
                wait(dve, mD, "kv", h)
                V.tensor_tensor(c_s[:, :, :], c_s[:, :, :], kv[:, :, :], ALU.add).then_inc(mD.sem, 1)
                rec_split(3)
                wait(dve, mD, "cs", h)
                wait(dve, mP, "qb", h)
                V.tensor_tensor(kv[:, :, :], c_s[:, :, :], row0, ALU.mult).then_inc(mD.sem, 1)
                wait(dve, mD, "cq", h)
                V.tensor_reduce(hnum_s[:, :], kv[:, :, :], AX.X, ALU.add).then_inc(mD.sem, 1)
                wait(dve, mA, "abs_s", h)
                V.tensor_tensor(den_s[:, :], den_s[:, :], w_s[:, 1, :], ALU.max).then_inc(mD.sem, 1)
                wait(dve, mD, "dn", h)
                V.reciprocal(den_s[:, :], den_s[:, :]).then_inc(mD.sem, 1)
                wait(dve, mD, "rd", h)
                V.tensor_tensor(h_head[:, T:NT], hnum_s[:, :], den_s[:, :], ALU.mult).then_inc(mD.sem, 1)
                rec_split(4)
                wait(dve, mA, "rms", h)
                V.tensor_tensor(hn[:, 0, :], h_head[:, :], rstd[:, :], ALU.mult).then_inc(mD.sem, 1)
                wait(dve, mD, "t", h)
                V.scalar_tensor_tensor(out=gate, in0=hn[:, 0, :], scalar=p_("g_m"), in1=gate, op0=ALU.mult,
                                       op1=ALU.mult).then_inc(mD.sem, 1)
                rec_split(5)
            wait(dve, hA, "hi")
            V.tensor_tensor(h_lo[:, 0:4, :], z[:, 12:16, :], h_hi[:, 0:4, :].bitcast(F32), ALU.subtract).then_inc(hD.sem, 1)

            wait(dve, lP, "up")
            dve.wait_ge(drained, S_REC_IN)
            dve.wait_ge(c_out, 16 * M_HEADS)
            dve.wait_ge(cs_out, 16 * M_HEADS)
            for p in range(G_PAIRS):
                ins = V.tensor_scalar(two(log_a[:, p, :]), pair(2 * p), p_("b_gate", p, 1), None, ALU.add)
            ins.then_inc(lD.sem, 1)
            wait(dve, lD, "z")
            V.scalar_tensor_tensor(out=ln_t[:, :, :], in0=log_a[:, :, :], scalar=-1.0, in1=log_a[:, :, :], op0=ALU.mult,
                                   op1=ALU.min).then_inc(lD.sem, 1)
            wait(dve, lA, "ln")
            V.scalar_tensor_tensor(out=log_a[:, :, :], in0=log_a[:, :, :], scalar=0.0, in1=ln_t[:, :, :], op0=ALU.min,
                                   op1=ALU.subtract).then_inc(lD.sem, 1)
            wait(dve, lD, "lf")
            V.tensor_scalar(log_a[:, :, :], log_a[:, :, :], 1.0 / 16.0, None, ALU.mult).then_inc(lD.sem, 1)
            V.tensor_scalar(z[:, 16:18, :], z[:, 16:18, :], float(G_KEY) ** -0.5, None, ALU.mult).then_inc(lD.sem, 1)
            V.memset(sub0[:, :, :], 0.0).then_inc(lD.sem, 1)
            wait(dve, lD, "sub0")
            mask = c_("diag_mask")
            for p in range(G_PAIRS):
                q, k = z[:, 16 + p, :], z[:, 18 + p, :]
                q_t = q[:, 0:T].rearrange("p (c t) -> p c t", c=NC_G)
                k_t = k[:, 0:T].rearrange("p (c t) -> p c t", c=NC_G)
                bc_c = bc[:, :].rearrange("p (c t) -> p c t", c=NC_G)
                V.tensor_tensor_scan(bc[:, :], c_("reset_g"), log_a[:, p, 0:T], 0.0, ALU.mult, ALU.add).then_inc(gD.sem, 1)
                wait(dve, gD, "bc", p)
                V.tensor_copy(sub0[:, :, 1:4], bc[:, :].rearrange("p (c j t) -> p c j t", c=NC_G, j=4)[:, :, 0:3, SUB - 1])\
                    .then_inc(gD.sem, 1)
                wait(dve, gD, "sb", p)
                V.tensor_tensor(g_qs[:, :].rearrange("p (j t) -> p j t", t=SUB),
                                bc[:, :].rearrange("p (j t) -> p j t", t=SUB),
                                rows(sub0[:, :, :].rearrange("p c j -> p (c j)"), SUB), ALU.subtract).then_inc(gD.sem, 1)
                V.tensor_tensor(ke[:, :, :, :], sub0[:, :, 1:4].unsqueeze(3).to_broadcast([P, NC_G, 3, 48]),
                                bc_c[:, :, 0:48].unsqueeze(2).to_broadcast([P, NC_G, 3, 48]), ALU.subtract).then_inc(gD.sem, 1)
                wait(dve, gD, "ke", p)
                V.tensor_scalar(ke[:, :, :, :], ke[:, :, :, :], 0.0, None, ALU.min).then_inc(gD.sem, 1)
                V.tensor_tensor(g_kd[:, :].rearrange("p (c t) -> p c t", c=NC_G),
                                bc_c[:, :, LC_G - 1:LC_G].to_broadcast([P, NC_G, LC_G]), bc_c, ALU.subtract).then_inc(gD.sem, 1)
                for n in range(4):
                    def block_rows(ap):
                        return ap[:, n * P:(n + 1) * P].rearrange("p (b t) -> p b t", t=SUB).unsqueeze(2)\
                            .to_broadcast([P, 8, SUB, SUB])

                    def block_cols(ap):
                        return ap[:, n * P:(n + 1) * P].rearrange("p (b t) -> p b t", t=SUB).unsqueeze(3)\
                            .to_broadcast([P, 8, SUB, SUB])
                    if n:
                        wait(dve, gP, f"dg{n - 1}", p)
                    V.tensor_tensor(lx[:, :, :, :], block_rows(bc), block_cols(bc), ALU.subtract).then_inc(gD.sem, 1)
                    wait(dve, gD, f"x{n}", p)
                    flat = lx[:, :, :, :].rearrange("p b s t -> p b (s t)")
                    V.tensor_tensor(flat, flat, cols_(mask, 8), ALU.add).then_inc(gD.sem, 1)
                    wait(dve, gA, f"ex{n}", p)
                    V.tensor_tensor(lx[:, :, :, :], lx[:, :, :, :], block_cols(k), ALU.mult).then_inc(gD.sem, 1)
                    wait(dve, gD, f"xk{n}", p)
                    V.tensor_tensor(lx[:, :, :, :], lx[:, :, :, :], block_rows(q), ALU.mult).then_inc(gD.sem, 1)
                V.tensor_tensor(g_qs[:, :], g_qs[:, :], q[:, 0:T], ALU.mult).then_inc(gD.sem, 1)
                V.tensor_tensor(g_qd[:, :], g_qd[:, :], q[:, 0:T], ALU.mult).then_inc(gD.sem, 1)
                wait(dve, gA, "ke", p)
                V.tensor_tensor(ke[:, :, :, :], ke[:, :, :, :], k_t[:, :, 0:48].unsqueeze(2).to_broadcast([P, NC_G, 3, 48]),
                                ALU.mult).then_inc(gD.sem, 1)
                V.tensor_tensor(g_kd[:, :], g_kd[:, :], k[:, 0:T], ALU.mult).then_inc(gD.sem, 1)
                for c in range(NC_G):
                    wait(dve, gP, f"s{c}", p)
                    if c == 0:
                        if p:
                            dve.wait_ge(gs_out, 16)
                        V.tensor_copy(g_s[:, :], ps[:, 0, 0:P]).then_inc(gD.sem, 1)
                    else:
                        wait(dve, gD, f"c{c - 1}", p)
                        V.scalar_tensor_tensor(out=g_s[:, :], in0=g_s[:, :], scalar=a_end[:, c:c + 1],
                                               in1=ps[:, c % 2, 0:P], op0=ALU.mult, op1=ALU.add).then_inc(gD.sem, 1)
                wait(dve, gP, "vb", p)
                V.tensor_tensor(g_kv[:, :, :], ps[:, 2:4, :].rearrange("p n (b k) -> p (n b) k", k=P), rows(k[:, T:NT], P),
                                ALU.mult).then_inc(gD.sem, 1)
                wait(dve, gG, "sa", p)
                wait(dve, gD, "kv", p)
                V.tensor_tensor(g_ss[:, :, :], g_ss[:, :, :], g_kv[:, :, :], ALU.add).then_inc(gD.sem, 1)
                for hh in range(2):
                    wait(dve, gA, f"o{hh}", p)
                    V.tensor_tensor(g_h[:, hh, LC_G:T], g_h[:, hh, LC_G:T], ps[:, 4 + hh, LC_G:T], ALU.add)
                    V.tensor_copy(g_h[:, hh, 0:LC_G], ps[:, 4 + hh, 0:LC_G]).then_inc(gD.sem, 1)
                for hh in range(2):
                    wait(dve, gP, "os", p)
                    V.tensor_copy(g_h[:, hh, T:NT], ps[:, hh, 256:256 + B]).then_inc(gD.sem, 1)
                for hh in range(2):
                    wait(dve, gA, f"rms{hh}", p)
                    V.tensor_tensor(g_h[:, hh, :], g_h[:, hh, :], rstd[:, :], ALU.mult).then_inc(gD.sem, 1)
                    wait(dve, gD, f"t{hh}", p)
                    V.scalar_tensor_tensor(out=hn[:, hh, :], in0=g_h[:, hh, :], scalar=p_("g_g"), in1=z[:, 24 + 2 * p + hh, :],
                                           op0=ALU.mult, op1=ALU.mult).then_inc(gD.sem, 1)
                    wait(dve, gA, f"hi{hh}", p)
                    c = 4 + 2 * p + hh
                    V.tensor_tensor(h_lo[:, c, :], hn[:, hh, :], h_hi[:, c, :].bitcast(F32), ALU.subtract).then_inc(gD.sem, 1)

            walk(dve, "rec_out", split, out_drain("rec_out"))
            norm(1, "g_ffn0")
            ffn(0)
            walk(dve, "down0", split, down_drain("down0"))
            norm(2, "g_mix1")
            walk(dve, "att_q", split, nothing)

            V.tensor_tensor(lam[0:64, 0:2], p_("lam_q")[0:64, :], p_("lam_k")[0:64, :], ALU.mult).then_inc(lamD.sem, 1)
            wait(dve, lamA, "exp")
            V.tensor_tensor(lam[:, 0:1], lam[:, 2:3], lam[:, 3:4], ALU.subtract).then_inc(lamD.sem, 1)
            wait(dve, lamD, "sub")
            V.tensor_scalar(lam[:, 0:1], lam[:, 0:1], LAM_INIT, None, ALU.add).then_inc(lamD.sem, 1)
            V.memset(coef[:, 0:1], 1.0).then_inc(lamD.sem, 1)
            wait(dve, lamD, "lam")
            V.tensor_copy(coef[:, 1:2], lam[:, 0:1]).then_inc(lamD.sem, 1)
            V.tensor_scalar(g_o2[:, :], p_("g_out"), 1.0 - LAM_INIT, None, ALU.mult).then_inc(lamD.sem, 1)
            dve.wait_ge(catt_in, 16)

            def at_(t, h, w=slice(0, NT)):
                return t[:, h, w] if isinstance(h, int) else t[:, ds(h, 1), w].rearrange("p o t -> p (o t)")

            wait(dve, bA, "rqs")
            V.scalar_tensor_tensor(out=qs[:, :, :], in0=zq[:, :, T:NT], scalar=p_("g_q"), in1=qs_t[:, :, :], op0=ALU.mult,
                                   op1=ALU.mult).then_inc(bD.sem, 1)
            wait(dve, bA, "rq")
            V.scalar_tensor_tensor(out=qn[:, 0, :], in0=zq[:, 0, :], scalar=p_("g_q"), in1=rs3[:, 0, :], op0=ALU.mult,
                                   op1=ALU.mult).then_inc(bD.sem, 1)
            split("att_kv", 0, 2, KT)
            split("att_kv", 0, 3, KT)
            wait(dve, bA, "rk")
            V.scalar_tensor_tensor(out=kn[:, 0, :], in0=kraw[:, :], scalar=p_("g_k"), in1=rs3[:, 1, :], op0=ALU.mult,
                                   op1=ALU.mult).then_inc(bD.sem, 1)

            def head(h, u, i, h0, last=False):
                sP_, sA_, sD_, r = (zP, zA, zD, 0) if last else (aP, aA, aD, h)

                def stats(k):
                    wait(dve, sP_, f"s{k}", r)
                    s = ps[:, 2:4, :]
                    V.tensor_tensor(s[:, :, k * P:(k + 1) * P], s[:, :, k * P:(k + 1) * P], cols_(c_("causal"), 2),
                                    ALU.add).then_inc(sD_.sem, 1)
                    wait(dve, sD_, f"m{k}", r)
                    V.tensor_reduce(mx[:, k % 2, :], s[:, :, 0:(k + 1) * P], AX.X, ALU.max).then_inc(sD_.sem, 1)
                    wait(dve, sD_, f"x{k}", r)
                    V.tensor_scalar(mx[:, k % 2, :], mx[:, k % 2, :], -(A_QK ** -0.5), None, ALU.mult).then_inc(sD_.sem, 1)

                def combine(k):
                    b = k % 2
                    w = slice(0, (k + 1) * P)
                    wait(dve, sA_, f"ex{k}", r)
                    V.reciprocal(rs[:, b, :], sm[:, b, :]).then_inc(sD_.sem, 1)
                    wait(dve, sD_, f"r{k}", r)
                    V.tensor_tensor(rs[:, b, :], rs[:, b, :], coef[:, :], ALU.mult).then_inc(sD_.sem, 1)
                    wait(dve, sD_, f"rc{k}", r)
                    V.tensor_scalar(e_att[:, b, 1, w], e_att[:, b, 1, w], rs[:, b, 1:2], None, ALU.mult).then_inc(sD_.sem, 1)
                    wait(dve, sD_, f"e{k}", r)
                    if k >= 2:
                        wait(dve, sP_, f"t{k - 2}", r)
                    V.scalar_tensor_tensor(out=a_att[:, b, w], in0=e_att[:, b, 0, w], scalar=rs[:, b, 0:1],
                                           in1=e_att[:, b, 1, w], op0=ALU.mult, op1=ALU.subtract).then_inc(sD_.sem, 1)

                def page(j):
                    if j == 0:
                        wait(dve, sA_, "qb", r)
                    else:
                        wait(dve, sD_, f"red{j - 1}", r)
                    dve.wait_ge(k_in[j], 16 * h + 16)
                    V.tensor_tensor(s_prod[:, :], k_pages[:, j, :], qb[:, :], ALU.mult).then_inc(sD_.sem, 1)
                    wait(dve, sD_, f"mul{j}", r)
                    V.tensor_reduce(s_sc[:, j, :], s_prod[:, :].rearrange("p (h d) -> p h d", d=A_QK), AX.X,
                                    ALU.add).then_inc(sD_.sem, 1)

                stats(0)
                combine(0)
                stats(1)
                page(0)
                combine(1)
                stats(2)
                page(1)
                combine(2)
                if not last:
                    split("att_kv", i, 2 * (h0 + 2), KT)
                stats(3)
                page(2)
                combine(3)
                page(3)
                wait(dve, sP_, "st", r)
                V.tensor_reduce(s_m[0:16, :], ps[0:16, 6, :], AX.X, ALU.max).then_inc(sD_.sem, 1)
                wait(dve, sD_, "smax", r)
                V.tensor_scalar(s_dm[0:16, :], IDENT[0:16, 0:16], s_m[0:16, :], None, ALU.mult).then_inc(sD_.sem, 1)
                if not last:
                    wait(dve, sA_, "rq", r)
                    V.scalar_tensor_tensor(out=qn[:, 1 - u, :], in0=at_(zq, h + 1), scalar=p_("g_q"), in1=rs3[:, 0, :],
                                           op0=ALU.mult, op1=ALU.mult).then_inc(sD_.sem, 1)
                    split("att_kv", i, 2 * (h0 + 2) + 1, KT)
                    wait(dve, sA_, "rk", r)
                    if h0:
                        dve.wait_ge(kn_out, 16 * h)
                    V.scalar_tensor_tensor(out=kn[:, 1 - u, :], in0=kraw[:, :], scalar=p_("g_k"), in1=rs3[:, 1, :],
                                           op0=ALU.mult, op1=ALU.mult).then_inc(sD_.sem, 1)
                wait(dve, sP_, "mb", r)
                V.tensor_copy(at_(m_all, h, slice(0, 16)), ps[:, 7, 0:16]).then_inc(sD_.sem, 1)
                V.tensor_tensor(s_sc[:, :, :], s_sc[:, :, :], cols_(ps[:, 7, 0:16], PAGES), ALU.subtract).then_inc(sD_.sem, 1)
                wait(dve, sA_, "ro", r)
                V.scalar_tensor_tensor(out=at_(zq, h, slice(0, T)), in0=ps[:, 5, :], scalar=g_o2[:, :], in1=rs3[:, 2, 0:T],
                                       op0=ALU.mult, op1=ALU.mult).then_inc(sD_.sem, 1)
                wait(dve, sP_, "pv", r)
                V.tensor_reduce(at_(o_all, h, slice(0, 16)), ps[:, 7, 64:128].rearrange("p (j k) -> p k j", j=PAGES), AX.X,
                                ALU.add).then_inc(sD_.sem, 1)
                V.tensor_copy(at_(l_all, h, slice(0, 16)), ps[:, 7, 16:32]).then_inc(sD_.sem, 1)

            head(0, 0, 0, 0)
            with dve.Fori(0, (A_HEADS - 2) // 2) as i:
                for w in range(2):
                    head(2 * i + (1 + w), 1 - w, i, 1 + w)
            head(A_HEADS - 1, 1, 0, A_HEADS - 1, last=True)
            for n, (first_, end_) in enumerate(((0, 4), (4, 7), (7, 8))):
                wait(dve, eA, f"hi{n}")
                V.tensor_tensor(h_lo[:, first_:end_, 0:T], zq[:, first_:end_, 0:T], h_hi[:, first_:end_, 0:T].bitcast(F32),
                                ALU.subtract).then_inc(eD.sem, 1)

            V.memset(s_new[:, :], 0.0).then_inc(tD.sem, 1)
            wait(dve, aG, "vs", A_HEADS - 1)
            wait(dve, tD, "zero")
            for c in range(2):
                g = slice(64 * c, 64 * c + 64)
                V.tensor_tensor(s_new[g, :].rearrange("p (b h c) -> p b h c", b=B, c=2)[:, :, :, c],
                                qs[g, :, :].rearrange("p h b -> p b h"), ks[g, :, :].rearrange("p h b -> p b h"),
                                ALU.mult).then_inc(tD.sem, 1)
            m_, l_, o_ = (t[:, :, :].rearrange("p b k -> p (b k)") for t in (m_all, l_all, o_all))
            new, w_past, w_new, m_both, total, out = (t[:, :] for t in s_w)

            def halves(t, c):
                return t.rearrange("p (k c) -> p k c", c=2)[:, :, c]

            wait(dve, tP, "new")
            V.tensor_copy(new, ps[:, 0, 0:P]).then_inc(tD.sem, 1)
            wait(dve, tD, "newc")
            V.tensor_tensor(m_both, m_, new, ALU.max).then_inc(tD.sem, 1)
            wait(dve, tD, "mt")
            V.tensor_tensor(w_past, m_, m_both, ALU.subtract).then_inc(tD.sem, 1)
            V.tensor_tensor(w_new, new, m_both, ALU.subtract).then_inc(tD.sem, 1)
            wait(dve, tA, "ex")
            V.tensor_tensor(total, l_, w_past, ALU.mult).then_inc(tD.sem, 1)
            wait(dve, tD, "l1")
            V.tensor_tensor(total, total, w_new, ALU.add).then_inc(tD.sem, 1)
            wait(dve, tD, "l2")
            V.reciprocal(total, total).then_inc(tD.sem, 1)
            V.tensor_tensor(out, o_, w_past, ALU.mult).then_inc(tD.sem, 1)
            V.tensor_tensor(new.rearrange("p (b h c) -> p b h c", b=B, c=2), w_new.rearrange("p (b h c) -> p b h c", b=B, c=2),
                            vs[:, :, :].rearrange("p h b -> p b h").unsqueeze(3).to_broadcast([P, B, A_HEADS, 2]),
                            ALU.mult).then_inc(tD.sem, 1)
            wait(dve, tD, "v1")
            V.tensor_tensor(out, out, new, ALU.add).then_inc(tD.sem, 1)
            wait(dve, tD, "o2")
            V.tensor_tensor(out, out, total, ALU.mult).then_inc(tD.sem, 1)
            wait(dve, tD, "o3")
            V.tensor_scalar(s_o2[:, :], halves(out, 1), lam[:, 0:1], None, ALU.mult).then_inc(tD.sem, 1)
            wait(dve, tD, "c1")
            V.tensor_tensor(s_o[:, :], halves(out, 0), s_o2[:, :], ALU.subtract).then_inc(tD.sem, 1)
            wait(dve, tA, "rms")
            V.scalar_tensor_tensor(out=s_o2[:, :], in0=s_o[:, :], scalar=g_o2[:, :], in1=s_r2[:, 1, :], op0=ALU.mult,
                                   op1=ALU.mult).then_inc(tD.sem, 1)
            wait(dve, tA, "hi")
            V.tensor_tensor(h_lo[:, :, T:NT], s_o2[:, :].rearrange("p (b h) -> p h b", b=B), h_hi[:, :, T:NT].bitcast(F32),
                            ALU.subtract).then_inc(tD.sem, 1)

            walk(dve, "att_out", split, out_drain("att_out"))
            norm(3, "g_ffn1")
            ffn(1)
            walk(dve, "down1", split, down_drain("down1"))

        @block.gpsimd
        def _(pool):
            def times_rows(out, a_, row, n):
                return G.tensor_tensor(out, a_, row.unsqueeze(2).to_broadcast([P, B, n]), ALU.mult)

            def spread(out, row, n=B):
                return G.tensor_tensor(out, IDENT.unsqueeze(1).to_broadcast([P, n, P]),
                                       row.unsqueeze(2).to_broadcast([P, n, P]), ALU.mult)

            G.memset(one[:, :], 1.0).then_inc(small.sem, 1)
            G.memset(eps[:, :], EPS).then_inc(small.sem, 1)
            pool.wait_ge(par_in, 32)
            for layer in range(2):
                pool.dma_start(a["o_conv_s1"][layer], p_(f"conv_s{layer}").rearrange("p (m j b) -> p m j b", j=2, b=B)[:, :, 1, :])\
                    .then_inc(outs, 16)
            wait(pool, gtD, "mo0")
            pool.dma_start(a["o_m"], m_out[:, :]).then_inc(outs, 16)
            wait(pool, gtA, "acol")
            for h in range(M_HEADS):
                if h:
                    pool.wait_ge(cs_out, 16 * h)
                    wait(pool, mD, "cq", h - 1)
                pool.dma_start(c_s[:, :, :], a["state_c"][:, h]).then_inc(c_s_in, 16)
                wait(pool, mP, "bc0", h)
                if h:
                    wait(pool, mD, "hs", h - 1)
                spread(diag_k[:, :, :], z[:, 4 + h, T:NT]).then_inc(mG.sem, 1)
                wait(pool, mA, "ws", h)
                pool.wait_ge(c_s_in, 16 * (h + 1))
                times_rows(c_s[:, :, :], c_s[:, :, :], w_s[:, 0, :], P).then_inc(mG.sem, 1)
                wait(pool, mP, "st3", h)
                spread(diag_q[:, :, :], z[:, h, T:NT]).then_inc(mG.sem, 1)
                wait(pool, mD, "nend", h)
                pool.dma_start(a["o_c"][:, h], c_n[:, 0:P]).then_inc(c_out, 16)
                wait(pool, mD, "cs", h)
                pool.dma_start(a["o_cs"][:, h], c_s[:, :, :]).then_inc(cs_out, 16)
            pool.dma_start(a["o_n"], n_end[:, :]).then_inc(outs, 16)
            pool.dma_start(a["o_ns"], n_s[:, :, :]).then_inc(outs, 16)

            pool.wait_ge(mD.sem, mD.all(M_HEADS))
            pool.wait_ge(drained, S_REC_IN)
            for p in range(G_PAIRS):
                if p:
                    pool.wait_ge(gD.sem, gD.all(p))
                    G.memset(g_att[:, :, :, :], 0.0).then_inc(gG.sem, 1)
                else:
                    pool.wait_ge(c_out, 16 * M_HEADS)
                    pool.wait_ge(cs_out, 16 * M_HEADS)
                    G.memset(g_att[:, :, :, :], 0.0).then_inc(gG.sem, 1)
                wait(pool, gP, "dg3", p)
                pool.wait_ge(dg_out, 32 * (p + 1))
                if p:
                    pool.wait_ge(gss_out, 16)
                pool.dma_start(g_ss[:, :, :], a["state_s"][:, p]).then_inc(g_s_in, 16)
                for hh in range(2):
                    ins = spread(g_dv[:, hh, :, :], z[:, 20 + 2 * p + hh, T:NT])
                ins.then_inc(gG.sem, 1)
                wait(pool, gA, "as", p)
                pool.wait_ge(g_s_in, 16 * (p + 1))
                times_rows(g_ss[:, :, :], g_ss[:, :, :], a_s[:, :], P).then_inc(gG.sem, 1)
                wait(pool, gD, "c7", p)
                pool.dma_start(a["o_s"][:, p], g_s[:, :]).then_inc(gs_out, 16)
                wait(pool, gD, "ss", p)
                pool.dma_start(a["o_ss"][:, p], g_ss[:, :, :]).then_inc(gss_out, 16)

            pool.wait_ge(gs_out, 16 * G_PAIRS)
            pool.wait_ge(gss_out, 16 * G_PAIRS)
            pool.wait_ge(outs, 16 * 5)
            pool.wait_ge(slab_done, FIRST["ffn0"])
            G.memset(ub[:, :, 0:2], 0.0).then_inc(pads.sem, 1)
            pool.wait_ge(fD.sem, fD.all(FT))
            pool.dma_start(a["o_conv"][0], conv_end[:, :, :]).then_inc(conv_out, 16)

            pool.wait_ge(slab_done, FIRST["att_q"])
            pool.dma_start(catt[:, :], a["catt"]).then_inc(catt_in, 16)

            def head(h, u, first=False):
                if first:
                    wait(pool, bD, "qs")
                else:
                    wait(pool, aP, "qb", h - 1)
                row = qs[:, :, h] if isinstance(h, int) else qs[:, :, ds(h, 1)].rearrange("p h o -> p (h o)")
                spread(qd[:, :, :], row, A_HEADS).then_inc(aG.sem, 1)
                if first:
                    wait(pool, bD, "kn")
                else:
                    wait(pool, aD, "kn", h - 1)
                one_head = slice(h, h + 1) if isinstance(h, int) else ds(h, 1)
                G.tensor_copy(ks[:, one_head, :], kn[:, u:u + 1, T:NT]).then_inc(aG.sem, 1)
                pool.dma_start(a["o_k"][:, one_head, :], kn[:, u:u + 1, :]).then_inc(kn_out, 16)
                if first:
                    wait(pool, bA, "vr")
                else:
                    wait(pool, aA, "vr", h - 1)
                G.tensor_copy(vs[:, one_head, :], vn[:, T:NT].rearrange("p (o b) -> p o b", o=1)).then_inc(aG.sem, 1)
                pool.dma_start(a["o_v"][:, one_head, :], vn[:, :].rearrange("p (o t) -> p o t", o=1)).then_inc(vn_out, 16)

            head(0, 0, True)
            with pool.Fori(0, (A_HEADS - 2) // 2) as i:
                for w in range(2):
                    head(2 * i + (1 + w), 1 - w)
            head(A_HEADS - 1, 1)

            pool.wait_ge(slab_done, FIRST["ffn1"])
            pool.wait_ge(kn_out, 16 * A_HEADS)
            G.memset(ub[:, :, 0:2], 0.0).then_inc(pads.sem, 1)
            pool.wait_ge(fD.sem, fD.all(2 * FT))
            pool.dma_start(a["o_conv"][1], conv_end[:, :, :]).then_inc(conv_out, 16)
            for c in range(KT):
                pool.wait_ge(drained, FIRST["down1"] + 2 * (c + 1))
                pool.dma_start(a["o_y"][:, c, :], x[:, c, :]).then_inc(outs, 16)
            pool.wait_ge(outs, 16 * (5 + KT))
            pool.wait_ge(c_out, 16 * M_HEADS)
            pool.wait_ge(cs_out, 16 * M_HEADS)
            pool.wait_ge(gs_out, 16 * G_PAIRS)
            pool.wait_ge(gss_out, 16 * G_PAIRS)
            pool.wait_ge(conv_out, 32)
            pool.wait_ge(kn_out, 16 * A_HEADS)
            pool.wait_ge(vn_out, 16 * A_HEADS)
            pool.wait_ge(dg_out, 32 * G_PAIRS)


def slabs(w):
    k, n = w.shape
    return w.reshape(k // P, P, n // P, P).transpose(2, 1, 0, 3).reshape(n // P, P, k)


def down_slabs(w):
    s = slabs(w)
    return s.reshape(s.shape[0], P, 2, KD * P).transpose(0, 2, 1, 3).reshape(2 * s.shape[0], P, KD * P)


def feature_tiles(v):
    return v.reshape(-1, P).T


def rec_columns(w):
    last = np.zeros((w.shape[0], P), w.dtype)
    last[:, 0:4], last[:, 32:36], last[:, 64:80] = w[:, 2048:2052], w[:, 2052:2056], w[:, 3592:3608]
    return np.concatenate([w[:, 0:2048], w[:, 2056:3592], last], axis=1)


def constants():
    f = np.float32
    i = np.arange(P)
    before = (i[:, None] <= i[None, :])
    lo = i < 64
    causal_t = np.where(before, 0, NEG).astype(f)
    sel = np.zeros((P, M_HEADS, P), f)
    for h in range(M_HEADS):
        sel[h, h] = 1
    half_sum = np.zeros((P, 32), f)
    half_sum[lo, 0] = half_sum[~lo, 1] = 1
    s = np.arange(SUB)
    diag = np.where(s[:, None] <= s[None, :], 0, NEG).astype(f).reshape(1, -1)
    t = np.arange(T)
    cst = {"ident": np.eye(P), "ones": np.ones((P, P))}
    rec = {"causal_T": causal_t, "ones_lo": np.tile(lo, (P, 1)), "ones_hi": np.tile(~lo, (P, 1)),
           "sel_head": sel.reshape(P, -1), "half_sum": half_sum, "diag_mask": np.tile(diag, (P, 1)),
           "reset_m": np.tile(t % LC_M != 0, (P, 1)), "reset_g": np.tile(t % LC_G != 0, (P, 1))}
    att = {"causal": causal_t.T, "ones_half": lo[:, None] == lo[None, :]}
    return cst, rec, att


def packed(table, parts):
    return np.ascontiguousarray(np.concatenate([np.asarray(parts[n], np.float32) for n, _ in table], axis=1))


def kernel(**inputs):
    import concourse.bacc as bacc
    from concourse.bass_utils import run_bass_kernel_spmd

    v = {k: np.asarray(x) for k, x in inputs.items()}
    f = np.float32

    def column(values, rows=P, at=0):
        out = np.zeros((P, 1), f)
        out[at:at + len(values), 0] = values
        return out

    x_all = np.concatenate([v["x_prompt"][0], v["x_sample"][:, 0]], axis=0)
    tokens = x_all.T.reshape(KT, P, NT).transpose(1, 0, 2)
    cst, rec, att = constants()
    gate_up = np.zeros((P, G_PAIRS * P), f)
    gate_up[64:80] = v["rec_w_gate_up"][0]
    rec["w_gate_up"] = gate_up
    b_mgate = np.zeros((P, 1), f)
    b_mgate[0:4, 0], b_mgate[32:36, 0] = v["rec_b_mgate"][0, :4], v["rec_b_mgate"][0, 4:]
    pads_ = lambda u: np.concatenate([u, np.zeros((P - u.shape[0], u.shape[1]), f)], axis=0)
    twice = lambda u: np.concatenate([u, u])[:, None]
    par = {"g_mix0": feature_tiles(v["norm_mix_g"][0]), "g_mix1": feature_tiles(v["norm_mix_g"][1]),
           "g_ffn0": feature_tiles(v["norm_ffn_g"][0]), "g_ffn1": feature_tiles(v["norm_ffn_g"][1]),
           "b_gate": feature_tiles(v["rec_b_gate"][0]), "g_m": v["rec_m_norm_g"][0][:, None],
           "g_g": v["rec_g_norm_g"][0][:, None], "g_q": twice(v["att_q_norm_g"][0]), "g_k": twice(v["att_k_norm_g"][0]),
           "g_out": v["att_out_norm_g"][0][:, None], "b_mgate": b_mgate,
           "lam_q": pads_(np.stack([v["att_lambda_q1"][0], v["att_lambda_q2"][0]], 1)),
           "lam_k": pads_(np.stack([v["att_lambda_k1"][0], v["att_lambda_k2"][0]], 1)),
           "m0": pads_(v["state_mlstm_m"][0].T), "n0": v["state_mlstm_n"][0].transpose(2, 1, 0).reshape(P, M_HEADS * B)}
    for layer in range(2):
        par[f"conv_w{layer}"] = v["ffn_conv_w"][layer].reshape(3, FT, P).transpose(2, 0, 1).reshape(P, 3 * FT)
        par[f"conv_b{layer}"] = feature_tiles(v["ffn_conv_b"][layer])
        par[f"conv_s{layer}"] = v["state_ffn_conv"][layer].reshape(B, 2, FT, P).transpose(3, 2, 1, 0).reshape(P, -1)

    def ffn_slabs(layer):
        up, gate = slabs(v["ffn_w_up"][layer]), slabs(v["ffn_w_gate"][layer])
        return np.stack([up, gate], 1).reshape(S_FFN, P, D_MODEL)

    att_in = slabs(v["att_w_in"][0])
    att_kv = np.stack([att_in[A_HEADS:2 * A_HEADS], att_in[2 * A_HEADS:]], 1).reshape(2 * A_HEADS, P, D_MODEL)
    arrays = {
        "x": tokens, "cst": packed(CONSTS, cst), "crec": packed(CONSTS_REC, rec), "catt": packed(CONSTS_ATT, att),
        "par": packed(PARAMS, par),
        "w_rec_in": slabs(rec_columns(v["rec_w_in"][0]))[REC_TILES], "w_rec_out": slabs(v["rec_w_out"][0]),
        "w_att_q": att_in[:A_HEADS], "w_att_kv": np.concatenate([att_kv, slabs(v["att_w_out"][0])]),
        "w_ffn0": ffn_slabs(0), "w_ffn1": ffn_slabs(1),
        "w_down0": down_slabs(v["ffn_w_down"][0]), "w_down1": down_slabs(v["ffn_w_down"][1]),
        "state_c": v["state_mlstm_C"][0].transpose(2, 1, 0, 3),
        "state_s": v["state_gla_S"][0].reshape(B, G_PAIRS, P, P).transpose(2, 1, 0, 3),
        "cache_k": v["cache_k"][0].reshape(POOL, PAGE, D_MODEL), "cache_v": v["cache_v"][0].reshape(POOL, PAGE, D_MODEL),
        "page_table": v["page_table"].reshape(1, B * PAGES),
    }
    outs = {"o_y": (P, KT, NT), "o_m": (4, 1 + B), "o_c": (P, M_HEADS, P), "o_cs": (P, M_HEADS, B, P),
            "o_n": (P, M_HEADS), "o_ns": (P, M_HEADS, B), "o_s": (P, G_PAIRS, P), "o_ss": (P, G_PAIRS, B, P),
            "o_k": (P, A_HEADS, NT), "o_v": (P, A_HEADS, NT), "o_conv": (2, P, FT, 2 + B), "o_conv_s1": (2, P, FT, B)}
    nc = bacc.Bacc("TRN2", target_bir_lowering=False, num_devices=1)
    aps = {}
    arrays = {n: np.ascontiguousarray(t) for n, t in arrays.items()}
    for n, t in arrays.items():
        aps[n] = nc.dram_tensor(f"in_{n}", t.shape, mybir.dt.from_np(t.dtype), kind="ExternalInput").ap()
    for n, shape in outs.items():
        aps[n] = nc.dram_tensor(f"out_{n}", shape, mybir.dt.float32, kind="ExternalOutput").ap()
    aps["blocks"] = nc.dram_tensor("blocks", (G_PAIRS, 2, 16, 512), mybir.dt.float32, kind="Internal").ap()
    build(nc, aps)
    r = run_bass_kernel_spmd(nc, [{f"in_{n}": t for n, t in arrays.items()}], core_ids=[0]).results[0]
    o = {n: np.asarray(r[f"out_{n}"]) for n in outs}

    y = o["o_y"].transpose(2, 1, 0).reshape(NT, D_MODEL)
    k = o["o_k"].transpose(2, 1, 0)
    vv = o["o_v"].transpose(2, 1, 0)
    conv = o["o_conv"].transpose(0, 3, 2, 1).reshape(2, 2 + B, FFN)
    s1 = o["o_conv_s1"].transpose(0, 3, 2, 1).reshape(2, B, FFN)
    c = np.ascontiguousarray
    return (c(y[None, :T]), c(y[T:, None]),
            c(o["o_c"].transpose(1, 2, 0)[None, None]), c(o["o_cs"].transpose(2, 1, 0, 3)[None]),
            c(o["o_n"].T[None, None]), c(o["o_ns"].transpose(2, 1, 0)[None]),
            c(o["o_m"][:, 0][None, None]), c(o["o_m"][:, 1:].T[None]),
            c(o["o_s"].transpose(1, 0, 2).reshape(1, 1, 4, G_KEY, P)),
            c(o["o_ss"].transpose(2, 1, 0, 3).reshape(1, B, 4, G_KEY, P)),
            c(k[None, None, :T]), c(k[T:][None, :, None]), c(vv[None, None, :T]), c(vv[T:][None, :, None]),
            c(conv[:, None, 0:2]), c(np.stack([s1, conv[:, 2:]], axis=2)))
```

```python
import math
from contextlib import ExitStack

import concourse.bass as bass
import numpy as np
from concourse import mybir

P = 128
D_MODEL, T, B = 1024, 512, 8
NT = T + B
HALF = NT // 2
KT = D_MODEL // P
M_HEADS, G_PAIRS, A_HEADS, A_QK = 4, 2, 8, 64
G_KEY = 64
FFN = 2816
FT = FFN // P
KD = FT // 2
PAGE, PAGES, POOL = 128, 4, 40
EPS = 1e-6
LC_M = 128
NC_M = T // LC_M
LC_G = 64
NC_G = T // LC_G
SUB = 16
LAM_INIT = 0.8 - 0.6 * math.exp(-0.3)
NEG = -1e30

S_REC_IN = 29
S_OUT = 8
S_FFN = 2 * FT
S_DOWN = 16
RAW = 4
PHASES = [("rec_in", S_REC_IN, KT), ("rec_out", S_OUT, KT), ("ffn0", S_FFN, KT), ("down0", S_DOWN, KD),
          ("att_q", A_HEADS, KT), ("att_kv", 2 * A_HEADS, KT), ("att_out", S_OUT, KT), ("ffn1", S_FFN, KT), ("down1", S_DOWN, KD)]
FIRST_SLABS = [28, 0, 4, 8, 12]
HEAD_SLABS = [[13, 1, 5, 9, 24, 25], [14, 2, 6, 10, 26, 27], [15, 3, 7, 11, 16, 17], [18, 19, 20, 21, 22, 23]]
REC_TILES = FIRST_SLABS + sum(HEAD_SLABS, [])
PER_HEAD = len(HEAD_SLABS[0])
FIRST = {}
_n = 0
for _name, _s, _k in PHASES:
    FIRST[_name] = _n
    _n += _s
N_SLABS = _n

PARAMS = [("g_mix0", KT), ("g_ffn0", KT), ("g_mix1", KT), ("g_ffn1", KT),
          ("conv_w0", 3 * FT), ("conv_b0", FT), ("conv_w1", 3 * FT), ("conv_b1", FT),
          ("b_gate", G_PAIRS), ("g_m", 1), ("g_g", 1), ("g_q", 1), ("g_k", 1), ("g_out", 1),
          ("b_mgate", 1), ("lam_q", 2), ("lam_k", 2), ("m0", B), ("n0", M_HEADS * B),
          ("conv_s0", FT * 2 * B), ("conv_s1", FT * 2 * B)]
CONSTS = [("ident", P), ("ones", P)]
CONSTS_REC = [("causal_T", P), ("ones_lo", P), ("ones_hi", P), ("sel_head", M_HEADS * P), ("half_sum", 32),
              ("diag_mask", SUB * SUB), ("reset_m", T), ("reset_g", T), ("w_gate_up", G_PAIRS * P)]
CONSTS_ATT = [("causal", P), ("ones_half", P)]


def columns(table):
    at, out = 0, {}
    for name, n in table:
        out[name] = (at, at + n)
        at += n
    return out, at


class Steps:

    def __init__(self, sem, names):
        self.sem, self.names = sem, names.split()
        self.n = len(self.names)

    def at(self, name, r=0):
        return r * self.n + self.names.index(name) + 1

    def all(self, r):
        return r * self.n


def build(nc, a):
    F32, F32R, I32 = mybir.dt.float32, mybir.dt.float32r, mybir.dt.int32
    ALU, ACT, AX = mybir.AluOpType, mybir.ActivationFunctionType, mybir.AxisListType
    V, S, G, TE = nc.vector, nc.scalar, nc.gpsimd, nc.tensor
    ds = bass.ds
    ctx = ExitStack()
    with ctx:
        END = 229344

        def place(name, shape, dt=F32, at=None):
            size = 4 * int(np.prod(shape[1:]))
            size += -size % 32
            assert at[0] + size <= END, (name, at[0] + size)
            t = nc.alloc_sbuf_tensor_at(name, shape, dt, offset=at[0])
            at[0] += size
            return t

        def sem(name):
            return ctx.enter_context(nc.semaphore(name))

        hold = [16512]
        x = place("x", [P, KT, NT], at=hold)
        cst = place("cst", [P, columns(CONSTS)[1]], at=hold)
        par = place("par", [P, columns(PARAMS)[1]], at=hold)
        eps = place("eps", [P, 1], at=hold)
        one = place("one", [P, 1], at=hold)
        conv_end = place("conv_end", [P, FT, 2 + B], at=hold)
        raw = place("raw", [P, RAW, KD * P], at=hold)
        w_hi = place("w_hi", [P, 2, KD * P], F32R, at=hold)
        w_lo = place("w_lo", [P, 2, KD * P], F32R, at=hold)
        h_hi_at = hold[0]
        h_hi = place("h_hi", [P, KT, NT], F32R, at=hold)
        h_lo_at = hold[0]
        h_lo = place("h_lo", [P, KT, NT], F32R, at=hold)
        region = hold[0]
        norm_at = END - 5 * 4 * NT
        at = [norm_at]
        sq = place("sq", [P, 2, NT], at=at)
        rstd = place("rstd", [P, NT], at=at)
        hn = place("hn", [P, 2, NT], at=at)

        at = [region]
        z = place("z", [P, 28, NT], at=at)
        gates = place("gates", [P, NT], at=at)
        crec = place("crec", [P, columns(CONSTS_REC)[1]], at=at)
        r_intra = place("r_intra", [4, T], at=at)
        r_inter = place("r_inter", [4, T], at=at)
        r_negm = place("r_negm", [4, T], at=at)
        r_s = place("r_s", [4, 3 * B], at=at)
        m_out = place("m_out", [4, 1 + B], at=at)
        a_col = place("a_col", [P, NC_M, 4], at=at)
        n_end = place("n_end", [P, M_HEADS], at=at)
        n_s = place("n_s", [P, M_HEADS, B], at=at)
        work = at[0]
        at = [work]
        i_pre = place("i_pre", [4, NT], at=at)
        f_pre = place("f_pre", [4, NT], at=at)
        f_neg = place("f_neg", [4, NT], at=at)
        f_log = place("f_log", [4, NT], at=at)
        m_run = place("m_run", [4, T], at=at)
        b_row = place("b_row", [4, T], at=at)
        a_row = place("a_row", [4, T], at=at)
        at = [work]
        e_mat = place("e_mat", [P, NC_M, LC_M], at=at)
        w_int = place("w_int", [P, T], at=at)
        q_w = place("q_w", [P, T], at=at)
        k_tok = place("k_tok", [P, NC_M, P], at=at)
        v_tok = place("v_tok", [P, NC_M, P], at=at)
        v_end = place("v_end", [P, NC_M, 2, P], at=at)
        c_s = place("c_s", [P, B, P], at=at)
        kv = place("kv", [P, B, P], at=at)
        c_n = place("c_n", [P, 2 * P], at=at)
        w_s = place("w_s", [P, 3, B], at=at)
        nw = place("nw", [P, B], at=at)
        nq = place("nq", [P, B], at=at)
        v_ws = place("v_ws", [P, B], at=at)
        k_ws = place("k_ws", [P, B], at=at)
        den_s = place("den_s", [P, B], at=at)
        hnum_s = place("hnum_s", [P, B], at=at)
        assert at[0] <= norm_at, (at[0], norm_at)
        diag_q, diag_k = v_end[:, :, :, :].rearrange("p c a v -> p (c a) v"), kv
        h_head, den, e_negm = sq[:, 1, :], rstd[:, 0:T], hn[:, 0, 0:T]
        at = [region]
        lx = place("lx", [P, 8, SUB, SUB], at=at)
        dg = place("dg", [P, 4, 512], at=at)
        ke = place("ke", [P, NC_G, 3, 48], at=at)
        g_vt = place("g_vt", [64, 2, NC_G, P], at=at)
        g_s = place("g_s", [P, P], at=at)
        assert at[0] <= region + 16 * NT * 4, at[0] - region - 16 * NT * 4
        at = [work]
        log_a = place("log_a", [P, G_PAIRS, NT], at=at)
        bc = place("bc", [P, T], at=at)
        sub0 = place("sub0", [P, NC_G, 4], at=at)
        a_end = place("a_end", [P, NC_G], at=at)
        a_s = place("a_s", [P, B], at=at)
        g_qs = place("g_qs", [P, T], at=at)
        g_qd = place("g_qd", [P, T], at=at)
        g_kd = place("g_kd", [P, T], at=at)
        g_att = place("g_att", [64, 2, NC_G, LC_G], at=at)
        g_kdt = place("g_kdt", [64, NC_G, P], at=at)
        g_h = place("g_h", [P, 2, NT], at=at)
        assert at[0] <= norm_at, (at[0], norm_at)
        ln_t = g_h
        at = [region]
        g_dv = place("g_dv", [P, 2, B, P], at=at)
        g_ss = place("g_ss", [P, B, P], at=at)
        g_kv = place("g_kv", [P, B, P], at=at)

        at = [region]
        a_hi = place("a_hi", [P, FT, NT], F32R, at=at)
        a_lo = place("a_lo", [P, FT, NT], F32R, at=at)
        ub = place("ub", [P, 2, 2 + NT], at=at)
        cc = place("cc", [P, NT], at=at)
        ge = place("ge", [P, NT], at=at)
        pr = place("pr", [P, NT], at=[norm_at])
        ssum = ge[:, :]
        assert at[0] <= norm_at, (at[0], norm_at)

        at = [region]
        k_pages = place("k_pages", [P, PAGES, D_MODEL], at=at)
        v_pages = place("v_pages", [P, PAGES, D_MODEL], at=at)
        zq = place("zq", [P, A_HEADS, NT], at=at)
        catt = place("catt", [P, columns(CONSTS_ATT)[1]], at=at)
        ptab = place("ptab", [1, B * PAGES], I32, at=at)
        lam = place("lam", [P, 4], at=at)
        coef = place("coef", [P, 2], at=at)
        g_o2 = place("g_o2", [P, 1], at=at)
        qs = place("qs", [P, A_HEADS, B], at=at)
        ks = place("ks", [P, A_HEADS, B], at=at)
        vs = place("vs", [P, A_HEADS, B], at=at)
        qs_r = place("qs_r", [P, A_HEADS, B], at=at)
        qs_t = place("qs_t", [P, A_HEADS, B], at=at)
        qn = place("qn", [P, 2, NT], at=at)
        kn = place("kn", [P, 2, NT], at=at)
        v_t2 = place("v_t2", [P, 2, 4, P], at=at)
        e_att = place("e_att", [P, 2, 2, T], at=at)
        kraw = place("kraw", [P, NT], at=at)
        a_att = place("a_att", [P, 2, T], at=at)
        mx = place("mx", [P, 2, 2], at=at)
        sm = place("sm", [P, 2, 2], at=at)
        rs = place("rs", [P, 2, 2], at=at)
        s_sc = place("s_sc", [P, PAGES, 16], at=at)
        s_m = place("s_m", [P, 1], at=at)
        s_dm = place("s_dm", [P, 16], at=at)
        m_all = place("m_all", [P, B, 16], at=at)
        l_all = place("l_all", [P, B, 16], at=at)
        s_sum = place("s_sum", [P, 16], at=at)
        vn = place("vn", [P, NT], at=at)
        at_t = place("at_t", [P, 2, T], at=at)
        sq3 = place("sq3", [P, 3, NT], at=at)
        rs3 = place("rs3", [P, 3, NT], at=at)
        s_prod = place("s_prod", [P, D_MODEL], at=at)
        o_row = s_prod[0:16, :]
        qb = place("qb", [P, D_MODEL], at=at)
        qd = place("qd", [P, A_HEADS, P], at=at)
        at = [region]
        s_new = place("s_new", [P, P], at=at)
        s_w = [place(f"s_w{i}", [P, P], at=at) for i in range(6)]
        o_rows = place("o_rows", [P, P], at=at)
        s_o = place("s_o", [P, 64], at=at)
        s_o2 = place("s_o2", [P, 64], at=at)
        s_r2 = place("s_r2", [P, 2, 64], at=at)

        ps = ctx.enter_context(nc.psum_tensor("ps", [P, 8, 512], F32))

        def p_(name, k=0, n=None):
            lo, hi = columns(PARAMS)[0][name]
            return par[:, lo + k:(hi if n is None else lo + k + n)]

        def c_(name):
            for table, t in ((CONSTS, cst), (CONSTS_REC, crec), (CONSTS_ATT, catt)):
                cols = columns(table)[0]
                if name in cols:
                    return t[:, cols[name][0]:cols[name][1]]

        def half(bank, h):
            return ps[:, bank + h, 0:HALF]

        def pair(bank):
            return ps[:, bank:bank + 2, 0:HALF]

        def two(ap):
            return ap.rearrange("p (a t) -> p a t", a=2)

        IDENT, ONES = c_("ident"), c_("ones")

        landed = [sem(f"landed{i}") for i in range(RAW)]
        hi_split, lo_split = sem("hi_split"), sem("lo_split")
        slab_done = sem("slab_done")
        drained = sem("drained")
        x_in, par_in = [sem("x_in0"), sem("x_in1")], sem("par_in")
        crec_in, catt_in, ptab_in = sem("crec_in"), sem("catt_in"), sem("ptab_in")
        small_set = sem("small_set")
        outs = sem("outs")
        c_s_in, g_s_in = sem("c_s_in"), sem("g_s_in")
        c_out, cs_out, gs_out, gss_out = sem("c_out"), sem("cs_out"), sem("gs_out"), sem("gss_out")
        conv_out = sem("conv_out")
        dg_out, diag_in = sem("dg_out"), sem("diag_in")
        kn_out = sem("kn_out")
        k_in = [sem(f"k_in{i}") for i in range(PAGES)]
        v_in = [sem(f"v_in{i}") for i in range(PAGES)]
        vn_out = sem("vn_out")

        squared, summed = sem("squared"), sem("summed")
        nA = Steps(sem("norm_act"), "lr rms hi0 hi1 hi2 hi3 hi4 hi5 hi6 hi7")
        nD = Steps(sem("norm_dve"), "n0 n1 lo0 n2 lo1 n3 lo2 n4 lo3 n5 lo4 n6 lo5 n7 lo6 lo7")
        nP = Steps(sem("norm_pe"), "sum")
        gtD = Steps(sem("gate_dve"), "f i neg lf b m lfm ms ri a nm r20 r21 r22 r23 s0 s1 s2 mo0")
        gtA = Steps(sem("gate_act"), "exp ln acol")
        gtP = Steps(sem("gate_pe"), "acol")
        mP = Steps(sem("mlstm_pe"), "bc0 bc1 bc2 bcs scores vtr ktr num0 st0 num1 st1 num2 st2 num3 st3 kb qb dens ssq")
        mA = Steps(sem("mlstm_act"), "ws wi en e kt vt gate abs abs_s sq lr rms")
        mD = Steps(sem("mlstm_dve"), "em qw ve p cn0 cn1 cn2 cn3 nend den rden h vw kw nw ns nq kv cs cq hs dn rd hs2 t mix")
        hA, hD = Steps(sem("mlstm_out_act"), "hi"), Steps(sem("mlstm_out_dve"), "lo")
        mG = Steps(sem("mlstm_pool"), "dk cw dq")
        lP = Steps(sem("decay_pe"), "up")
        lA = Steps(sem("decay_act"), "exp ln")
        lD = Steps(sem("decay_dve"), "z neg lf la q8 sub0")
        fA = Steps(sem("ffn_act"), "u tail gelu hi")
        fD = Steps(sem("ffn_dve"), "t0 t1 s1 t2 s0 prod lo")
        dA = Steps(sem("gla_decay_act"), "eb qe aend ke kend")
        dD = Steps(sem("gla_decay_dve"), "bc sb qe ke kem kend qs ks qd kd")
        xD = Steps(sem("gla_diff_dve"), "x0 xm0 x1 xm1")
        gP = Steps(sem("gla_pe"), "vt kdt dg0 s0 " + " ".join(f"dg{c} o{c} s{c}" for c in range(1, NC_G - 1))
                   + " dg7 off o7 s7 vb oi os ssq0 ssq1")
        gA = Steps(sem("gla_act"), "vt ex0 ex1 kdt as ex2 dgc0 ex3 ex4 dgc1 ex5 ex6 dgc2 ex7 dgc3 at "
                   "sq0 sq1 lr0 rms0 lr1 rms1 hi0 hi1")
        gD = Steps(sem("gla_dve"), " ".join(
            f"xk{i} xq{i} xk{i + 1} xq{i + 1} c{i} " + (f"x{i + 2} xm{i + 2} c{i + 1} x{i + 3} xm{i + 3}" if i + 2 < NC_G
                                                        else f"c{i + 1}") for i in range(0, NC_G, 2))
                   + " kv ss tp0 t0 mix0 tp1 t1 mix1 lo0 lo1")
        gG = Steps(sem("gla_pool"), "za dv sa")
        small = Steps(sem("small"), "one eps")
        pads = Steps(sem("pads"), "pad")
        NEXT = "sqq lrq rq kr sqk vr lrk rk vt ssq ssk vtr qn kn"
        def both(engine, names):
            last = " ".join(n for n in names.split() if n not in NEXT.split())
            return Steps(sem("att_" + engine), names), Steps(sem("last_" + engine), last)
        aP, zP = both("pe", "s0 qb s1 ssq t0 v0 s2 t1 v1 s3 t2 v2 t3 v3 st ssk sso mb vtr pv sum")
        aA, zA = both("act", "sqq ex0 qb ex1 lrq rq att0 ex2 att1 kr sqk ex3 att2 att3 sqo vr lrk rk lro ro se vt orow")
        aD, zD = both("dve", "m0 x0 nx0 r0 rc0 e0 a0 m1 x1 nx1 mul0 red0 r1 rc1 e1 a1 m2 x2 nx2 mul1 red1 r2 rc2 e2 a2 "
                      "m3 x3 nx3 mul2 red2 r3 rc3 e3 a3 mul3 red3 smax dmx qn kn msv sub ls mix lall")
        aG = Steps(sem("att_pool"), "qd ks vs")
        bP = Steps(sem("first_pe"), "sqs ssq ssk vtr")
        bA = Steps(sem("first_act"), "sqs lrs rqs sqq lrq rq kr sqk vr lrk rk vt")
        bD = Steps(sem("first_dve"), "qs qn kn")
        lamP = Steps(sem("lam_pe"), "sum")
        lamA = Steps(sem("lam_act"), "exp")
        lamD = Steps(sem("lam_dve"), "prod sub lam c0 c1 go")
        tP = Steps(sem("soft_pe"), "new turn ssq")
        tA = Steps(sem("soft_act"), "ex sq lr rms hi")
        tD = Steps(sem("soft_dve"), "zero new0 new1 newc mt d1 d2 l1 l2 r v1 o1 o2 o3 c1 a mix lo")
        past_out, past_in = sem("past_out"), sem("past_in")
        eA = Steps(sem("heads_act"), "hi0 hi1 hi2")
        eD = Steps(sem("heads_dve"), "lo0 lo1 lo2")

        block = ctx.enter_context(nc.Block())

        def wait(eng, steps, name, r=0):
            eng.wait_ge(steps.sem, steps.at(name, r))

        def is_a_wait(v):
            return not isinstance(v, int) or v > 0

        @block.sync
        def _(sp):
            def load_slab(name, nk, i, s):
                f = FIRST[name]
                before = 4 * i + (f + s - RAW + 1)
                if is_a_wait(before):
                    sp.wait_ge(lo_split, before)
                slot = (f + s) % RAW
                sp.dma_start(raw[:, slot, 0:nk * P], a["w_" + name][4 * i + s]).then_inc(landed[slot], 16)

            def load_phase(name, groups):
                nk = dict((n, k) for n, _, k in PHASES)[name]
                first, end = groups
                if end - first <= 1:
                    for i in range(first, end):
                        for s in range(4):
                            load_slab(name, nk, i, s)
                else:
                    with sp.Fori(first, end) as i:
                        for s in range(4):
                            load_slab(name, nk, i, s)

            for n in range(2):
                sp.dma_start(x[:, 4 * n:4 * n + 4, :], a["x"][:, 4 * n:4 * n + 4, :]).then_inc(x_in[n], 16)
            load_phase("rec_in", (0, 1))
            sp.dma_start(crec[:, :], a["crec"]).then_inc(crec_in, 16)
            load_phase("rec_in", (1, 7))
            load_slab("rec_in", KT, 7, 0)
            load_phase("rec_out", (0, 1))
            for p in range(G_PAIRS):
                wait(sp, gA, "dgc3", p)
                wait(sp, gG, "za", p)
                for hh in range(2):
                    sp.dma_start(a["blocks"][p, hh].rearrange("(q m) x -> m q x", m=4),
                                 dg[hh::32, :, :]).then_inc(dg_out, 16)
                sp.wait_ge(dg_out, 32 * (p + 1))
                for j in range(4):
                    t = slice(SUB * j, SUB * (j + 1))
                    src = a["blocks"][p].rearrange("h (c j) (u s t) -> j u s h c t", c=NC_G, u=2, t=SUB)[j // 2, j % 2]
                    for hh in range(2):
                        sp.dma_start(g_att[t, hh, :, t], src[:, hh]).then_inc(diag_in, 16)
            load_phase("rec_out", (1, 2))
            load_phase("ffn0", (0, S_FFN // 4))
            load_phase("down0", (0, S_DOWN // 4))
            load_phase("att_q", (0, 1))
            sp.wait_ge(slab_done, FIRST["att_q"])
            sp.dma_start(ptab[:, :], a["page_table"]).then_inc(ptab_in, 16)
            sp.wait_ge(ptab_in, 16)

            def load_page(cache, buf, landed_, b, j, free=None):
                page = sp.value_load(ptab[0:1, ds(PAGES * b + j, 1)], min_val=0, max_val=POOL - 1)
                if free is not None:
                    wait(sp, *free)
                sp.dma_start(buf[:, j, :], a[cache][page]).then_inc(landed_[j], 16)

            for j in range(PAGES):
                load_page("cache_k", k_pages, k_in, 0, j)
            load_phase("att_q", (1, 2))
            for j in range(PAGES):
                load_page("cache_v", v_pages, v_in, 0, j)
            load_phase("att_kv", (0, 2))

            def sample_pages(h, slabs_):
                for j in range(PAGES):
                    load_page("cache_k", k_pages, k_in, h + 1, j, (aD, f"mul{j}", h))
                    if j in (1, 3):
                        slabs_(j // 2)
                for j in range(PAGES):
                    load_page("cache_v", v_pages, v_in, h + 1, j, (aP, "pv", h))

            sample_pages(0, lambda u: load_slab("att_kv", KT, 0, 8 + u))
            with sp.Fori(0, (A_HEADS - 2) // 2) as i:
                for w in range(2):
                    sample_pages(2 * i + (1 + w), lambda u: load_slab("att_kv", KT, i, 10 + 2 * w + u))
            load_slab("att_kv", KT, 0, 22)
            load_slab("att_kv", KT, 0, 23)
            load_phase("ffn1", (0, S_FFN // 4))
            load_phase("down1", (0, S_DOWN // 4))

        @block.tensor
        def _(pe):
            def multiply(name, hi, lo, i, s, bank, k_at, ks, first, last, ready=None):
                f = FIRST[name]
                buf = (f + s) % 2
                pe.wait_ge(lo_split, 4 * i + (f + s + 1))
                free = 4 * i + (f + s - 3)
                if is_a_wait(free):
                    pe.wait_ge(drained, free)
                for k in range(ks):
                    if ready is not None:
                        wait(pe, nD, f"lo{k}", ready)
                    w = slice(k * P, (k + 1) * P)
                    for w_part, parts in ((w_hi, (hi, lo)), (w_lo, (hi,))):
                        for m_part in parts:
                            for h in range(2):
                                start = first and k == 0 and w_part is w_hi and m_part is hi
                                stop = last and k == ks - 1 and w_part is w_lo
                                ins = TE.matmul(half(bank, h), w_part[:, buf, w],
                                                m_part[:, k_at + k, h * HALF:(h + 1) * HALF],
                                                start=start, stop=stop)
                ins.then_inc(slab_done, 1)

            def project(name, n, norm=None):
                def group(i, slabs=4):
                    for s in range(slabs):
                        multiply(name, h_hi, h_lo, i, s, 2 * s, 0, KT, True, True,
                                 norm if s == 0 else None)
                groups = n // 4
                group(0)
                if groups > 2:
                    with pe.Fori(1, groups) as i:
                        group(i)
                elif groups == 2:
                    group(1)
                if n % 4:
                    group(groups, n % 4)

            def down(name):
                with pe.Fori(0, S_DOWN // 4) as i:
                    for s in range(4):
                        multiply(name, a_hi, a_lo, i, s, 4 * (s // 2), KD * (s % 2), KD, s % 2 == 0, s % 2 == 1)

            def slab_part(n, buf, ks, bank):
                if ks[0] == 0:
                    pe.wait_ge(lo_split, n + 1)
                for k in ks:
                    w = slice(k * P, (k + 1) * P)
                    for w_part, parts in ((w_hi, (h_hi, h_lo)), (w_lo, (h_hi,))):
                        for m_part in parts:
                            for g in range(2):
                                ins = TE.matmul(half(bank, g), w_part[:, buf, w], m_part[:, k, g * HALF:(g + 1) * HALF],
                                                start=k == 0 and w_part is w_hi and m_part is h_hi,
                                                stop=k == KT - 1 and w_part is w_lo)
                if KT - 1 in ks:
                    ins.then_inc(slab_done, 1)

            def norm(r, bank, after=None):
                if after is not None:
                    pe.wait_ge(drained, after)
                pe.wait_ge(summed, (KT - 1) * (r + 1))
                for h in range(2):
                    TE.matmul(half(bank, h), ONES, ssum[:, h * HALF:(h + 1) * HALF], start=True, stop=False)
                pe.wait_ge(squared, KT * (r + 1))
                for h in range(2):
                    ins = TE.matmul(half(bank, h), ONES, sq[:, (KT - 1) % 2, h * HALF:(h + 1) * HALF], start=False, stop=True)
                ins.then_inc(nP.sem, 1)

            pe.wait_ge(par_in, 32)
            norm(0, 6)
            for n in range(len(FIRST_SLABS)):
                multiply("rec_in", h_hi, h_lo, 0, n, 2 * (n % 4), 0, KT, True, True, 0 if n == 0 else None)

            pe.wait_ge(drained, 4)
            wait(pe, gtD, "a")
            for c in range(NC_M):
                ins = TE.transpose(ps[:, 7, 4 * c:4 * c + 4], a_row[0:4, c * P:(c + 1) * P], IDENT[0:4, 0:4])
            ins.then_inc(gtP.sem, 1)

            SEL = c_("sel_head").rearrange("p (h m) -> p h m", h=M_HEADS)
            for h in range(M_HEADS):
                q, k, v = z[:, h, :], z[:, 4 + h, :], z[:, 8 + h, :]
                first = len(FIRST_SLABS) + PER_HEAD * h

                def part(j, k0=0, k1=KT):
                    n = first + j
                    if k0 == 0:
                        pe.wait_ge(drained, n)
                    slab_part(n, n % 2, range(k0, k1), 2)

                if h == 0:
                    pe.wait_ge(drained, len(FIRST_SLABS))
                    wait(pe, gtD, "mo0")
                    wait(pe, gtA, "acol")
                else:
                    wait(pe, mD, "cq", h - 1)
                    wait(pe, mA, "rms", h - 1)
                for bank, row in ((0, r_intra), (1, r_inter), (6, r_negm)):
                    TE.matmul(ps[:, bank, :], SEL[0:4, h, :], row[:, :], start=True, stop=True).then_inc(mP.sem, 1)
                TE.matmul(ps[:, 4, 0:3 * B], SEL[0:4, h, :], r_s[:, :], start=True, stop=True).then_inc(mP.sem, 1)
                for c in range(NC_M):
                    t = slice(c * P, (c + 1) * P)
                    ins = TE.matmul(ps[:, 7, t], k[:, t], q[:, t], start=True, stop=True)
                ins.then_inc(mP.sem, 1)
                for bank, rows in ((5, v), (4, k)):
                    if bank == 4:
                        wait(pe, mA, "ws", h)
                    for c in range(NC_M):
                        ins = TE.transpose(ps[:, bank, c * P:(c + 1) * P], rows[:, c * P:(c + 1) * P], IDENT)
                    ins.then_inc(mP.sem, 1)
                part(0)
                part(1)
                wait(pe, mD, "p", h)
                wait(pe, mA, "en", h)
                for c in range(NC_M):
                    t = slice(c * P, (c + 1) * P)
                    if c:
                        wait(pe, mD, f"cn{c - 1}", h)
                    TE.matmul(ps[:, 6, t], v_tok[:, c, :], e_mat[:, c, :], start=True, stop=c == 0)
                    ins = TE.matmul(ps[:, 7, t], ONES, e_mat[:, c, :], start=True, stop=c == 0) if c == 0 else None
                    if c:
                        TE.matmul(ps[:, 6, t], c_n[:, 0:P], q_w[:, t], start=False, stop=True)
                        TE.matmul(ps[:, 7, t], ONES, e_mat[:, c, :], start=True, stop=False)
                        ins = TE.matmul(ps[:, 7, t], c_n[:, P:2 * P], q_w[:, t], start=False, stop=True)
                    ins.then_inc(mP.sem, 1)
                    TE.matmul(ps[:, c % 2, 0:2 * P], k_tok[:, c, :], v_end[:, c, :, :].rearrange("p a v -> p (a v)"),
                              start=True, stop=True).then_inc(mP.sem, 1)
                    part(2, 2 * c, 2 * c + 2)
                wait(pe, mG, "dk", h)
                for n in range(2):
                    ins = TE.matmul(ps[:, 4 + n, :], ONES, diag_k[:, 4 * n:4 * n + 4, :].rearrange("p b k -> p (b k)"),
                                    start=True, stop=True)
                ins.then_inc(mP.sem, 1)
                part(3)
                wait(pe, mG, "dq", h)
                wait(pe, mD, "cn3", h)
                for n in range(2):
                    ins = TE.matmul(ps[:, n, :], ONES, diag_q[:, 4 * n:4 * n + 4, :].rearrange("p b k -> p (b k)"),
                                    start=True, stop=True)
                ins.then_inc(mP.sem, 1)
                wait(pe, mD, "nq", h)
                TE.matmul(ps[:, 6, 0:B], ONES, nq[:, :], start=True, stop=True).then_inc(mP.sem, 1)
                part(4)
                wait(pe, mA, "sq", h)
                wait(pe, mD, "kv", h)
                for n in range(2):
                    ins = TE.matmul(half(4, n), ONES, sq[:, 0, n * HALF:(n + 1) * HALF], start=True, stop=True)
                ins.then_inc(mP.sem, 1)
                if h < M_HEADS - 1:
                    part(5)

            for p in range(G_PAIRS):
                for n in range(2):
                    ins = TE.matmul(half(6 * p, n), c_("w_gate_up")[64:80, p * P:(p + 1) * P],
                                    gates[64:80, n * HALF:(n + 1) * HALF], start=True, stop=True)
            ins.then_inc(lP.sem, 1)
            part(PER_HEAD - 1)
            pe.wait_ge(drained, S_REC_IN)
            wait(pe, lD, "z")
            for p in range(G_PAIRS):
                if p:
                    wait(pe, gD, "t1", p - 1)
                for hh in range(2):
                    for c in range(NC_G):
                        bank = (6, 0)[hh] + c // 4
                        ins = TE.transpose(ps[0:64, bank, (c % 4) * P:(c % 4 + 1) * P],
                                           z[:, 20 + 2 * p + hh, c * LC_G:(c + 1) * LC_G], IDENT)
                ins.then_inc(gP.sem, 1)
                wait(pe, dD, "kd", p)
                if p:
                    wait(pe, gA, "rms1", p - 1)
                for c in range(NC_G):
                    ins = TE.transpose(ps[0:64, 2 + c // 4, (c % 4) * P:(c % 4 + 1) * P],
                                       g_kd[:, c * LC_G:(c + 1) * LC_G], IDENT)
                ins.then_inc(gP.sem, 1)
                wait(pe, gA, "vt", p)
                wait(pe, gA, "kdt", p)
                for c in range(NC_G):
                    wait(pe, gD, f"xq{c}", p)
                    if c in (4, 6):
                        wait(pe, gA, f"dgc{c // 2 - 2}", p)
                    flat = lx[:, 4 * (c % 2):4 * (c % 2) + 4, :, :].rearrange("p b s t -> p (b s t)")
                    for m in range(2):
                        row = 32 * (2 * (c % 2) + m)
                        ins = TE.matmul(ps[row:row + 32, 2 + c // 2 % 2, :], c_("half_sum"), flat[:, 512 * m:512 * m + 512],
                                        start=True, stop=True)
                    ins.then_inc(gP.sem, 1)
                    for hh in range(2):
                        r = slice(64 * hh, 64 * hh + 64)
                        for j in range(1, 4):
                            at_ = c * LC_G + j * SUB
                            ins = TE.matmul(ps[0:SUB * j, 4 + hh, at_:at_ + SUB], ke[r, c, j - 1, 0:SUB * j],
                                            g_qs[r, at_:at_ + SUB], start=True, stop=True)
                    if c == NC_G - 1:
                        ins.then_inc(gP.sem, 1)
                    t = slice(c * LC_G, (c + 1) * LC_G)
                    if c:
                        wait(pe, gD, f"c{c - 1}", p)
                        for hh in range(2):
                            r = slice(64 * hh, 64 * hh + 64)
                            ins = TE.matmul(ps[:, 6 + hh, t], g_s[r, :], g_qd[r, t], start=c == 1, stop=False)
                        ins.then_inc(gP.sem, 1)
                    for hh in range(2):
                        r = slice(64 * hh, 64 * hh + 64)
                        ins = TE.matmul(ps[r, c % 2, 0:P], g_kdt[:, c, r], g_vt[:, hh, c, :], start=True, stop=True)
                    ins.then_inc(gP.sem, 1)
                wait(pe, gG, "dv", p)
                wait(pe, gA, "dgc3", p)
                for n in range(2):
                    for hh, half_ones in ((0, c_("ones_lo")), (1, c_("ones_hi"))):
                        ins = TE.matmul(ps[:, 2 + n, :], half_ones,
                                        g_dv[:, hh, 4 * n:4 * n + 4, :].rearrange("p b v -> p (b v)"),
                                        start=hh == 0, stop=hh == 1)
                ins.then_inc(gP.sem, 1)
                wait(pe, gP, "vb", p)
                wait(pe, gA, "at", p)
                pe.wait_ge(diag_in, 8 * 16 * (p + 1))
                for c in range(NC_G):
                    for hh in range(2):
                        ins = TE.matmul(ps[:, 6 + hh, c * LC_G:(c + 1) * LC_G], g_vt[:, hh, c, :], g_att[:, hh, c, :],
                                        start=False, stop=c == NC_G - 1)
                ins.then_inc(gP.sem, 1)
                wait(pe, gD, "ss", p)
                for hh in range(2):
                    r = slice(64 * hh, 64 * hh + 64)
                    for b in range(B):
                        ins = TE.matmul(ps[:, hh, 256 + b:257 + b], g_ss[r, b, :], z[r, 16 + p, T + b:T + b + 1],
                                        start=True, stop=True)
                ins.then_inc(gP.sem, 1)
                for hh in range(2):
                    wait(pe, gA, f"sq{hh}", p)
                    bank = (4, 2)[hh]
                    for n in range(2):
                        ins = TE.matmul(half(bank, n), ONES, sq[:, hh, n * HALF:(n + 1) * HALF], start=True, stop=True)
                    ins.then_inc(gP.sem, 1)

            pe.wait_ge(gD.sem, gD.all(G_PAIRS))
            project("rec_out", S_OUT)
            norm(1, 0, FIRST["rec_out"] + 5)
            project("ffn0", S_FFN, 1)
            wait(pe, fD, "lo", FT - 1)
            down("down0")
            norm(2, 6)
            project("att_q", A_HEADS, 2)

            pe.wait_ge(catt_in, 16)
            pe.wait_ge(drained, FIRST["att_kv"])
            wait(pe, lamD, "prod")
            TE.matmul(ps[:, 0, 0:2], ONES[0:64, :], lam[0:64, 0:2], start=True, stop=True).then_inc(lamP.sem, 1)
            HALVES = c_("ones_half")

            def sums(bank, n, steps):
                for g in range(2):
                    ins = TE.matmul(half(bank, g), HALVES, sq3[:, n, g * HALF:(g + 1) * HALF], start=True, stop=True)
                ins.then_inc(steps.sem, 1)

            def v_rows(steps):
                for c in range(4):
                    ins = TE.transpose(ps[:, 0, c * P:(c + 1) * P], vn[:, c * P:(c + 1) * P], IDENT)
                ins.then_inc(steps.sem, 1)

            wait(pe, bA, "sqs")
            TE.matmul(ps[:, 6, 0:64], HALVES, qs_r[:, :, :].rearrange("p h b -> p (h b)"), start=True,
                      stop=True).then_inc(bP.sem, 1)
            wait(pe, lamA, "exp")
            slab_part(FIRST["att_kv"], FIRST["att_kv"] % 2, range(KT), 0)
            wait(pe, bA, "sqq")
            sums(2, 0, bP)
            wait(pe, bA, "sqk")
            slab_part(FIRST["att_kv"] + 1, (FIRST["att_kv"] + 1) % 2, range(KT), 0)
            sums(4, 1, bP)
            wait(pe, bA, "vr")
            v_rows(bP)

            def head(h, u, r_=None, first=False, last=False):
                sP_, sA_, sD_, r = (zP, zA, zD, 0) if last else (aP, aA, aD, h)
                n = FIRST["att_kv"] + 2 * (h + 1)
                bufs = (FIRST["att_kv"] % 2, (FIRST["att_kv"] + 1) % 2)

                def part(s, k0, k1):
                    if not last:
                        slab_part(n + s, bufs[s], range(k0, k1), 0)

                def scores(i):
                    for c in range(2):
                        g = slice(64 * c, 64 * c + 64)
                        ins = TE.matmul(ps[:, 2 + c, 0:(i + 1) * P], qn[g, u, i * P:(i + 1) * P],
                                        kn[g, u, 0:(i + 1) * P], start=True, stop=True)
                    ins.then_inc(sP_.sem, 1)

                def turn(i):
                    wait(pe, sD_, f"a{i}", r)
                    for c in range(i + 1):
                        ins = TE.transpose(ps[:, 4, c * P:(c + 1) * P], a_att[:, i % 2, c * P:(c + 1) * P], IDENT)
                    ins.then_inc(sP_.sem, 1)

                def values(i):
                    wait(pe, sA_, f"att{i}", r)
                    for c in range(i + 1):
                        ins = TE.matmul(ps[:, 5, i * P:(i + 1) * P], v_t2[:, u, c, :], at_t[:, i % 2, c * P:(c + 1) * P],
                                        start=c == 0, stop=c == i)
                    ins.then_inc(sP_.sem, 1)

                if first:
                    wait(pe, bD, "kn")
                else:
                    wait(pe, aD, "kn", h - 1)
                scores(0)
                if first:
                    wait(pe, bA, "vt")
                else:
                    wait(pe, aA, "vt", h - 1)
                part(0, 0, 2)
                if first:
                    wait(pe, bA, "rqs")
                    wait(pe, aG, "qd", 0)
                else:
                    wait(pe, aA, "orow", h - 1)
                    wait(pe, aD, "lall", h - 1)
                    wait(pe, aG, "qd", h)
                for g in range(2):
                    ins = TE.matmul(ps[:, 6 + g, :], ONES, qd[:, 4 * g:4 * g + 4, :].rearrange("p h k -> p (h k)"),
                                    start=True, stop=True)
                ins.then_inc(sP_.sem, 1)
                part(0, 2, 4)
                wait(pe, sA_, "ex0", r)
                scores(1)
                if not last:
                    wait(pe, sA_, "qb", r)
                    wait(pe, sA_, "sqq", r)
                    sums(6, 0, sP_)
                turn(0)
                part(0, 4, 6)
                values(0)
                wait(pe, sA_, "ex1", r)
                scores(2)
                turn(1)
                part(0, 6, 8)
                values(1)
                wait(pe, sA_, "ex2", r)
                scores(3)
                turn(2)
                if not last:
                    wait(pe, sA_, "sqk", r)
                part(1, 0, 3)
                values(2)
                turn(3)
                part(1, 3, 6)
                values(3)
                wait(pe, sD_, "red3", r)
                if last:
                    wait(pe, sA_, "qb", r)
                else:
                    wait(pe, sA_, "rq", r)
                for j in range(PAGES):
                    ins = TE.transpose(ps[0:16, 6, j * P:(j + 1) * P], s_sc[:, j, :], IDENT)
                ins.then_inc(sP_.sem, 1)
                part(1, 6, 8)
                if not last:
                    wait(pe, sA_, "ex3", r)
                    sums(2, 1, sP_)
                wait(pe, sA_, "sqo", r)
                TE.matmul(ps[:, 4, :], ONES, sq3[:, 2, 0:T], start=True, stop=True).then_inc(sP_.sem, 1)
                wait(pe, sD_, "dmx", r)
                TE.matmul(ps[:, 7, 0:16], ONES[0:16, :], s_dm[0:16, :], start=True, stop=True).then_inc(sP_.sem, 1)
                if not last:
                    wait(pe, sA_, "vr", r)
                    v_rows(sP_)
                wait(pe, sA_, "se", r)
                wait(pe, sD_, "sub", r)
                for j in range(PAGES):
                    pe.wait_ge(v_in[j], 16 * h + 16)
                    for g in range(2):
                        ins = TE.matmul(ps[0:16, 6 + g, :], s_sc[:, j, :], v_pages[:, j, g * 512:(g + 1) * 512],
                                        start=j == 0, stop=j == PAGES - 1)
                ins.then_inc(sP_.sem, 1)
                wait(pe, sD_, "ls", r)
                wait(pe, sA_, "ro", r)
                TE.matmul(ps[:, 4, 0:16], ONES, s_sum[:, :], start=True, stop=True).then_inc(sP_.sem, 1)

            head(0, 0, first=True)
            with pe.Fori(0, (A_HEADS - 2) // 2) as i:
                for u in range(2):
                    head(2 * i + (1 + u), 1 - u)
            head(A_HEADS - 1, 1, last=True)

            wait(pe, tD, "new1")
            TE.matmul(ps[:, 0, 0:P], ONES, s_new[:, :], start=True, stop=True).then_inc(tP.sem, 1)
            pe.wait_ge(past_in, 16 * A_HEADS)
            TE.transpose(ps[:, 1, 0:P], o_rows[:, :], IDENT).then_inc(tP.sem, 1)
            wait(pe, tA, "sq")
            TE.matmul(ps[:, 6, 0:64], ONES, s_r2[:, 0, :], start=True, stop=True).then_inc(tP.sem, 1)
            wait(pe, tD, "lo")
            wait(pe, eD, "lo2")
            project("att_out", S_OUT)
            norm(3, 0, FIRST["att_out"] + 5)
            project("ffn1", S_FFN, 3)
            wait(pe, fD, "lo", 2 * FT - 1)
            down("down1")

        def walk(eng, name, split, drain):
            nk = dict((n, k) for n, _, k in PHASES)[name]
            total = dict((n, s) for n, s, _ in PHASES)[name]
            loops = (total - 2) // 4

            def step(i, s, left=2):
                if left >= 2:
                    split(name, i, s + 2, nk)
                else:
                    order = [n for n, _, _ in PHASES]
                    after = order.index(name) + 1
                    if after < len(PHASES):
                        split(order[after], 0, 1 - left, PHASES[after][2])
                drain(i, s)

            peeled = 1 if loops == 1 or FIRST[name] == 0 else 0
            for s in range(4 * peeled):
                step(0, s)
            if loops > peeled:
                with eng.Fori(peeled, loops) as i:
                    for s in range(4):
                        step(i, s)
            for n in range(4 * loops, total):
                step(loops, n - 4 * loops, total - 1 - n)

        @block.scalar
        def _(act):
            LN_EXP = "natural_log_exp_and_others"

            def rsqrt(out, total, n, steps, ln, r=0):
                S.activation(out, total, ACT.Ln, bias=eps[:, :], scale=1.0 / n).then_inc(steps.sem, 1)
                wait(act, steps, ln, r)
                return S.activation(out, out, ACT.Exp, scale=-0.5)

            def split(name, i, s, nk):
                n = FIRST[name] + s
                act.wait_ge(landed[n % RAW], 16 * (i + n // RAW + 1))
                if is_a_wait(4 * i + (n - 1)):
                    act.wait_ge(slab_done, 4 * i + (n - 1))
                S.copy(w_hi[:, n % 2, 0:nk * P], raw[:, n % RAW, 0:nk * P]).then_inc(hi_split, 1)

            def square(r, i, c):
                if c >= 2 or not isinstance(i, int) or i:
                    act.wait_ge(summed, 2 * i + ((KT - 1) * r + c - 1))
                xc = x[:, 2 * i + c, :] if isinstance(i, int) else x[:, ds(2 * i + c, 1), :].rearrange("p o t -> p (o t)")
                S.activation(sq[:, c % 2, :], xc, ACT.Square).then_inc(squared, 1)

            def out_squares(name, r):
                def drain(i, s):
                    act.wait_ge(drained, FIRST[name] + 4 * i + s + 1)
                    square(r, 0, 4 * i + s)
                return drain

            def down_squares(name, r):
                def drain(i, s):
                    if s % 2:
                        act.wait_ge(drained, 4 * i + (FIRST[name] + s + 1))
                        square(r, i, s // 2)
                return drain

            def norm(r, bank):
                wait(act, nP, "sum", r)
                wait(act, small, "eps")
                rsqrt(two(rstd[:, :]), pair(bank), D_MODEL, nA, "lr", r).then_inc(nA.sem, 1)
                for c in range(KT):
                    wait(act, nD, f"n{c}", r)
                    S.copy(h_hi[:, c, :], hn[:, c % 2, :]).then_inc(nA.sem, 1)

            def tile_out(name, out):
                def drain(i, s):
                    act.wait_ge(slab_done, 4 * i + (FIRST[name] + s + 1))
                    S.copy(two(out[:, 4 * i + s, :]) if isinstance(i, int) else
                           out[:, ds(4 * i + s, 1), :].rearrange("p o (a t) -> p (o a) t", a=2),
                           pair(2 * (s % 4))).then_inc(drained, 1)
                return drain

            def rec_step(n):
                if n + 2 < S_REC_IN:
                    split("rec_in", 0, n + 2, KT)
                else:
                    split("rec_out", 0, n + 2 - S_REC_IN, KT)
                act.wait_ge(slab_done, n + 1)
                out = gates[:, :] if REC_TILES[n] == 28 else z[:, REC_TILES[n], :]
                bank = 2 * (n % 4) if n < len(FIRST_SLABS) else 2
                S.copy(two(out), pair(bank)).then_inc(drained, 1)

            def nothing(i, s):
                pass

            def ffn(layer):
                name = f"ffn{layer}"

                def drain(i, s):
                    r = 2 * i + (s // 2 + layer * FT)
                    m = 2 * i + s // 2
                    act.wait_ge(slab_done, 4 * i + (FIRST[name] + s + 1))
                    if s % 2 == 0:
                        S.copy(two(ub[:, s // 2, 2:2 + NT]), pair(2 * (s % 4))).then_inc(fA.sem, 1)
                        S.copy(conv_end[:, ds(m, 1), :] if not isinstance(m, int) else conv_end[:, m:m + 1, :],
                               ps[:, 2 * s + 1:2 * s + 2, HALF - 2 - B:HALF]).then_inc(fA.sem, 1)
                        act.wait_ge(fD.sem, fD.at("s0", r))
                        S.activation(ge[:, :], cc[:, :], ACT.Gelu_apprx_tanh).then_inc(fA.sem, 1)
                    else:
                        act.wait_ge(fD.sem, fD.at("prod", r))
                        S.copy(a_hi[:, ds(m, 1), :] if not isinstance(m, int) else a_hi[:, m:m + 1, :],
                               pr[:, :].rearrange("p (o t) -> p o t", o=1)).then_inc(fA.sem, 1)
                S.preload_act_table(ACT.Gelu_apprx_tanh)
                if layer:
                    act.wait_ge(conv_out, 16)
                walk(act, name, split, drain)

            act.dma_start(par[:, :], a["par"]).then_inc(par_in, 16)
            act.dma_start(cst[:, :], a["cst"]).then_inc(par_in, 16)
            S.preload_act_table_set(LN_EXP)
            for c in range(KT):
                if c % 4 == 0:
                    act.wait_ge(x_in[c // 4], 16)
                square(0, 0, c)
            split("rec_in", 0, 0, KT)
            norm(0, 6)
            split("rec_in", 0, 1, KT)
            rec_step(0)

            rec_step(1)
            wait(act, gtD, "neg")
            S.activation(f_log[:, :], f_neg[:, :], ACT.Exp).then_inc(gtA.sem, 1)
            wait(act, gtA, "exp")
            S.activation(f_log[:, :], f_log[:, :], ACT.Ln, bias=one[0:4, :]).then_inc(gtA.sem, 1)
            for n in range(2, len(FIRST_SLABS)):
                rec_step(n)
            wait(act, gtP, "acol")
            S.copy(a_col[:, :, :], ps[:, 7, 0:4 * NC_M].rearrange("p (c h) -> p c h", h=4)).then_inc(gtA.sem, 1)

            for h in range(M_HEADS):
                first = len(FIRST_SLABS) + PER_HEAD * h
                wait(act, mP, "bcs", h)
                S.activation(w_s[:, :, :].rearrange("p a b -> p (a b)"), ps[:, 4, 0:3 * B], ACT.Exp).then_inc(mA.sem, 1)
                S.activation(w_int[:, :], ps[:, 1, :], ACT.Exp).then_inc(mA.sem, 1)
                if h:
                    wait(act, mD, "mix", h - 1)
                S.activation(e_negm[:, :], ps[:, 6, :], ACT.Exp).then_inc(mA.sem, 1)
                wait(act, mD, "em", h)
                for c in range(NC_M):
                    ins = S.activation(e_mat[:, c, :], e_mat[:, c, :], ACT.Exp, bias=a_col[:, c, h:h + 1])
                ins.then_inc(mA.sem, 1)
                wait(act, mP, "ktr", h)
                S.copy(k_tok[:, :, :].rearrange("p c k -> p (c k)"), ps[:, 4, :]).then_inc(mA.sem, 1)
                S.copy(v_tok[:, :, :].rearrange("p c k -> p (c k)"), ps[:, 5, :]).then_inc(mA.sem, 1)
                rec_step(first)
                act.wait_ge(drained, first + 1)
                gate = (z[:, 12:14, :], z[:, 14, :], z[:, 15, :], None)[h]
                if gate is not None:
                    ins = S.activation(gate, gate, ACT.Sigmoid)
                if h == 2:
                    S.activation(z[:, 24:28, :], z[:, 24:28, :], ACT.Silu)
                if gate is not None:
                    S.preload_act_table_set(LN_EXP)
                act.sem_inc(mA.sem, 1)
                rec_step(first + 1)
                wait(act, mP, "num3", h)
                S.activation(den[:, :], ps[:, 7, :], ACT.Abs).then_inc(mA.sem, 1)
                rec_step(first + 2)
                rec_step(first + 3)
                wait(act, mP, "dens", h)
                S.activation(den_s[:, :], ps[:, 6, 0:B], ACT.Abs).then_inc(mA.sem, 1)
                wait(act, mD, "hs2", h)
                S.activation(sq[:, 0, :], h_head[:, :], ACT.Square).then_inc(mA.sem, 1)
                rec_step(first + 4)
                wait(act, mP, "ssq", h)
                rsqrt(two(rstd[:, :]), pair(4), P, mA, "lr", h).then_inc(mA.sem, 1)
                if h < M_HEADS - 1:
                    rec_step(first + 5)

            wait(act, lD, "neg")
            S.activation(ln_t[:, :, :], ln_t[:, :, :], ACT.Exp).then_inc(lA.sem, 1)
            wait(act, lA, "exp")
            S.activation(ln_t[:, :, :], ln_t[:, :, :], ACT.Ln, bias=one[:, :]).then_inc(lA.sem, 1)

            def decays(p):
                wait(act, dD, "bc", p)
                S.activation(g_qd[:, :], bc[:, :], ACT.Exp).then_inc(dA.sem, 1)
                wait(act, dD, "qe", p)
                S.activation(g_qs[:, :], g_qs[:, :], ACT.Exp).then_inc(dA.sem, 1)
                S.activation(a_end[:, :], bc[:, LC_G - 1::LC_G], ACT.Exp).then_inc(dA.sem, 1)
                wait(act, dD, "kem", p)
                S.activation(ke[:, :, :, :].rearrange("p c j s -> p (c j s)"),
                             ke[:, :, :, :].rearrange("p c j s -> p (c j s)"), ACT.Exp).then_inc(dA.sem, 1)
                wait(act, dD, "kend", p)
                S.activation(g_kd[:, :], g_kd[:, :], ACT.Exp).then_inc(dA.sem, 1)

            def chunks(p):
                wait(act, gP, "vt", p)
                wait(act, hD, "lo")
                for hh in range(2):
                    bank = (6, 0)[hh]
                    ins = S.copy(g_vt[:, hh, :, :].rearrange("p (n c) v -> p n (c v)", n=2), ps[0:64, bank:bank + 2, :])
                ins.then_inc(gA.sem, 1)
                if p:
                    act.wait_ge(gss_out, 16)

                def exps(i):
                    wait(act, xD if i < 2 else gD, f"xm{i}", p)
                    flat = lx[:, 4 * (i % 2):4 * (i % 2) + 4, :, :].rearrange("p b s t -> p (b s t)")
                    S.activation(flat, flat, ACT.Exp).then_inc(gA.sem, 1)

                def blocks(n):
                    wait(act, gP, f"dg{2 * n + 1}", p)
                    S.copy(dg[:, n, :], ps[:, 2 + n % 2, :]).then_inc(gA.sem, 1)

                exps(0)
                exps(1)
                wait(act, gP, "kdt", p)
                S.copy(g_kdt[:, :, :].rearrange("p (n c) v -> p n (c v)", n=2), ps[0:64, 2:4, :]).then_inc(gA.sem, 1)
                S.activation(a_s[:, :], log_a[:, p, T:NT], ACT.Exp).then_inc(gA.sem, 1)
                exps(2)
                blocks(0)
                exps(3)
                exps(4)
                blocks(1)
                exps(5)
                exps(6)
                blocks(2)
                exps(7)
                blocks(3)
                wait(act, gP, "off", p)
                wait(act, gG, "za", p)
                for hh in range(2):
                    for j in range(1, 4):
                        r, t = slice(0, SUB * j), slice(SUB * j, SUB * (j + 1))
                        ins = S.copy(g_att[r, hh, :, t],
                                     ps[r, 4 + hh, :].rearrange("p (c t) -> p c t", c=NC_G)[:, :, t])
                ins.then_inc(gA.sem, 1)

            def outputs(p):
                for hh in range(2):
                    wait(act, gP, "oi", p)
                    S.activation(sq[:, hh, 0:T], ps[:, 6 + hh, :], ACT.Square)
                    wait(act, gP, "os", p)
                    S.activation(sq[:, hh, T:NT], ps[:, hh, 256:256 + B], ACT.Square).then_inc(gA.sem, 1)
                for hh in range(2):
                    wait(act, gP, f"ssq{hh}", p)
                    rsqrt(two(sq[:, hh, :]), pair((4, 2)[hh]), P, gA, f"lr{hh}", p).then_inc(gA.sem, 1)
                for hh in range(2):
                    wait(act, gD, f"mix{hh}", p)
                    S.copy(h_hi[:, 4 + 2 * p + hh, :], hn[:, hh, :]).then_inc(gA.sem, 1)

            decays(0)
            rec_step(S_REC_IN - 1)
            act.wait_ge(slab_done, S_REC_IN)
            wait(act, mD, "mix", M_HEADS - 1)
            S.copy(h_hi[:, 0:4, :], z[:, 12:16, :]).then_inc(hA.sem, 1)
            for p in range(G_PAIRS):
                chunks(p)
                if p + 1 < G_PAIRS:
                    decays(p + 1)
                outputs(p)

            walk(act, "rec_out", split, out_squares("rec_out", 1))
            norm(1, 0)
            ffn(0)
            S.preload_act_table_set(LN_EXP)
            walk(act, "down0", split, down_squares("down0", 2))
            norm(2, 6)
            walk(act, "att_q", split, tile_out("att_q", zq))

            S.preload_act_table_set(LN_EXP)
            wait(act, lamP, "sum")
            S.activation(lam[:, 2:4], ps[:, 0, 0:2], ACT.Exp).then_inc(lamA.sem, 1)

            def zq_of(h):
                return zq[:, h, :] if isinstance(h, int) else zq[:, ds(h, 1), :].rearrange("p o t -> p (o t)")

            F_KV = FIRST["att_kv"]
            act.wait_ge(drained, F_KV)
            S.activation(qs_r[:, :, :], zq[:, :, T:NT], ACT.Square).then_inc(bA.sem, 1)
            wait(act, bP, "sqs")
            rsqrt(qs_t[:, :, :].rearrange("p h b -> p (h b)"), ps[:, 6, 0:64], A_QK, bA, "lrs").then_inc(bA.sem, 1)
            S.activation(sq3[:, 0, :], zq[:, 0, :], ACT.Square).then_inc(bA.sem, 1)
            wait(act, bP, "ssq")
            rsqrt(two(rs3[:, 0, :]), pair(2), A_QK, bA, "lrq").then_inc(bA.sem, 1)
            act.wait_ge(slab_done, F_KV + 1)
            S.copy(two(kraw[:, :]), pair(0)).then_inc(bA.sem, 1)
            S.activation(two(sq3[:, 1, :]), pair(0), ACT.Square).then_inc(bA.sem, 1)
            split("att_kv", 0, 2, KT)
            act.wait_ge(slab_done, F_KV + 2)
            S.copy(two(vn[:, :]), pair(0)).then_inc(bA.sem, 1)
            split("att_kv", 0, 3, KT)
            wait(act, bP, "ssk")
            rsqrt(two(rs3[:, 1, :]), pair(4), A_QK, bA, "lrk").then_inc(bA.sem, 1)
            wait(act, bP, "vtr")
            S.copy(v_t2[:, 0, :, :].rearrange("p c v -> p (c v)"), ps[:, 0, :]).then_inc(bA.sem, 1)

            def head(h, u, i, h0, last=False):
                sP_, sA_, sD_, r = (zP, zA, zD, 0) if last else (aP, aA, aD, h)

                def exps(k):
                    wait(act, sD_, f"nx{k}", r)
                    for c in range(2):
                        ins = S.activation(e_att[:, k % 2, c, 0:(k + 1) * P], ps[:, 2 + c, 0:(k + 1) * P], ACT.Exp,
                                           bias=mx[:, k % 2, c:c + 1], scale=A_QK ** -0.5, accum_out=sm[:, k % 2, c:c + 1])
                    ins.then_inc(sA_.sem, 1)

                def copy_t(k):
                    wait(act, sP_, f"t{k}", r)
                    S.copy(at_t[:, k % 2, 0:(k + 1) * P], ps[:, 4, 0:(k + 1) * P]).then_inc(sA_.sem, 1)

                if not last:
                    S.activation(sq3[:, 0, :], zq_of(h + 1), ACT.Square).then_inc(sA_.sem, 1)
                exps(0)
                wait(act, sP_, "qb", r)
                S.copy(qb[:, :].rearrange("p (n k) -> p n k", n=2), ps[:, 6:8, :]).then_inc(sA_.sem, 1)
                exps(1)
                if not last:
                    wait(act, sP_, "ssq", r)
                    rsqrt(two(rs3[:, 0, :]), pair(6), A_QK, sA_, "lrq", r).then_inc(sA_.sem, 1)
                copy_t(0)
                exps(2)
                copy_t(1)
                if not last:
                    n0 = F_KV + 2 * (h + 1)
                    act.wait_ge(slab_done, n0 + 1)
                    S.copy(two(kraw[:, :]), pair(0)).then_inc(sA_.sem, 1)
                    S.activation(two(sq3[:, 1, :]), pair(0), ACT.Square).then_inc(sA_.sem, 1)
                    split("att_kv", i, 2 * (h0 + 2), KT)
                exps(3)
                if last:
                    S.copy(h_hi[:, 0:4, 0:T], zq[:, 0:4, 0:T]).then_inc(eA.sem, 1)
                copy_t(2)
                copy_t(3)
                if last:
                    S.copy(h_hi[:, 4:7, 0:T], zq[:, 4:7, 0:T]).then_inc(eA.sem, 1)
                wait(act, sP_, "v3", r)
                S.activation(sq3[:, 2, 0:T], ps[:, 5, :], ACT.Square).then_inc(sA_.sem, 1)
                if not last:
                    act.wait_ge(slab_done, n0 + 2)
                    act.wait_ge(vn_out, 16 * (h + 1))
                    wait(act, aG, "vs", h)
                    S.copy(two(vn[:, :]), pair(0)).then_inc(sA_.sem, 1)
                    split("att_kv", i, 2 * (h0 + 2) + 1, KT)
                    wait(act, sP_, "ssk", r)
                    rsqrt(two(rs3[:, 1, :]), pair(2), A_QK, sA_, "lrk", r).then_inc(sA_.sem, 1)
                wait(act, sP_, "sso", r)
                rsqrt(rs3[:, 2, 0:T], ps[:, 4, :], P, sA_, "lro", r).then_inc(sA_.sem, 1)
                wait(act, sD_, "sub", r)
                flat = s_sc[:, :, :].rearrange("p j k -> p (j k)")
                S.activation(flat, flat, ACT.Exp, scale=A_QK ** -0.5).then_inc(sA_.sem, 1)
                if not last:
                    wait(act, sP_, "vtr", r)
                    S.copy(v_t2[:, 1 - u, :, :].rearrange("p c v -> p (c v)"), ps[:, 0, :]).then_inc(sA_.sem, 1)
                else:
                    wait(act, zD, "mix")
                    S.copy(h_hi[:, A_HEADS - 1, 0:T], zq[:, A_HEADS - 1, 0:T]).then_inc(eA.sem, 1)
                wait(act, sP_, "pv", r)
                S.copy(o_row.rearrange("p (n k) -> p n k", n=2), ps[0:16, 6:8, :]).then_inc(sA_.sem, 1)

            head(0, 0, 0, 0)
            with act.Fori(0, (A_HEADS - 2) // 2) as i:
                for w in range(2):
                    head(2 * i + (1 + w), 1 - w, i, 1 + w)
            head(A_HEADS - 1, 1, 0, A_HEADS - 1, last=True)

            wait(act, tD, "d2")
            S.activation(s_w[1][:, :], s_w[1][:, :], ACT.Exp, scale=A_QK ** -0.5)
            S.activation(s_w[2][:, :], s_w[2][:, :], ACT.Exp, scale=A_QK ** -0.5).then_inc(tA.sem, 1)
            wait(act, tD, "a")
            S.activation(s_r2[:, 0, :], s_o[:, :], ACT.Square).then_inc(tA.sem, 1)
            wait(act, tP, "ssq")
            rsqrt(s_r2[:, 1, :], ps[:, 6, 0:64], P, tA, "lr").then_inc(tA.sem, 1)
            wait(act, tD, "mix")
            S.copy(h_hi[:, :, T:NT], s_o2[:, :].rearrange("p (b h) -> p h b", b=B)).then_inc(tA.sem, 1)
            act.sem_inc(drained, 2 * A_HEADS)
            act.wait_ge(vn_out, 16 * A_HEADS)

            walk(act, "att_out", split, out_squares("att_out", 3))
            norm(3, 0)
            ffn(1)
            walk(act, "down1", split, nothing)

        def add_squares(eng, ops, r, c):
            eng.wait_ge(squared, KT * r + c + 1)
            if c == 0:
                ops.tensor_copy(ssum[:, :], sq[:, 0, :]).then_inc(summed, 1)
            else:
                eng.wait_ge(summed, (KT - 1) * r + c)
                ops.tensor_tensor(ssum[:, :], ssum[:, :], sq[:, c % 2, :], ALU.add).then_inc(summed, 1)

        @block.vector
        def _(dve):
            def split(name, i, s, nk):
                n = FIRST[name] + s
                dve.wait_ge(hi_split, 4 * i + (n + 1))
                V.tensor_tensor(w_lo[:, n % 2, 0:nk * P], raw[:, n % RAW, 0:nk * P],
                                w_hi[:, n % 2, 0:nk * P].bitcast(F32), ALU.subtract).then_inc(lo_split, 1)

            def norm(r, gain):
                wait(dve, nA, "rms", r)

                def lo(c):
                    wait(dve, nA, f"hi{c}", r)
                    V.tensor_tensor(h_lo[:, c, :], hn[:, c % 2, :], h_hi[:, c, :].bitcast(F32),
                                    ALU.subtract).then_inc(nD.sem, 1)

                for c in range(KT):
                    if c >= 2:
                        wait(dve, nD, f"lo{c - 2}", r)
                    V.scalar_tensor_tensor(out=hn[:, c % 2, :], in0=x[:, c, :], scalar=p_(gain, c, 1), in1=rstd[:, :],
                                           op0=ALU.mult, op1=ALU.mult).then_inc(nD.sem, 1)
                    if c:
                        lo(c - 1)
                lo(KT - 1)

            def nothing(i, s):
                pass

            def out_drain(name):
                def drain(i, s):
                    c = 4 * i + s
                    dve.wait_ge(slab_done, 4 * i + (FIRST[name] + s + 1))
                    xc = x[:, c, :]
                    V.tensor_tensor(two(xc), two(xc), pair(2 * (s % 4)), ALU.add).then_inc(drained, 1)
                return drain

            def down_drain(name):
                def drain(i, s):
                    if s % 2:
                        dve.wait_ge(slab_done, 4 * i + (FIRST[name] + s + 1))
                        xc = x[:, 2 * i + s // 2, :] if isinstance(i, int) else \
                            x[:, ds(2 * i + s // 2, 1), :].rearrange("p o t -> p (o t)")
                        V.tensor_tensor(two(xc), two(xc), pair(4 * (s // 2)), ALU.add).then_inc(drained, 2)
                return drain

            def ffn(layer):
                name = f"ffn{layer}"
                cw, cb, cs = (columns(PARAMS)[0][f"{n}{layer}"][0] for n in ("conv_w", "conv_b", "conv_s"))

                def drain(i, s):
                    r = 2 * i + (s // 2 + layer * FT)
                    m = 2 * i + s // 2

                    def col(at, k=0, n=1, step=1):
                        return par[:, ds(step * m + (at + k), n)] if not isinstance(m, int) else \
                            par[:, at + k + step * m:at + k + step * m + n]
                    u = ub[:, s // 2, :]
                    if s % 2 == 0:
                        dve.wait_ge(fA.sem, fA.at("u", r))
                        V.tensor_scalar(cc[:, :], u[:, 2:2 + NT], col(cw, 2 * FT), col(cb), ALU.mult,
                                        ALU.add).then_inc(fD.sem, 1)
                        dve.wait_ge(fD.sem, fD.at("t0", r))
                        V.scalar_tensor_tensor(out=cc[:, 0:T], in0=u[:, 1:1 + T], scalar=col(cw, FT), in1=cc[:, 0:T],
                                               op0=ALU.mult, op1=ALU.add).then_inc(fD.sem, 1)
                        V.scalar_tensor_tensor(out=cc[:, T:NT], in0=col(cs, B, B, 2 * B), scalar=col(cw, FT),
                                               in1=cc[:, T:NT], op0=ALU.mult, op1=ALU.add).then_inc(fD.sem, 1)
                        dve.wait_ge(fD.sem, fD.at("s1", r))
                        V.scalar_tensor_tensor(out=cc[:, 0:T], in0=u[:, 0:T], scalar=col(cw), in1=cc[:, 0:T],
                                               op0=ALU.mult, op1=ALU.add).then_inc(fD.sem, 1)
                        V.scalar_tensor_tensor(out=cc[:, T:NT], in0=col(cs, 0, B, 2 * B), scalar=col(cw),
                                               in1=cc[:, T:NT], op0=ALU.mult, op1=ALU.add).then_inc(fD.sem, 1)
                    else:
                        dve.wait_ge(fA.sem, fA.at("gelu", r))
                        dve.wait_ge(slab_done, 4 * i + (FIRST[name] + s + 1))
                        V.tensor_tensor(two(pr[:, :]), two(ge[:, :]), pair(2 * (s % 4)), ALU.mult).then_inc(fD.sem, 1)
                        dve.wait_ge(fD.sem, fD.at("prod", r))
                        dve.sem_inc(drained, 2)
                        dve.wait_ge(fA.sem, fA.at("hi", r))
                        lo = a_lo[:, ds(m, 1), :] if not isinstance(m, int) else a_lo[:, m:m + 1, :]
                        hi = a_hi[:, ds(m, 1), :] if not isinstance(m, int) else a_hi[:, m:m + 1, :]
                        V.tensor_tensor(lo, pr[:, :].rearrange("p (o t) -> p o t", o=1), hi.bitcast(F32),
                                        ALU.subtract).then_inc(fD.sem, 1)
                wait(dve, pads, "pad", layer)
                walk(dve, name, split, drain)

            dve.wait_ge(par_in, 32)
            for c in range(KT - 1):
                add_squares(dve, V, 0, c)
            split("rec_in", 0, 0, KT)
            norm(0, "g_mix0")
            split("rec_in", 0, 1, KT)
            split("rec_in", 0, 2, KT)

            dve.wait_ge(drained, 1)
            dve.wait_ge(crec_in, 16)
            bm = columns(PARAMS)[0]["b_mgate"][0]
            V.tensor_scalar(f_pre[:, :], gates[32:36, :], par[32:36, bm:bm + 1], None, ALU.add).then_inc(gtD.sem, 1)
            V.tensor_scalar(i_pre[:, :], gates[0:4, :], par[0:4, bm:bm + 1], None, ALU.add).then_inc(gtD.sem, 1)
            wait(dve, gtD, "i")
            V.scalar_tensor_tensor(out=f_neg[:, :], in0=f_pre[:, :], scalar=-1.0, in1=f_pre[:, :], op0=ALU.mult,
                                   op1=ALU.min).then_inc(gtD.sem, 1)
            split("rec_in", 0, 3, KT)
            wait(dve, gtA, "ln")
            V.scalar_tensor_tensor(out=f_neg[:, :], in0=f_pre[:, :], scalar=0.0, in1=f_log[:, :], op0=ALU.min,
                                   op1=ALU.subtract).then_inc(gtD.sem, 1)
            wait(dve, gtD, "lf")
            V.tensor_tensor_scan(b_row[:, :], c_("reset_m")[0:4, :], f_neg[:, 0:T], 0.0, ALU.mult, ALU.add).then_inc(gtD.sem, 1)
            V.tensor_tensor_scan(m_run[:, :], f_neg[:, 0:T], i_pre[:, 0:T], 0.0, ALU.add, ALU.max).then_inc(gtD.sem, 1)
            V.tensor_tensor(r_s[:, 0:B], f_neg[:, T:NT], p_("m0")[0:4, :], ALU.add).then_inc(gtD.sem, 1)
            wait(dve, gtD, "lfm")
            V.tensor_tensor(m_out[:, 1:1 + B], r_s[:, 0:B], i_pre[:, T:NT], ALU.max).then_inc(gtD.sem, 1)
            V.tensor_tensor(r_intra[:, :], b_row[:, :], m_run[:, :], ALU.subtract).then_inc(gtD.sem, 1)
            V.tensor_tensor(a_row[:, :], i_pre[:, 0:T], b_row[:, :], ALU.subtract).then_inc(gtD.sem, 1)
            split("rec_in", 0, 4, KT)
            V.tensor_scalar(r_negm[:, :], m_run[:, :], -1.0, None, ALU.mult).then_inc(gtD.sem, 1)
            wait(dve, gtD, "nm")
            V.tensor_copy(r_inter[:, 0:P], r_intra[:, 0:P]).then_inc(gtD.sem, 1)
            for c in range(1, NC_M):
                t = slice(c * P, (c + 1) * P)
                V.tensor_scalar(r_inter[:, t], r_intra[:, t], m_run[:, c * P - 1:c * P], None, ALU.add).then_inc(gtD.sem, 1)
            V.tensor_tensor(r_s[:, 0:B], r_s[:, 0:B], m_out[:, 1:1 + B], ALU.subtract).then_inc(gtD.sem, 1)
            V.tensor_scalar(r_s[:, B:2 * B], m_out[:, 1:1 + B], -1.0, None, ALU.mult).then_inc(gtD.sem, 1)
            V.tensor_tensor(r_s[:, 2 * B:3 * B], i_pre[:, T:NT], m_out[:, 1:1 + B], ALU.subtract).then_inc(gtD.sem, 1)
            V.tensor_copy(m_out[:, 0:1], m_run[:, T - 1:T]).then_inc(gtD.sem, 1)
            split("rec_in", 0, 5, KT)
            split("rec_in", 0, 6, KT)

            K_SCALE = float(P) ** -0.5

            def rows(ap, n):
                return ap.unsqueeze(2).to_broadcast([P, ap.shape[1], n])

            def cols_(ap, n):
                return ap.unsqueeze(1).to_broadcast([P, n, ap.shape[1]])

            for h in range(M_HEADS):
                q, k, v, gate = z[:, h, :], z[:, 4 + h, :], z[:, 8 + h, :], z[:, 12 + h, :]

                def rec_split(j):
                    n = len(FIRST_SLABS) + PER_HEAD * h + j + 2
                    if n < S_REC_IN:
                        split("rec_in", 0, n, KT)
                    else:
                        split("rec_out", 0, n - S_REC_IN, KT)

                wait(dve, mP, "bc0", h)
                V.tensor_tensor(e_mat[:, :, :], ps[:, 0, :].rearrange("p (c t) -> p c t", c=NC_M),
                                cols_(c_("causal_T"), NC_M), ALU.add).then_inc(mD.sem, 1)
                wait(dve, mA, "wi", h)
                V.tensor_tensor(q_w[:, :], q[:, 0:T], w_int[:, :], ALU.mult).then_inc(mD.sem, 1)
                wait(dve, mA, "vt", h)
                for c in range(NC_M):
                    end = e_mat[:, c, P - 1:P]
                    V.tensor_scalar(v_end[:, c, 0, :], v_tok[:, c, :], end, K_SCALE, ALU.mult, ALU.mult)
                    ins = V.tensor_scalar(v_end[:, c, 1, :], ONES, end, K_SCALE, ALU.mult, ALU.mult)
                ins.then_inc(mD.sem, 1)
                wait(dve, mP, "scores", h)
                wait(dve, mD, "ve", h)
                flat = e_mat[:, :, :].rearrange("p c t -> p (c t)")
                V.scalar_tensor_tensor(out=flat, in0=ps[:, 7, :], scalar=K_SCALE, in1=flat, op0=ALU.mult,
                                       op1=ALU.mult).then_inc(mD.sem, 1)
                rec_split(0)
                rec_split(1)
                for c in range(NC_M):
                    wait(dve, mP, f"st{c}", h)
                    if c == 0:
                        if h:
                            dve.wait_ge(c_out, 16 * h)
                        V.tensor_copy(c_n[:, :], ps[:, 0, 0:2 * P]).then_inc(mD.sem, 1)
                    else:
                        wait(dve, mD, f"cn{c - 1}", h)
                        V.scalar_tensor_tensor(out=c_n[:, :], in0=c_n[:, :], scalar=w_int[:, (c + 1) * P - 1:(c + 1) * P],
                                               in1=ps[:, c % 2, 0:2 * P], op0=ALU.mult, op1=ALU.add).then_inc(mD.sem, 1)
                wait(dve, mD, "cn3", h)
                V.tensor_copy(n_end[:, h:h + 1], c_n[:, P:P + 1]).then_inc(mD.sem, 1)
                wait(dve, mA, "abs", h)
                V.tensor_tensor(den[:, :], den[:, :], e_negm[:, :], ALU.max).then_inc(mD.sem, 1)
                wait(dve, mD, "den", h)
                V.reciprocal(den[:, :], den[:, :]).then_inc(mD.sem, 1)
                rec_split(2)
                wait(dve, mD, "rden", h)
                V.tensor_tensor(h_head[:, 0:T], ps[:, 6, :], den[:, :], ALU.mult).then_inc(mD.sem, 1)
                V.scalar_tensor_tensor(out=v_ws[:, :], in0=v[:, T:NT], scalar=K_SCALE, in1=w_s[:, 2, :], op0=ALU.mult,
                                       op1=ALU.mult).then_inc(mD.sem, 1)
                V.scalar_tensor_tensor(out=k_ws[:, :], in0=k[:, T:NT], scalar=K_SCALE, in1=w_s[:, 2, :], op0=ALU.mult,
                                       op1=ALU.mult).then_inc(mD.sem, 1)
                V.tensor_tensor(nw[:, :], p_("n0", h * B, B), w_s[:, 0, :], ALU.mult).then_inc(mD.sem, 1)
                wait(dve, mD, "nw", h)
                V.tensor_tensor(n_s[:, h, :], nw[:, :], k_ws[:, :], ALU.add).then_inc(mD.sem, 1)
                wait(dve, mD, "ns", h)
                V.tensor_tensor(nq[:, :], n_s[:, h, :], q[:, T:NT], ALU.mult).then_inc(mD.sem, 1)
                wait(dve, mP, "kb", h)
                row4 = ps[:, 4:6, :].rearrange("p n (b k) -> p (n b) k", k=P)
                row0 = ps[:, 0:2, :].rearrange("p n (b k) -> p (n b) k", k=P)
                V.tensor_tensor(kv[:, :, :], row4, rows(v_ws[:, :], P), ALU.mult).then_inc(mD.sem, 1)
                wait(dve, mG, "cw", h)
                wait(dve, mD, "kv", h)
                V.tensor_tensor(c_s[:, :, :], c_s[:, :, :], kv[:, :, :], ALU.add).then_inc(mD.sem, 1)
                rec_split(3)
                wait(dve, mD, "cs", h)
                wait(dve, mP, "qb", h)
                V.tensor_tensor(kv[:, :, :], c_s[:, :, :], row0, ALU.mult).then_inc(mD.sem, 1)
                wait(dve, mD, "cq", h)
                V.tensor_reduce(hnum_s[:, :], kv[:, :, :], AX.X, ALU.add).then_inc(mD.sem, 1)
                wait(dve, mA, "abs_s", h)
                V.tensor_tensor(den_s[:, :], den_s[:, :], w_s[:, 1, :], ALU.max).then_inc(mD.sem, 1)
                wait(dve, mD, "dn", h)
                V.reciprocal(den_s[:, :], den_s[:, :]).then_inc(mD.sem, 1)
                wait(dve, mD, "rd", h)
                V.tensor_tensor(h_head[:, T:NT], hnum_s[:, :], den_s[:, :], ALU.mult).then_inc(mD.sem, 1)
                rec_split(4)
                wait(dve, mA, "rms", h)
                V.tensor_tensor(hn[:, 0, :], h_head[:, :], rstd[:, :], ALU.mult).then_inc(mD.sem, 1)
                wait(dve, mD, "t", h)
                V.scalar_tensor_tensor(out=gate, in0=hn[:, 0, :], scalar=p_("g_m"), in1=gate, op0=ALU.mult,
                                       op1=ALU.mult).then_inc(mD.sem, 1)
                if h < M_HEADS - 1:
                    rec_split(5)

            wait(dve, lP, "up")
            dve.wait_ge(c_out, 16 * M_HEADS)
            dve.wait_ge(cs_out, 16 * M_HEADS)
            for p in range(G_PAIRS):
                ins = V.tensor_scalar(two(log_a[:, p, :]), pair(6 * p), p_("b_gate", p, 1), None, ALU.add)
            ins.then_inc(lD.sem, 1)
            wait(dve, lD, "z")
            V.scalar_tensor_tensor(out=ln_t[:, :, :], in0=log_a[:, :, :], scalar=-1.0, in1=log_a[:, :, :], op0=ALU.mult,
                                   op1=ALU.min).then_inc(lD.sem, 1)
            wait(dve, lA, "ln")
            V.scalar_tensor_tensor(out=log_a[:, :, :], in0=log_a[:, :, :], scalar=0.0, in1=ln_t[:, :, :], op0=ALU.min,
                                   op1=ALU.subtract).then_inc(lD.sem, 1)
            wait(dve, lD, "lf")
            V.tensor_scalar(log_a[:, :, :], log_a[:, :, :], 1.0 / 16.0, None, ALU.mult).then_inc(lD.sem, 1)
            V.tensor_scalar(z[:, 16:18, :], z[:, 16:18, :], float(G_KEY) ** -0.5, None, ALU.mult).then_inc(lD.sem, 1)
            V.memset(sub0[:, :, :], 0.0).then_inc(lD.sem, 1)
            wait(dve, lD, "sub0")
            mask = c_("diag_mask")

            def block_rows(ap, i):
                return ap[:, i * LC_G:(i + 1) * LC_G].rearrange("p (b t) -> p b t", t=SUB).unsqueeze(2)\
                    .to_broadcast([P, 4, SUB, SUB])

            def block_cols(ap, i):
                return ap[:, i * LC_G:(i + 1) * LC_G].rearrange("p (b t) -> p b t", t=SUB).unsqueeze(3)\
                    .to_broadcast([P, 4, SUB, SUB])

            def differences(i, p):
                steps = xD if i < 2 else gD
                if i >= 2:
                    wait(dve, gP, f"dg{i - 2}", p)
                buf = lx[:, 4 * (i % 2):4 * (i % 2) + 4, :, :]
                V.tensor_tensor(buf, block_rows(bc, i), block_cols(bc, i), ALU.subtract).then_inc(steps.sem, 1)
                wait(dve, steps, f"x{i}", p)
                flat = buf.rearrange("p b s t -> p b (s t)")
                V.tensor_tensor(flat, flat, cols_(mask, 4), ALU.add).then_inc(steps.sem, 1)

            def decays(p):
                bc_c = bc[:, :].rearrange("p (c t) -> p c t", c=NC_G)
                V.tensor_tensor_scan(bc[:, :], c_("reset_g"), log_a[:, p, 0:T], 0.0, ALU.mult, ALU.add).then_inc(dD.sem, 1)
                wait(dve, dD, "bc", p)
                V.tensor_copy(sub0[:, :, 1:4], bc[:, :].rearrange("p (c j t) -> p c j t", c=NC_G, j=4)[:, :, 0:3, SUB - 1])\
                    .then_inc(dD.sem, 1)
                wait(dve, dD, "sb", p)
                V.tensor_tensor(g_qs[:, :].rearrange("p (j t) -> p j t", t=SUB),
                                bc[:, :].rearrange("p (j t) -> p j t", t=SUB),
                                rows(sub0[:, :, :].rearrange("p c j -> p (c j)"), SUB), ALU.subtract).then_inc(dD.sem, 1)
                V.tensor_tensor(ke[:, :, :, :], sub0[:, :, 1:4].unsqueeze(3).to_broadcast([P, NC_G, 3, 48]),
                                bc_c[:, :, 0:48].unsqueeze(2).to_broadcast([P, NC_G, 3, 48]), ALU.subtract).then_inc(dD.sem, 1)
                wait(dve, dD, "ke", p)
                V.tensor_scalar(ke[:, :, :, :], ke[:, :, :, :], 0.0, None, ALU.min).then_inc(dD.sem, 1)
                V.tensor_tensor(g_kd[:, :].rearrange("p (c t) -> p c t", c=NC_G),
                                bc_c[:, :, LC_G - 1:LC_G].to_broadcast([P, NC_G, LC_G]), bc_c, ALU.subtract).then_inc(dD.sem, 1)

            def factors(p):
                q, k = z[:, 16 + p, :], z[:, 18 + p, :]
                k_t = k[:, 0:T].rearrange("p (c t) -> p c t", c=NC_G)
                wait(dve, dA, "qe", p)
                V.tensor_tensor(g_qs[:, :], g_qs[:, :], q[:, 0:T], ALU.mult).then_inc(dD.sem, 1)
                wait(dve, dA, "ke", p)
                V.tensor_tensor(ke[:, :, :, :], ke[:, :, :, :],
                                k_t[:, :, 0:48].unsqueeze(2).to_broadcast([P, NC_G, 3, 48]), ALU.mult).then_inc(dD.sem, 1)
                V.tensor_tensor(g_qd[:, :], g_qd[:, :], q[:, 0:T], ALU.mult).then_inc(dD.sem, 1)
                wait(dve, dA, "kend", p)
                V.tensor_tensor(g_kd[:, :], g_kd[:, :], k[:, 0:T], ALU.mult).then_inc(dD.sem, 1)

            def chunks(p):
                q, k = z[:, 16 + p, :], z[:, 18 + p, :]

                def products(i):
                    buf = lx[:, 4 * (i % 2):4 * (i % 2) + 4, :, :]
                    wait(dve, gA, f"ex{i}", p)
                    V.tensor_tensor(buf, buf, block_cols(k, i), ALU.mult).then_inc(gD.sem, 1)
                    wait(dve, gD, f"xk{i}", p)
                    V.tensor_tensor(buf, buf, block_rows(q, i), ALU.mult).then_inc(gD.sem, 1)

                def state(c):
                    wait(dve, gP, f"s{c}", p)
                    if c == 0:
                        if p:
                            dve.wait_ge(gs_out, 16)
                        V.tensor_copy(g_s[:, :], ps[:, 0, 0:P]).then_inc(gD.sem, 1)
                    else:
                        wait(dve, gP, f"o{c}", p)
                        wait(dve, gD, f"c{c - 1}", p)
                        V.scalar_tensor_tensor(out=g_s[:, :], in0=g_s[:, :], scalar=a_end[:, c:c + 1],
                                               in1=ps[:, c % 2, 0:P], op0=ALU.mult, op1=ALU.add).then_inc(gD.sem, 1)

                for i in range(0, NC_G, 2):
                    products(i)
                    products(i + 1)
                    for n in (i, i + 1):
                        state(n)
                        if n + 2 < NC_G:
                            differences(n + 2, p)

            def outputs(p):
                q, k = z[:, 16 + p, :], z[:, 18 + p, :]
                wait(dve, gP, "vb", p)
                V.tensor_tensor(g_kv[:, :, :], ps[:, 2:4, :].rearrange("p n (b k) -> p (n b) k", k=P), rows(k[:, T:NT], P),
                                ALU.mult).then_inc(gD.sem, 1)
                wait(dve, gG, "sa", p)
                wait(dve, gD, "kv", p)
                V.tensor_tensor(g_ss[:, :, :], g_ss[:, :, :], g_kv[:, :, :], ALU.add).then_inc(gD.sem, 1)
                if p + 1 < G_PAIRS:
                    differences(0, p + 1)
                    differences(1, p + 1)
                for hh in range(2):
                    wait(dve, gA, f"rms{hh}", p)
                    V.tensor_tensor(g_h[:, hh, 0:T], ps[:, 6 + hh, :], sq[:, hh, 0:T], ALU.mult).then_inc(gD.sem, 1)
                    V.tensor_tensor(g_h[:, hh, T:NT], ps[:, hh, 256:256 + B], sq[:, hh, T:NT], ALU.mult).then_inc(gD.sem, 1)
                    wait(dve, gD, f"t{hh}", p)
                    V.scalar_tensor_tensor(out=hn[:, hh, :], in0=g_h[:, hh, :], scalar=p_("g_g"), in1=z[:, 24 + 2 * p + hh, :],
                                           op0=ALU.mult, op1=ALU.mult).then_inc(gD.sem, 1)
                for hh in range(2):
                    wait(dve, gA, f"hi{hh}", p)
                    c = 4 + 2 * p + hh
                    V.tensor_tensor(h_lo[:, c, :], hn[:, hh, :], h_hi[:, c, :].bitcast(F32), ALU.subtract).then_inc(gD.sem, 1)

            decays(0)
            differences(0, 0)
            rec_split(PER_HEAD - 1)
            wait(dve, hA, "hi")
            V.tensor_tensor(h_lo[:, 0:4, :], z[:, 12:16, :], h_hi[:, 0:4, :].bitcast(F32), ALU.subtract).then_inc(hD.sem, 1)
            differences(1, 0)
            factors(0)
            for p in range(G_PAIRS):
                chunks(p)
                if p + 1 < G_PAIRS:
                    decays(p + 1)
                    factors(p + 1)
                outputs(p)

            walk(dve, "rec_out", split, out_drain("rec_out"))
            norm(1, "g_ffn0")
            ffn(0)
            walk(dve, "down0", split, down_drain("down0"))
            norm(2, "g_mix1")
            walk(dve, "att_q", split, nothing)

            V.tensor_tensor(lam[0:64, 0:2], p_("lam_q")[0:64, :], p_("lam_k")[0:64, :], ALU.mult).then_inc(lamD.sem, 1)
            wait(dve, lamA, "exp")
            V.tensor_tensor(lam[:, 0:1], lam[:, 2:3], lam[:, 3:4], ALU.subtract).then_inc(lamD.sem, 1)
            wait(dve, lamD, "sub")
            V.tensor_scalar(lam[:, 0:1], lam[:, 0:1], LAM_INIT, None, ALU.add).then_inc(lamD.sem, 1)
            V.memset(coef[:, 0:1], 1.0).then_inc(lamD.sem, 1)
            wait(dve, lamD, "lam")
            V.tensor_copy(coef[:, 1:2], lam[:, 0:1]).then_inc(lamD.sem, 1)
            V.tensor_scalar(g_o2[:, :], p_("g_out"), 1.0 - LAM_INIT, None, ALU.mult).then_inc(lamD.sem, 1)
            dve.wait_ge(catt_in, 16)

            def at_(t, h, w=slice(0, NT)):
                return t[:, h, w] if isinstance(h, int) else t[:, ds(h, 1), w].rearrange("p o t -> p (o t)")

            wait(dve, bA, "rqs")
            V.scalar_tensor_tensor(out=qs[:, :, :], in0=zq[:, :, T:NT], scalar=p_("g_q"), in1=qs_t[:, :, :], op0=ALU.mult,
                                   op1=ALU.mult).then_inc(bD.sem, 1)
            wait(dve, bA, "rq")
            V.scalar_tensor_tensor(out=qn[:, 0, :], in0=zq[:, 0, :], scalar=p_("g_q"), in1=rs3[:, 0, :], op0=ALU.mult,
                                   op1=ALU.mult).then_inc(bD.sem, 1)
            split("att_kv", 0, 2, KT)
            split("att_kv", 0, 3, KT)
            wait(dve, bA, "rk")
            V.scalar_tensor_tensor(out=kn[:, 0, :], in0=kraw[:, :], scalar=p_("g_k"), in1=rs3[:, 1, :], op0=ALU.mult,
                                   op1=ALU.mult).then_inc(bD.sem, 1)

            def finish():
                V.memset(s_new[:, :], 0.0).then_inc(tD.sem, 1)
                wait(dve, aG, "vs", A_HEADS - 1)
                wait(dve, tD, "zero")
                for c in range(2):
                    g = slice(64 * c, 64 * c + 64)
                    V.tensor_tensor(s_new[g, :].rearrange("p (b h c) -> p b h c", b=B, c=2)[:, :, :, c],
                                    qs[g, :, :].rearrange("p h b -> p b h"), ks[g, :, :].rearrange("p h b -> p b h"),
                                    ALU.mult).then_inc(tD.sem, 1)
                for n, (start, end) in enumerate(((0, 4), (4, 7), (7, 8))):
                    wait(dve, eA, f"hi{n}")
                    V.tensor_tensor(h_lo[:, start:end, 0:T], zq[:, start:end, 0:T], h_hi[:, start:end, 0:T].bitcast(F32),
                                    ALU.subtract).then_inc(eD.sem, 1)

            def head(h, u, i, h0, last=False):
                sP_, sA_, sD_, r = (zP, zA, zD, 0) if last else (aP, aA, aD, h)

                def stats(k):
                    wait(dve, sP_, f"s{k}", r)
                    s = ps[:, 2:4, :]
                    V.tensor_tensor(s[:, :, k * P:(k + 1) * P], s[:, :, k * P:(k + 1) * P], cols_(c_("causal"), 2),
                                    ALU.add).then_inc(sD_.sem, 1)
                    wait(dve, sD_, f"m{k}", r)
                    V.tensor_reduce(mx[:, k % 2, :], s[:, :, 0:(k + 1) * P], AX.X, ALU.max).then_inc(sD_.sem, 1)
                    wait(dve, sD_, f"x{k}", r)
                    V.tensor_scalar(mx[:, k % 2, :], mx[:, k % 2, :], -(A_QK ** -0.5), None, ALU.mult).then_inc(sD_.sem, 1)

                def combine(k):
                    b = k % 2
                    w = slice(0, (k + 1) * P)
                    wait(dve, sA_, f"ex{k}", r)
                    V.reciprocal(rs[:, b, :], sm[:, b, :]).then_inc(sD_.sem, 1)
                    wait(dve, sD_, f"r{k}", r)
                    V.tensor_tensor(rs[:, b, :], rs[:, b, :], coef[:, :], ALU.mult).then_inc(sD_.sem, 1)
                    wait(dve, sD_, f"rc{k}", r)
                    V.tensor_scalar(e_att[:, b, 1, w], e_att[:, b, 1, w], rs[:, b, 1:2], None, ALU.mult).then_inc(sD_.sem, 1)
                    wait(dve, sD_, f"e{k}", r)
                    if k >= 2:
                        wait(dve, sP_, f"t{k - 2}", r)
                    V.scalar_tensor_tensor(out=a_att[:, b, w], in0=e_att[:, b, 0, w], scalar=rs[:, b, 0:1],
                                           in1=e_att[:, b, 1, w], op0=ALU.mult, op1=ALU.subtract).then_inc(sD_.sem, 1)

                def page(j):
                    if j == 0:
                        wait(dve, sA_, "qb", r)
                        if h0:
                            dve.wait_ge(past_out, 16 * h)
                    else:
                        wait(dve, sD_, f"red{j - 1}", r)
                    dve.wait_ge(k_in[j], 16 * h + 16)
                    V.tensor_tensor(s_prod[:, :], k_pages[:, j, :], qb[:, :], ALU.mult).then_inc(sD_.sem, 1)
                    wait(dve, sD_, f"mul{j}", r)
                    V.tensor_reduce(s_sc[:, j, :], s_prod[:, :].rearrange("p (h d) -> p h d", d=A_QK), AX.X,
                                    ALU.add).then_inc(sD_.sem, 1)

                stats(0)
                combine(0)
                stats(1)
                page(0)
                combine(1)
                stats(2)
                page(1)
                combine(2)
                if not last:
                    split("att_kv", i, 2 * (h0 + 2), KT)
                stats(3)
                page(2)
                combine(3)
                page(3)
                wait(dve, sP_, "st", r)
                V.tensor_reduce(s_m[0:16, :], ps[0:16, 6, :], AX.X, ALU.max).then_inc(sD_.sem, 1)
                wait(dve, sD_, "smax", r)
                V.tensor_scalar(s_dm[0:16, :], IDENT[0:16, 0:16], s_m[0:16, :], None, ALU.mult).then_inc(sD_.sem, 1)
                if not last:
                    wait(dve, sA_, "rq", r)
                    V.scalar_tensor_tensor(out=qn[:, 1 - u, :], in0=at_(zq, h + 1), scalar=p_("g_q"), in1=rs3[:, 0, :],
                                           op0=ALU.mult, op1=ALU.mult).then_inc(sD_.sem, 1)
                    split("att_kv", i, 2 * (h0 + 2) + 1, KT)
                    wait(dve, sA_, "rk", r)
                    if h0:
                        dve.wait_ge(kn_out, 16 * h)
                    V.scalar_tensor_tensor(out=kn[:, 1 - u, :], in0=kraw[:, :], scalar=p_("g_k"), in1=rs3[:, 1, :],
                                           op0=ALU.mult, op1=ALU.mult).then_inc(sD_.sem, 1)
                wait(dve, sP_, "mb", r)
                V.tensor_copy(at_(m_all, h, slice(0, 16)), ps[:, 7, 0:16]).then_inc(sD_.sem, 1)
                V.tensor_tensor(s_sc[:, :, :], s_sc[:, :, :], cols_(ps[:, 7, 0:16], PAGES), ALU.subtract).then_inc(sD_.sem, 1)
                wait(dve, sA_, "se", r)
                V.tensor_reduce(s_sum[:, :], s_sc[:, :, :].rearrange("p j k -> p k j"), AX.X, ALU.add).then_inc(sD_.sem, 1)
                wait(dve, sA_, "ro", r)
                V.scalar_tensor_tensor(out=at_(zq, h, slice(0, T)), in0=ps[:, 5, :], scalar=g_o2[:, :], in1=rs3[:, 2, 0:T],
                                       op0=ALU.mult, op1=ALU.mult).then_inc(sD_.sem, 1)
                if last:
                    finish()
                wait(dve, sP_, "sum", r)
                V.tensor_copy(at_(l_all, h, slice(0, 16)), ps[:, 4, 0:16]).then_inc(sD_.sem, 1)

            head(0, 0, 0, 0)
            with dve.Fori(0, (A_HEADS - 2) // 2) as i:
                for w in range(2):
                    head(2 * i + (1 + w), 1 - w, i, 1 + w)
            head(A_HEADS - 1, 1, 0, A_HEADS - 1, last=True)
            m_, l_ = (t[:, :, :].rearrange("p b k -> p (b k)") for t in (m_all, l_all))
            new, w_past, w_new, m_both, total, out = (t[:, :] for t in s_w)

            def halves(t, c):
                return t.rearrange("p (k c) -> p k c", c=2)[:, :, c]

            wait(dve, tP, "new")
            V.tensor_copy(new, ps[:, 0, 0:P]).then_inc(tD.sem, 1)
            wait(dve, tD, "newc")
            V.tensor_tensor(m_both, m_, new, ALU.max).then_inc(tD.sem, 1)
            wait(dve, tD, "mt")
            V.tensor_tensor(w_past, m_, m_both, ALU.subtract).then_inc(tD.sem, 1)
            V.tensor_tensor(w_new, new, m_both, ALU.subtract).then_inc(tD.sem, 1)
            wait(dve, tA, "ex")
            V.tensor_tensor(total, l_, w_past, ALU.mult).then_inc(tD.sem, 1)
            wait(dve, tD, "l1")
            V.tensor_tensor(total, total, w_new, ALU.add).then_inc(tD.sem, 1)
            wait(dve, tD, "l2")
            V.reciprocal(total, total).then_inc(tD.sem, 1)
            V.tensor_tensor(new.rearrange("p (b h c) -> p b h c", b=B, c=2), w_new.rearrange("p (b h c) -> p b h c", b=B, c=2),
                            vs[:, :, :].rearrange("p h b -> p b h").unsqueeze(3).to_broadcast([P, B, A_HEADS, 2]),
                            ALU.mult).then_inc(tD.sem, 1)
            wait(dve, tP, "turn")
            V.tensor_tensor(out.rearrange("p (b h c) -> p b h c", b=B, c=2),
                            ps[:, 1, 0:P].rearrange("p (h b c) -> p b h c", b=B, c=2),
                            w_past.rearrange("p (b h c) -> p b h c", b=B, c=2), ALU.mult).then_inc(tD.sem, 1)
            wait(dve, tD, "o1")
            V.tensor_tensor(out, out, new, ALU.add).then_inc(tD.sem, 1)
            wait(dve, tD, "o2")
            V.tensor_tensor(out, out, total, ALU.mult).then_inc(tD.sem, 1)
            wait(dve, tD, "o3")
            V.tensor_scalar(s_o2[:, :], halves(out, 1), lam[:, 0:1], None, ALU.mult).then_inc(tD.sem, 1)
            wait(dve, tD, "c1")
            V.tensor_tensor(s_o[:, :], halves(out, 0), s_o2[:, :], ALU.subtract).then_inc(tD.sem, 1)
            wait(dve, tA, "rms")
            V.scalar_tensor_tensor(out=s_o2[:, :], in0=s_o[:, :], scalar=g_o2[:, :], in1=s_r2[:, 1, :], op0=ALU.mult,
                                   op1=ALU.mult).then_inc(tD.sem, 1)
            wait(dve, tA, "hi")
            V.tensor_tensor(h_lo[:, :, T:NT], s_o2[:, :].rearrange("p (b h) -> p h b", b=B), h_hi[:, :, T:NT].bitcast(F32),
                            ALU.subtract).then_inc(tD.sem, 1)

            walk(dve, "att_out", split, out_drain("att_out"))
            norm(3, "g_ffn1")
            ffn(1)
            walk(dve, "down1", split, down_drain("down1"))

        @block.gpsimd
        def _(pool):
            def times_rows(out, a_, row, n):
                return G.tensor_tensor(out, a_, row.unsqueeze(2).to_broadcast([P, B, n]), ALU.mult)

            def spread(out, row, n=B):
                return G.tensor_tensor(out, IDENT.unsqueeze(1).to_broadcast([P, n, P]),
                                       row.unsqueeze(2).to_broadcast([P, n, P]), ALU.mult)

            G.memset(one[:, :], 1.0).then_inc(small.sem, 1)
            G.memset(eps[:, :], EPS).then_inc(small.sem, 1)
            pool.wait_ge(par_in, 32)
            for layer in range(2):
                pool.dma_start(a["o_conv_s1"][layer], p_(f"conv_s{layer}").rearrange("p (m j b) -> p m j b", j=2, b=B)[:, :, 1, :])\
                    .then_inc(outs, 16)
            wait(pool, gtD, "mo0")
            pool.dma_start(a["o_m"], m_out[:, :]).then_inc(outs, 16)
            wait(pool, gtA, "acol")
            for h in range(M_HEADS):
                if h:
                    pool.wait_ge(cs_out, 16 * h)
                    wait(pool, mD, "cq", h - 1)
                pool.dma_start(c_s[:, :, :], a["state_c"][:, h]).then_inc(c_s_in, 16)
                wait(pool, mP, "bc0", h)
                if h:
                    wait(pool, mD, "hs", h - 1)
                spread(diag_k[:, :, :], z[:, 4 + h, T:NT]).then_inc(mG.sem, 1)
                wait(pool, mA, "ws", h)
                pool.wait_ge(c_s_in, 16 * (h + 1))
                times_rows(c_s[:, :, :], c_s[:, :, :], w_s[:, 0, :], P).then_inc(mG.sem, 1)
                wait(pool, mP, "st3", h)
                spread(diag_q[:, :, :], z[:, h, T:NT]).then_inc(mG.sem, 1)
                wait(pool, mD, "nend", h)
                pool.dma_start(a["o_c"][:, h], c_n[:, 0:P]).then_inc(c_out, 16)
                wait(pool, mD, "cs", h)
                pool.dma_start(a["o_cs"][:, h], c_s[:, :, :]).then_inc(cs_out, 16)
            pool.dma_start(a["o_n"], n_end[:, :]).then_inc(outs, 16)
            pool.dma_start(a["o_ns"], n_s[:, :, :]).then_inc(outs, 16)

            pool.wait_ge(mD.sem, mD.all(M_HEADS))
            pool.wait_ge(drained, S_REC_IN)
            for p in range(G_PAIRS):
                if p:
                    wait(pool, gP, "oi", p - 1)
                    G.memset(g_att[:, :, :, :], 0.0).then_inc(gG.sem, 1)
                else:
                    pool.wait_ge(c_out, 16 * M_HEADS)
                    pool.wait_ge(cs_out, 16 * M_HEADS)
                    G.memset(g_att[:, :, :, :], 0.0).then_inc(gG.sem, 1)
                wait(pool, gP, f"dg{NC_G - 1}", p)
                pool.wait_ge(dg_out, 32 * (p + 1))
                if p:
                    pool.wait_ge(gss_out, 16)
                pool.dma_start(g_ss[:, :, :], a["state_s"][:, p]).then_inc(g_s_in, 16)
                for hh in range(2):
                    ins = spread(g_dv[:, hh, :, :], z[:, 20 + 2 * p + hh, T:NT])
                ins.then_inc(gG.sem, 1)
                wait(pool, gA, "as", p)
                pool.wait_ge(g_s_in, 16 * (p + 1))
                times_rows(g_ss[:, :, :], g_ss[:, :, :], a_s[:, :], P).then_inc(gG.sem, 1)
                wait(pool, gD, "c7", p)
                pool.dma_start(a["o_s"][:, p], g_s[:, :]).then_inc(gs_out, 16)
                wait(pool, gD, "ss", p)
                pool.dma_start(a["o_ss"][:, p], g_ss[:, :, :]).then_inc(gss_out, 16)

            pool.wait_ge(gs_out, 16 * G_PAIRS)
            pool.wait_ge(gss_out, 16 * G_PAIRS)
            pool.wait_ge(outs, 16 * 5)
            for c in range(KT - 1):
                add_squares(pool, G, 1, c)
            pool.wait_ge(slab_done, FIRST["ffn0"])
            G.memset(ub[:, :, 0:2], 0.0).then_inc(pads.sem, 1)
            pool.wait_ge(fD.sem, fD.all(FT))
            pool.dma_start(a["o_conv"][0], conv_end[:, :, :]).then_inc(conv_out, 16)

            for c in range(KT - 1):
                add_squares(pool, G, 2, c)
            pool.wait_ge(slab_done, FIRST["att_q"])
            pool.dma_start(catt[:, :], a["catt"]).then_inc(catt_in, 16)

            def store_past(b, steps, r=None):
                wait(pool, steps, "orow", b if r is None else r)
                pool.dma_start(a["past"][b], o_row).then_inc(past_out, 16)

            def head(h, u, first=False):
                if first:
                    wait(pool, bD, "qs")
                else:
                    wait(pool, aP, "qb", h - 1)
                row = qs[:, :, h] if isinstance(h, int) else qs[:, :, ds(h, 1)].rearrange("p h o -> p (h o)")
                spread(qd[:, :, :], row, A_HEADS).then_inc(aG.sem, 1)
                if not first:
                    store_past(h - 1, aA)
                if first:
                    wait(pool, bD, "kn")
                else:
                    wait(pool, aD, "kn", h - 1)
                one_head = slice(h, h + 1) if isinstance(h, int) else ds(h, 1)
                G.tensor_copy(ks[:, one_head, :], kn[:, u:u + 1, T:NT]).then_inc(aG.sem, 1)
                pool.dma_start(a["o_k"][:, one_head, :], kn[:, u:u + 1, :]).then_inc(kn_out, 16)
                if first:
                    wait(pool, bA, "vr")
                else:
                    wait(pool, aA, "vr", h - 1)
                G.tensor_copy(vs[:, one_head, :], vn[:, T:NT].rearrange("p (o b) -> p o b", o=1)).then_inc(aG.sem, 1)
                pool.dma_start(a["o_v"][:, one_head, :], vn[:, :].rearrange("p (o t) -> p o t", o=1)).then_inc(vn_out, 16)

            head(0, 0, True)
            with pool.Fori(0, (A_HEADS - 2) // 2) as i:
                for w in range(2):
                    head(2 * i + (1 + w), 1 - w)
            head(A_HEADS - 1, 1)
            store_past(B - 1, zA, 0)
            pool.wait_ge(past_out, 16 * B)
            for g in range(A_HEADS):
                pool.dma_start(o_rows[16 * g:16 * g + 16, :], a["past"][:, 2 * g:2 * g + 2, g * P:(g + 1) * P])\
                    .then_inc(past_in, 16)

            pool.wait_ge(kn_out, 16 * A_HEADS)
            for c in range(KT - 1):
                add_squares(pool, G, 3, c)
            pool.wait_ge(slab_done, FIRST["ffn1"])
            G.memset(ub[:, :, 0:2], 0.0).then_inc(pads.sem, 1)
            pool.wait_ge(fD.sem, fD.all(2 * FT))
            pool.dma_start(a["o_conv"][1], conv_end[:, :, :]).then_inc(conv_out, 16)
            for c in range(KT):
                pool.wait_ge(drained, FIRST["down1"] + 2 * (c + 1))
                pool.dma_start(a["o_y"][:, c, :], x[:, c, :]).then_inc(outs, 16)
            pool.wait_ge(outs, 16 * (5 + KT))
            pool.wait_ge(c_out, 16 * M_HEADS)
            pool.wait_ge(cs_out, 16 * M_HEADS)
            pool.wait_ge(gs_out, 16 * G_PAIRS)
            pool.wait_ge(gss_out, 16 * G_PAIRS)
            pool.wait_ge(conv_out, 32)
            pool.wait_ge(kn_out, 16 * A_HEADS)
            pool.wait_ge(vn_out, 16 * A_HEADS)
            pool.wait_ge(dg_out, 32 * G_PAIRS)


def slabs(w):
    k, n = w.shape
    return w.reshape(k // P, P, n // P, P).transpose(2, 1, 0, 3).reshape(n // P, P, k)


def down_slabs(w):
    s = slabs(w)
    return s.reshape(s.shape[0], P, 2, KD * P).transpose(0, 2, 1, 3).reshape(2 * s.shape[0], P, KD * P)


def feature_tiles(v):
    return v.reshape(-1, P).T


def rec_columns(w):
    last = np.zeros((w.shape[0], P), w.dtype)
    last[:, 0:4], last[:, 32:36], last[:, 64:80] = w[:, 2048:2052], w[:, 2052:2056], w[:, 3592:3608]
    return np.concatenate([w[:, 0:2048], w[:, 2056:3592], last], axis=1)


def constants():
    f = np.float32
    i = np.arange(P)
    before = (i[:, None] <= i[None, :])
    lo = i < 64
    causal_t = np.where(before, 0, NEG).astype(f)
    sel = np.zeros((P, M_HEADS, P), f)
    for h in range(M_HEADS):
        sel[h, h] = 1
    half_sum = np.zeros((P, 32), f)
    half_sum[lo, 0] = half_sum[~lo, 1] = 1
    s = np.arange(SUB)
    diag = np.where(s[:, None] <= s[None, :], 0, NEG).astype(f).reshape(1, -1)
    t = np.arange(T)
    cst = {"ident": np.eye(P), "ones": np.ones((P, P))}
    rec = {"causal_T": causal_t, "ones_lo": np.tile(lo, (P, 1)), "ones_hi": np.tile(~lo, (P, 1)),
           "sel_head": sel.reshape(P, -1), "half_sum": half_sum, "diag_mask": np.tile(diag, (P, 1)),
           "reset_m": np.tile(t % LC_M != 0, (P, 1)), "reset_g": np.tile(t % LC_G != 0, (P, 1))}
    att = {"causal": causal_t.T, "ones_half": lo[:, None] == lo[None, :]}
    return cst, rec, att


def packed(table, parts):
    return np.ascontiguousarray(np.concatenate([np.asarray(parts[n], np.float32) for n, _ in table], axis=1))


def kernel(**inputs):
    import concourse.bacc as bacc
    from concourse.bass_utils import run_bass_kernel_spmd

    v = {k: np.asarray(x) for k, x in inputs.items()}
    f = np.float32

    def column(values, rows=P, at=0):
        out = np.zeros((P, 1), f)
        out[at:at + len(values), 0] = values
        return out

    x_all = np.concatenate([v["x_prompt"][0], v["x_sample"][:, 0]], axis=0)
    tokens = x_all.T.reshape(KT, P, NT).transpose(1, 0, 2)
    cst, rec, att = constants()
    gate_up = np.zeros((P, G_PAIRS * P), f)
    gate_up[64:80] = v["rec_w_gate_up"][0]
    rec["w_gate_up"] = gate_up
    b_mgate = np.zeros((P, 1), f)
    b_mgate[0:4, 0], b_mgate[32:36, 0] = v["rec_b_mgate"][0, :4], v["rec_b_mgate"][0, 4:]
    pads_ = lambda u: np.concatenate([u, np.zeros((P - u.shape[0], u.shape[1]), f)], axis=0)
    twice = lambda u: np.concatenate([u, u])[:, None]
    par = {"g_mix0": feature_tiles(v["norm_mix_g"][0]), "g_mix1": feature_tiles(v["norm_mix_g"][1]),
           "g_ffn0": feature_tiles(v["norm_ffn_g"][0]), "g_ffn1": feature_tiles(v["norm_ffn_g"][1]),
           "b_gate": feature_tiles(v["rec_b_gate"][0]), "g_m": v["rec_m_norm_g"][0][:, None],
           "g_g": v["rec_g_norm_g"][0][:, None], "g_q": twice(v["att_q_norm_g"][0]), "g_k": twice(v["att_k_norm_g"][0]),
           "g_out": v["att_out_norm_g"][0][:, None], "b_mgate": b_mgate,
           "lam_q": pads_(np.stack([v["att_lambda_q1"][0], v["att_lambda_q2"][0]], 1)),
           "lam_k": pads_(np.stack([v["att_lambda_k1"][0], v["att_lambda_k2"][0]], 1)),
           "m0": pads_(v["state_mlstm_m"][0].T), "n0": v["state_mlstm_n"][0].transpose(2, 1, 0).reshape(P, M_HEADS * B)}
    for layer in range(2):
        par[f"conv_w{layer}"] = v["ffn_conv_w"][layer].reshape(3, FT, P).transpose(2, 0, 1).reshape(P, 3 * FT)
        par[f"conv_b{layer}"] = feature_tiles(v["ffn_conv_b"][layer])
        par[f"conv_s{layer}"] = v["state_ffn_conv"][layer].reshape(B, 2, FT, P).transpose(3, 2, 1, 0).reshape(P, -1)

    def ffn_slabs(layer):
        up, gate = slabs(v["ffn_w_up"][layer]), slabs(v["ffn_w_gate"][layer])
        return np.stack([up, gate], 1).reshape(S_FFN, P, D_MODEL)

    att_in = slabs(v["att_w_in"][0])
    att_kv = np.stack([att_in[A_HEADS:2 * A_HEADS], att_in[2 * A_HEADS:]], 1).reshape(2 * A_HEADS, P, D_MODEL)
    arrays = {
        "x": tokens, "cst": packed(CONSTS, cst), "crec": packed(CONSTS_REC, rec), "catt": packed(CONSTS_ATT, att),
        "par": packed(PARAMS, par),
        "w_rec_in": slabs(rec_columns(v["rec_w_in"][0]))[REC_TILES], "w_rec_out": slabs(v["rec_w_out"][0]),
        "w_att_q": att_in[:A_HEADS], "w_att_kv": np.concatenate([att_kv, slabs(v["att_w_out"][0])]),
        "w_ffn0": ffn_slabs(0), "w_ffn1": ffn_slabs(1),
        "w_down0": down_slabs(v["ffn_w_down"][0]), "w_down1": down_slabs(v["ffn_w_down"][1]),
        "state_c": v["state_mlstm_C"][0].transpose(2, 1, 0, 3),
        "state_s": v["state_gla_S"][0].reshape(B, G_PAIRS, P, P).transpose(2, 1, 0, 3),
        "cache_k": v["cache_k"][0].reshape(POOL, PAGE, D_MODEL), "cache_v": v["cache_v"][0].reshape(POOL, PAGE, D_MODEL),
        "page_table": v["page_table"].reshape(1, B * PAGES),
    }
    outs = {"o_y": (P, KT, NT), "o_m": (4, 1 + B), "o_c": (P, M_HEADS, P), "o_cs": (P, M_HEADS, B, P),
            "o_n": (P, M_HEADS), "o_ns": (P, M_HEADS, B), "o_s": (P, G_PAIRS, P), "o_ss": (P, G_PAIRS, B, P),
            "o_k": (P, A_HEADS, NT), "o_v": (P, A_HEADS, NT), "o_conv": (2, P, FT, 2 + B), "o_conv_s1": (2, P, FT, B)}
    nc = bacc.Bacc("TRN2", target_bir_lowering=False, num_devices=1)
    aps = {}
    arrays = {n: np.ascontiguousarray(t) for n, t in arrays.items()}
    for n, t in arrays.items():
        aps[n] = nc.dram_tensor(f"in_{n}", t.shape, mybir.dt.from_np(t.dtype), kind="ExternalInput").ap()
    for n, shape in outs.items():
        aps[n] = nc.dram_tensor(f"out_{n}", shape, mybir.dt.float32, kind="ExternalOutput").ap()
    aps["blocks"] = nc.dram_tensor("blocks", (G_PAIRS, 2, 16, 512), mybir.dt.float32, kind="Internal").ap()
    aps["past"] = nc.dram_tensor("past", (B, 16, D_MODEL), mybir.dt.float32, kind="Internal").ap()
    build(nc, aps)
    r = run_bass_kernel_spmd(nc, [{f"in_{n}": t for n, t in arrays.items()}], core_ids=[0]).results[0]
    o = {n: np.asarray(r[f"out_{n}"]) for n in outs}

    y = o["o_y"].transpose(2, 1, 0).reshape(NT, D_MODEL)
    k = o["o_k"].transpose(2, 1, 0)
    vv = o["o_v"].transpose(2, 1, 0)
    conv = o["o_conv"].transpose(0, 3, 2, 1).reshape(2, 2 + B, FFN)
    s1 = o["o_conv_s1"].transpose(0, 3, 2, 1).reshape(2, B, FFN)
    c = np.ascontiguousarray
    return (c(y[None, :T]), c(y[T:, None]),
            c(o["o_c"].transpose(1, 2, 0)[None, None]), c(o["o_cs"].transpose(2, 1, 0, 3)[None]),
            c(o["o_n"].T[None, None]), c(o["o_ns"].transpose(2, 1, 0)[None]),
            c(o["o_m"][:, 0][None, None]), c(o["o_m"][:, 1:].T[None]),
            c(o["o_s"].transpose(1, 0, 2).reshape(1, 1, 4, G_KEY, P)),
            c(o["o_ss"].transpose(2, 1, 0, 3).reshape(1, B, 4, G_KEY, P)),
            c(k[None, None, :T]), c(k[T:][None, :, None]), c(vv[None, None, :T]), c(vv[T:][None, :, None]),
            c(conv[:, None, 0:2]), c(np.stack([s1, conv[:, 2:]], axis=2)))
```
